# Optimizing a Trainium2 kernel written in Bass

```python
import math
import jax, jax.numpy as jnp
from jax import lax
import numpy as np

D_MODEL = 2048
BATCH = 1
SEQ = 256
DEPTH = 1

N_MEM = 256
EPS = 1e-6
MIX_WIDTH = D_MODEL
ATTN_WIDTH = MIX_WIDTH // 2
SSM_WIDTH = MIX_WIDTH - ATTN_WIDTH
DIFF_HEADS = 8
DIFF_VDIM = ATTN_WIDTH // DIFF_HEADS
DIFF_QKDIM = DIFF_VDIM // 2
ROT_DIM = DIFF_QKDIM // 4
ROPE_THETA = 500000.0
Q_BLOCK = 128
IN_COLS = 3 * ATTN_WIDTH + SSM_WIDTH
SSM_GROUP = 16
SSM_GROUPS = SSM_WIDTH // SSM_GROUP
SSM_STATE = 64
DT_MIN = 0.001
DT_MAX = 0.1
XATTN_HEADS = 4
XATTN_HEAD_DIM = 128
XATTN_WIDTH = XATTN_HEADS * XATTN_HEAD_DIM
PEER_HEADS = 8
PEER_KEYS = 128
PEER_EXPERTS = PEER_KEYS * PEER_KEYS
PEER_QDIM = 256
PEER_TOPK = 16
PEER_CHUNK = 128

kernel_name = 'hymba_diffattn_s5_peer_block'

def rmsnorm(x, g):
    xf = x.astype(jnp.float32)
    y = xf * lax.rsqrt(jnp.mean(xf * xf, axis=-1, keepdims=True) + EPS)
    return (y * g.astype(jnp.float32)).astype(x.dtype)

def rope_tables(positions):
    freqs = ROPE_THETA ** (-jnp.arange(0, ROT_DIM, 2, dtype=jnp.float32) / ROT_DIM)
    ang = positions.astype(jnp.float32)[..., None] * freqs
    return jnp.cos(ang)[:, :, None, None, :], jnp.sin(ang)[:, :, None, None, :]

def partial_rope(t, cos, sin):
    half = ROT_DIM // 2
    r1, r2, rest = t[..., :half], t[..., half:ROT_DIM], t[..., ROT_DIM:]
    c, s = cos.astype(t.dtype), sin.astype(t.dtype)
    return jnp.concatenate([r1 * c - r2 * s, r1 * s + r2 * c, rest], axis=-1)

def diff_attention(q, k, v, lam):
    B, S, H, _, d = q.shape
    nblk = S // Q_BLOCK
    scale = DIFF_QKDIM ** -0.5
    qb = q.reshape(B, nblk, Q_BLOCK, H, 2, d).transpose(1, 0, 2, 3, 4, 5)
    k_idx = jnp.arange(S)

    def one_block(args):
        qblk, bi = args
        s = jnp.einsum('bqhcd,bkhcd->bhcqk', qblk, k).astype(jnp.float32) * scale
        q_idx = bi * Q_BLOCK + jnp.arange(Q_BLOCK)
        mask = k_idx[None, :] <= q_idx[:, None]
        p = jax.nn.softmax(jnp.where(mask, s, -jnp.inf), axis=-1)
        a = p[:, :, 0] - lam * p[:, :, 1]
        return jnp.einsum('bhqk,bkhe->bqhe', a.astype(v.dtype), v)

    out = lax.map(one_block, (qb, jnp.arange(nblk)))
    return out.transpose(1, 0, 2, 3, 4).reshape(B, S, H, v.shape[-1])

def s5_ssm(u, a_re, a_im, log_dt, b_re, b_im, c_re, c_im, d_skip):
    f32 = jnp.float32
    dt = jnp.exp(log_dt.astype(f32))[:, None]
    lre, lim = a_re.astype(f32), a_im.astype(f32)
    mag = jnp.exp(lre * dt)
    ang = lim * dt
    ab_re, ab_im = mag * jnp.cos(ang), mag * jnp.sin(ang)
    den = lre * lre + lim * lim
    f_re = ((ab_re - 1.0) * lre + ab_im * lim) / den
    f_im = (ab_im * lre - (ab_re - 1.0) * lim) / den
    br, bim = b_re.astype(f32), b_im.astype(f32)
    bb_re = f_re[..., None] * br - f_im[..., None] * bim
    bb_im = f_re[..., None] * bim + f_im[..., None] * br
    uf = u.astype(f32)
    bu_re = jnp.einsum('bsgh,gph->bsgp', uf, bb_re)
    bu_im = jnp.einsum('bsgh,gph->bsgp', uf, bb_im)
    S = u.shape[1]
    a_full_re = jnp.broadcast_to(ab_re, (1, S) + ab_re.shape)
    a_full_im = jnp.broadcast_to(ab_im, (1, S) + ab_im.shape)

    def combine(e1, e2):
        a1r, a1i, b1r, b1i = e1
        a2r, a2i, b2r, b2i = e2
        return (a2r * a1r - a2i * a1i,
                a2r * a1i + a2i * a1r,
                a2r * b1r - a2i * b1i + b2r,
                a2r * b1i + a2i * b1r + b2i)

    _, _, xr, xi = lax.associative_scan(combine, (a_full_re, a_full_im, bu_re, bu_im), axis=1)
    y = (jnp.einsum('bsgp,ghp->bsgh', xr, c_re.astype(f32))
         - jnp.einsum('bsgp,ghp->bsgh', xi, c_im.astype(f32))
         + d_skip.astype(f32) * uf)
    return y.astype(u.dtype)

def cross_attention(h, mem, wq, wkv, wo):
    B, S, _ = h.shape
    M = mem.shape[1]
    q = (h @ wq).reshape(B, S, XATTN_HEADS, XATTN_HEAD_DIM)
    kv = (mem @ wkv).reshape(M, B, 2, XATTN_HEADS, XATTN_HEAD_DIM) if False else (mem @ wkv).reshape(B, M, 2, XATTN_HEADS, XATTN_HEAD_DIM)
    k, v = kv[:, :, 0], kv[:, :, 1]
    s = jnp.einsum('bshd,bmhd->bhsm', q, k).astype(jnp.float32) * XATTN_HEAD_DIM ** -0.5
    p = jax.nn.softmax(s, axis=-1).astype(h.dtype)
    o = jnp.einsum('bhsm,bmhd->bshd', p, v).reshape(B, S, XATTN_WIDTH)
    return o @ wo

def peer(h, wq, sub_k1, sub_k2, u_tab, v_tab):
    B, S, D = h.shape
    half = PEER_QDIM // 2
    q = (h @ wq).reshape(B, S, PEER_HEADS, PEER_QDIM)
    s1 = jnp.einsum('bshd,hnd->bshn', q[..., :half], sub_k1).astype(jnp.float32)
    s2 = jnp.einsum('bshd,hnd->bshn', q[..., half:], sub_k2).astype(jnp.float32)
    t1, i1 = lax.top_k(s1, PEER_TOPK)
    t2, i2 = lax.top_k(s2, PEER_TOPK)
    cand = (t1[..., :, None] + t2[..., None, :]).reshape(B, S, PEER_HEADS, PEER_TOPK * PEER_TOPK)
    ts, ic = lax.top_k(cand, PEER_TOPK)
    e1 = jnp.take_along_axis(i1, ic // PEER_TOPK, axis=-1)
    e2 = jnp.take_along_axis(i2, ic % PEER_TOPK, axis=-1)
    experts = e1 * PEER_KEYS + e2
    gates = jax.nn.softmax(ts, axis=-1).astype(h.dtype)
    nc = (B * S) // PEER_CHUNK
    E = PEER_HEADS * PEER_TOPK
    hx = h.reshape(nc, PEER_CHUNK, D)
    ex = experts.reshape(nc, PEER_CHUNK, E)
    gt = gates.reshape(nc, PEER_CHUNK, E)

    def chunk(args):
        xc, ec, gc = args
        act = jnp.einsum('cd,ced->ce', xc, u_tab[ec])
        w = gc * jax.nn.gelu(act, approximate=False)
        return jnp.einsum('ce,ced->cd', w, v_tab[ec])

    return lax.map(chunk, (hx, ex, gt)).reshape(B, S, D)

def setup_inputs(seed: int = 0) -> dict:
    key = jax.random.key(seed)
    ks = iter(jax.random.split(key, 48))
    L, D, f32 = DEPTH, D_MODEL, jnp.float32

    def nrm(shape, scale):
        return jax.random.normal(next(ks), shape, f32) * scale

    def gain(shape):
        return 1.0 + 0.05 * jax.random.normal(next(ks), shape, f32)

    x = nrm((BATCH, SEQ, D), 1.0)
    mem = nrm((BATCH, N_MEM, D), 1.0)
    positions = (jax.random.randint(next(ks), (BATCH, 1), 0, 4096, dtype=jnp.int32)
                 + jnp.arange(SEQ, dtype=jnp.int32)[None, :])
    G, P, Hc = SSM_GROUPS, SSM_STATE, SSM_GROUP
    n = jnp.arange(P, dtype=f32)
    ssm_a_re = -0.5 * jnp.exp(0.02 * jax.random.normal(next(ks), (L, G, P), f32))
    ssm_a_im = math.pi * n + 0.02 * jax.random.normal(next(ks), (L, G, P), f32)
    ssm_log_dt = math.log(DT_MIN) + jax.random.uniform(next(ks), (L, G), f32) * (math.log(DT_MAX) - math.log(DT_MIN))
    return {
        'x': x,
        'mem': mem,
        'positions': positions,
        'mix_norm_g': gain((L, D)),
        'w_in': nrm((L, D, IN_COLS), D ** -0.5),
        'lam_q1': nrm((L, DIFF_QKDIM), 0.1),
        'lam_k1': nrm((L, DIFF_QKDIM), 0.1),
        'lam_q2': nrm((L, DIFF_QKDIM), 0.1),
        'lam_k2': nrm((L, DIFF_QKDIM), 0.1),
        'attn_head_g': gain((L, DIFF_VDIM)),
        'ssm_a_re': ssm_a_re,
        'ssm_a_im': ssm_a_im,
        'ssm_log_dt': ssm_log_dt,
        'ssm_b_re': nrm((L, G, P, Hc), (2 * Hc) ** -0.5),
        'ssm_b_im': nrm((L, G, P, Hc), (2 * Hc) ** -0.5),
        'ssm_c_re': nrm((L, G, Hc, P), (2 * P) ** -0.5),
        'ssm_c_im': nrm((L, G, Hc, P), (2 * P) ** -0.5),
        'ssm_d': nrm((L, G, Hc), 1.0),
        'glu_w': nrm((L, SSM_WIDTH, SSM_WIDTH), SSM_WIDTH ** -0.5),
        'glu_b': nrm((L, SSM_WIDTH), 0.01),
        'ssm_out_g': gain((L, SSM_WIDTH)),
        'w_out': nrm((L, MIX_WIDTH, D), MIX_WIDTH ** -0.5),
        'xattn_norm_g': gain((L, D)),
        'mem_norm_g': gain((L, D)),
        'xattn_wq': nrm((L, D, XATTN_WIDTH), D ** -0.5),
        'xattn_wkv': nrm((L, D, 2 * XATTN_WIDTH), D ** -0.5),
        'xattn_wo': nrm((L, XATTN_WIDTH, D), XATTN_WIDTH ** -0.5),
        'ffn_norm_g': gain((L, D)),
        'peer_wq': nrm((L, D, PEER_HEADS * PEER_QDIM), D ** -0.5),
        'peer_k1': nrm((L, PEER_HEADS, PEER_KEYS, PEER_QDIM // 2), (PEER_QDIM // 2) ** -0.5),
        'peer_k2': nrm((L, PEER_HEADS, PEER_KEYS, PEER_QDIM // 2), (PEER_QDIM // 2) ** -0.5),
        'peer_u': nrm((L, PEER_EXPERTS, D), D ** -0.5),
        'peer_v': nrm((L, PEER_EXPERTS, D), 0.5),
        'final_norm_g': gain((D,)),
    }

def reference(x, mem, positions, mix_norm_g, w_in, lam_q1, lam_k1, lam_q2, lam_k2,
              attn_head_g, ssm_a_re, ssm_a_im, ssm_log_dt, ssm_b_re, ssm_b_im,
              ssm_c_re, ssm_c_im, ssm_d, glu_w, glu_b, ssm_out_g, w_out,
              xattn_norm_g, mem_norm_g, xattn_wq, xattn_wkv, xattn_wo, ffn_norm_g,
              peer_wq, peer_k1, peer_k2, peer_u, peer_v, final_norm_g):
    B, S, D = x.shape
    cos, sin = rope_tables(positions)
    h = x
    for l in range(DEPTH):
        lam_init = 0.8 - 0.6 * math.exp(-0.3 * l)
        xn = rmsnorm(h, mix_norm_g[l])
        z = xn @ w_in[l]
        q = z[..., :ATTN_WIDTH].reshape(B, S, DIFF_HEADS, 2, DIFF_QKDIM)
        k = z[..., ATTN_WIDTH:2 * ATTN_WIDTH].reshape(B, S, DIFF_HEADS, 2, DIFF_QKDIM)
        v = z[..., 2 * ATTN_WIDTH:3 * ATTN_WIDTH].reshape(B, S, DIFF_HEADS, DIFF_VDIM)
        u = z[..., 3 * ATTN_WIDTH:].reshape(B, S, SSM_GROUPS, SSM_GROUP)
        q = partial_rope(q, cos, sin)
        k = partial_rope(k, cos, sin)
        lam = (jnp.exp(jnp.sum(lam_q1[l].astype(jnp.float32) * lam_k1[l].astype(jnp.float32)))
               - jnp.exp(jnp.sum(lam_q2[l].astype(jnp.float32) * lam_k2[l].astype(jnp.float32)))
               + lam_init)
        att = diff_attention(q, k, v, lam)
        att = (rmsnorm(att, attn_head_g[l]) * (1.0 - lam_init)).reshape(B, S, ATTN_WIDTH)
        y = s5_ssm(u, ssm_a_re[l], ssm_a_im[l], ssm_log_dt[l], ssm_b_re[l], ssm_b_im[l],
                   ssm_c_re[l], ssm_c_im[l], ssm_d[l]).reshape(B, S, SSM_WIDTH)
        g = jax.nn.gelu(y, approximate=False)
        g = g * jax.nn.sigmoid(g @ glu_w[l] + glu_b[l])
        ssm_out = rmsnorm(g, ssm_out_g[l])
        h = h + jnp.concatenate([att, ssm_out], axis=-1) @ w_out[l]
        hn = rmsnorm(h, xattn_norm_g[l])
        mn = rmsnorm(mem, mem_norm_g[l])
        h = h + cross_attention(hn, mn, xattn_wq[l], xattn_wkv[l], xattn_wo[l])
        h = h + peer(rmsnorm(h, ffn_norm_g[l]), peer_wq[l], peer_k1[l], peer_k2[l],
                     peer_u[l], peer_v[l])
    return rmsnorm(h, final_norm_g)


_drawn_inputs = setup_inputs


def setup_inputs(seed=0):
    import zlib

    import numpy as np

    out = dict(_drawn_inputs(seed))
    spreads = {}
    factors = {'lam_k1': 4.825,
     'lam_q2': 5.149,
     'ssm_a_re': 8.0,
     'glu_b': 5.98,
     'xattn_norm_g': 4.171,
     'mem_norm_g': 3.662}
    for name, (base, spread) in spreads.items():
        noise = np.random.default_rng([zlib.crc32(name.encode()), seed]).standard_normal(out[name].shape)
        drawn = base * np.exp(spread * noise) if base else spread * noise
        out[name] = __import__('jax').numpy.asarray(drawn.astype(out[name].dtype))
    for name, factor in factors.items():
        out[name] = (out[name] * factor).astype(out[name].dtype)
    return out
```

```python
import math
from contextlib import ExitStack

import concourse.bass as bass
from concourse import mybir

F32 = mybir.dt.float32
F32R = mybir.dt.float32r
I32 = mybir.dt.int32
U32 = mybir.dt.uint32
ALU = mybir.AluOpType
ACT = mybir.ActivationFunctionType
AX = mybir.AxisListType

P = 128
D = 2048
S = 256
NT = S // P
DC = D // P
HEADS = 8
ATT = 1024
QK = 64
SSM_W = 1024
SSM_C = SSM_W // P
NBLK = 32
XH = 4
XW = 512
PH = 8
KEYS = 128
TOPK = 16
EPS = 1e-6
LAM_INIT = 0.8 - 0.6 * math.exp(-0.3 * 0)
TWO_PI = 2 * math.pi
PI_IN = 3.1415925
C1 = 6.28125
C2 = float(int((TWO_PI - C1) * 2 ** 20)) / 2 ** 20
C3 = TWO_PI - C1 - C2
ROUND = 1.5 * 2 ** 23
ROUND15 = 1.5 * 2 ** 8
NEG = -1e30
ROPE = [500000.0 ** (-j / 16.0) for j in range(0, 16, 2)]

UW0 = 8
QKV0 = 16
GLU0 = 40
WO0 = 44
XQ0 = 60
XO0 = 64
PQ0 = 68
U0 = 84
V0 = U0 + KEYS
END = V0 + KEYS
UA = 32
POOL_UNITS = U0 + UA
SLOTS = 4


class Banks:

    def __init__(self):
        self.uses = [0] * 8
        self.at = {}
        self.unit = {}

    def add(self, name, bank, unit=None):
        self.at[name] = (bank, self.uses[bank])
        self.uses[bank] += 1
        if unit is not None:
            self.unit[name] = unit


def plan_banks():
    b = Banks()

    def norm(k):
        for cp in range(8):
            b.add(("norm", k, cp), cp % 4)

    norm(0)
    for j in range(4):
        b.add(("mk", j), j, j)
    for t in range(2):
        b.add(("mv", t), t, 7)
    norm(1)
    for j in range(8):
        b.add(("uw", j), j % 4, UW0 + j)
    for cb in range(6):
        for t in range(2):
            b.add(("qkv", cb, t), 2 * (cb % 2) + t, QKV0 + 4 * cb + 3)
    for s in range(NBLK):
        b.add(("bu", s), 4 + s % 2)
    for i in range(8):
        b.add(("qkT", i), i % 4)
    for i in range(4):
        b.add(("s0", i), i)
    for i in range(8):
        b.add(("s1", i), i % 4)
    for i in range(6):
        b.add(("aT", i), i % 4)
    for i in range(4):
        b.add(("av", i), (2 + i) % 4)
    for i in range(4):
        b.add(("oT", i), (2 + i) % 4)
    for ct in range(8):
        b.add(("glu", ct), ct % 4, GLU0 + ct // 2)
    b.add(("ssq", 0), 4)
    for cb in range(4):
        for t in range(2):
            b.add(("wo", cb, t), 2 * (cb % 2) + t, WO0 + 4 * cb + 3)
    norm(2)
    for j in range(4):
        b.add(("xq", j), j, XQ0 + j)
    for i in range(4):
        b.add(("xs", i), i)
    for h in range(4):
        b.add(("xp", h), h)
    for h in range(4):
        b.add(("xo", h), h)
    for cb in range(4):
        for t in range(2):
            b.add(("xw", cb, t), 2 * (cb % 2) + t, XO0 + cb)
    norm(3)
    for c in range(16):
        b.add(("pq", c), c % 4, PQ0 + c)
    for i in range(8):
        b.add(("ps", i), i % 4)
    count, b.fills = [0] * 8, {}
    for name, (bank, _) in b.at.items():
        if name not in b.unit:
            count[bank] += 1
            b.fills[name] = count[bank]
    return b


class Chain:

    def __init__(self, eng, sem):
        self.eng, self.sem, self.n = eng, sem, 0

    def __call__(self, ins):
        ins.then_inc(self.sem, 1)
        self.n += 1
        return self.n

    def settle(self):
        self.eng.wait_ge(self.sem, self.n)


def hymba_peer(nc, T):
    ctx = ExitStack()
    with ctx:
        base = 16512

        def at(name, kb, shape, dt=F32):
            return nc.alloc_sbuf_tensor_at(name, shape, dt, offset=base + int(kb * 1024))

        def sem(name):
            return ctx.enter_context(nc.semaphore(name))

        def sems(name, n):
            return [sem(f"{name}{i}") for i in range(n)]

        raw = [at(f"raw{i}", 8 * i, [P, 2048]) for i in range(SLOTS)]
        lo = [at(f"lo{i}", 8 * i, [P, 2048], F32R) for i in range(SLOTS)]
        hi = [at(f"hi{i}", 32 + 8 * i, [P, 2048], F32R) for i in range(SLOTS)]
        H = at("H", 64, [P, NT, D])
        k = 80.0
        small = {}

        def sm(name, shape, dt=F32):
            nonlocal k
            n = 4
            for x in shape[1:]:
                n *= x
            small[name] = at(name, k, shape, dt)
            k += max(n, 32) / 1024
            k = math.ceil(k * 32) / 32
            return small[name]

        ident = sm("ident", [P, P])
        maskd = sm("maskd", [P, 2, P])
        gains = sm("gains", [P, 4, DC])
        g_att = sm("g_att", [P, 1])
        g_att8 = sm("g_att8", [P, 1])
        g_ssm = sm("g_ssm", [P, SSM_C])
        glu_b = sm("glu_b", [P, SSM_C])
        d_skip = sm("d_skip", [P, SSM_C])
        lamv = sm("lamv", [P, 4, QK])
        lams = sm("lams", [P, 8])
        posi = sm("posi", [P, NT], I32)
        posf = sm("posf", [P, NT])
        freq = sm("freq", [P, 8])
        rcos = sm("rcos", [P, NT, 8])
        rsin = sm("rsin", [P, NT, 8])
        stat = sm("stat", [P, 16])
        assert k <= 84.1, k
        k = 84.25
        prm = at("prm", k, [P, 20, NBLK])
        k += 2.5
        st_max = at("st_max", k, [P, 32])
        st_sum = at("st_sum", k + 0.125, [P, 32])
        st_rec = at("st_rec", k + 0.25, [P, 32])
        head_ms = at("head_ms", k + 0.375, [P, 16])
        ones = at("ones", 207, [P, P])
        eps = at("eps", k + 0.5, [P, 1])
        magic = at("magic", k + 0.53125, [P, 1])
        one = at("one", k + 0.5625, [P, 1])
        half_mask = at("half_mask", k + 0.59375, [P, 2])

        XTh = at("XTh", 88, [P, DC, S], F32R)
        XTl = at("XTl", 104, [P, DC, S], F32R)
        qT = at("qT", 88, [P, HEADS, S])
        kT = at("kT", 96, [P, HEADS, S])
        aT0 = at("aT0", 104, [P, HEADS, P])
        aT1 = at("aT1", 108, [P, HEADS, 2, P])
        p0 = at("p0", 112, [P, 2 * HEADS, P])
        mixh = at("mixh", 88, [P, DC, S], F32R)
        mixl = at("mixl", 104, [P, DC, S], F32R)
        uT = at("uT", 120, [P, SSM_C, S])
        sig = at("sig", 120, [P, SSM_C, S])
        nat = at("nat", 128, [P, NT, D])
        zqk = at("zqk", 128, [P, NT, D])
        p1 = at("p1", 128, [P, 2 * HEADS, S])
        att_n = at("att_n", 128, [P, NT, ATT])
        vnat = at("vnat", 144, [P, NT, ATT])
        junk = at("junk", 144, [P, D])
        BW = at("BW", 152, [P, 2, SSM_C, P])
        CW = at("CW", 160, [P, NBLK, 2, 32])
        yT = at("yT", 168, [P, SSM_C, S])
        tab = at("tab", 176, [P, 2, 2, S])
        m1 = at("m1", 180, [P, 2, S])
        m2 = at("m2", 182, [P, 2, S])
        wmod = at("wmod", 184, [P, 2, S])
        sst = at("sst", 186, [P, 2, S])
        xst = at("xst", 188, [P, 2, S])
        phA = at("phA", 190, [P, S])
        phR = at("phR", 191, [P, S])
        phF = at("phF", 192, [P, S])
        phS = at("phS", 193, [P, S])
        kxT = at("kxT", 194, [P, XH, S])
        vx = at("vx", 198, [P, NT, XW])
        iota_t = at("iota_t", 202, [P, S])
        zero = at("zero", 203, [P, 1024])
        braw = at("braw", 180, [P, 2, SSM_C, 64])
        craw = at("craw", 184, [P, 2, NBLK, 16])
        ctmp = at("ctmp", 188, [P, 2, NBLK, 16])
        gTh = at("gTh", 152, [P, SSM_C, S], F32R)
        gTl = at("gTl", 160, [P, SSM_C, S], F32R)
        sqb = at("sqb", 176, [P, SSM_C, S])
        qxT = at("qxT", 144, [P, XH, S])
        px = at("px", 148, [P, NT, XH, S])
        pxT = at("pxT", 156, [P, XH, 2, S])
        oxh = at("oxh", 164, [P, XH, S], F32R)
        oxl = at("oxl", 168, [P, XH, S], F32R)
        keys = at("keys", 120, [P, 2 * PH, KEYS])
        qP = at("qP", 144, [P, 2 * PH, S])
        sc = at("sc", 160, [P, NT, 2 * PH, KEYS])
        cand = at("cand", 176, [P, PH, TOPK, TOPK])
        repl = at("repl", 184, [P, 256])
        k = 185.0
        tv = at("tv", k, [P, 2 * PH, TOPK])
        ti = at("ti", k + 1, [P, 2 * PH, TOPK], U32)
        tif = at("tif", k + 2, [P, 2 * PH, TOPK])
        ts = at("ts", k + 3, [P, PH, TOPK])
        ic = at("ic", k + 3.5, [P, PH, TOPK], U32)
        icx = at("icx", k + 4, [P, 2, PH, TOPK], U32)
        icf = at("icf", k + 5, [P, 2, PH, TOPK])
        ef = at("ef", k + 6, [P, 2, PH, TOPK])
        ei = at("ei", k + 7, [P, PH, TOPK])
        gate = at("gate", k + 7.5, [P, NT, PH, TOPK])
        eidx = at("eidx", k + 8.5, [P, NT, PH, TOPK], I32)
        io16 = at("io16", k + 9.5, [P, TOPK])
        tokf = at("tokf", k + 9.5625, [P, NT])
        g1 = at("g1", k + 9.625, [P, PH])
        g2 = at("g2", k + 9.6875, [P, PH])
        eq = at("eq", 144, [P, PH, TOPK, TOPK])
        eqv = at("eqv", 152, [P, PH, TOPK, TOPK])
        gbuf = at("gbuf", 128, [P, 2, 4, S])
        As = at("As", 144, [P, 2, 4, S])
        Gs = at("Gs", 152, [P, 2, 4, S])
        Wf = at("Wf", 160, [P, 4, S])
        Wh = at("Wh", 164, [P, 2, 4, S], F32R)
        Wl = at("Wl", 172, [P, 2, 4, S], F32R)
        zr = at("zr", 195, [P, 512], F32R)
        g_fin = at("g_fin", 197, [P, D])

        ps = [ctx.enter_context(nc.psum_tensor(f"ps{i}", [P, 512], F32)) for i in range(8)]
        ACTS = nc.dram_tensor("acts_dram", (KEYS, P, S), F32, kind="Internal").ap()
        GD = nc.dram_tensor("gates_dram", (KEYS * P * S, 1), F32, kind="Internal").ap()
        gd_zero = GD.rearrange("(z p n) o -> z p (n o)", p=P, n=1024)
        gd_slab = GD.rearrange("(n p t) o -> n p (t o)", p=P, t=S)

        plan = plan_banks()
        full = sems("full", 8)
        taken = sems("taken", 8)

        s_small = sem("s_small")
        s_bc = sem("s_bc")
        s_mem = sem("s_mem")
        s_x = sem("s_x")
        s_keys = sem("s_keys")
        s_gf = sem("s_gf")
        s_raw = sems("s_raw", SLOTS)
        s_hi = sem("s_hi")
        s_lo_pool = sem("s_lo_pool")
        s_lo_vec = sem("s_lo_vec")
        s_used = sem("s_used")
        s_cst = sem("s_cst")
        s_zero = sem("s_zero")
        s_gz = sem("s_gz")
        s_sq = sem("s_sq")
        s_ms = sem("s_ms")
        s_rt = sem("s_rt")
        s_xn = sem("s_xn")
        s_hc = sem("s_hc")
        s_dve = sem("s_dve")
        s_act = sem("s_act")
        s_par = sem("s_par")
        s_parv = sem("s_parv")
        s_bw = sem("s_bw")
        s_tA = sem("s_tA")
        s_tB = sem("s_tB")
        s_tC = sem("s_tC")
        s_tC2 = sem("s_tC2")
        s_dem = sem("s_dem")
        s_xs = sem("s_xs")
        s_ymm = sem("s_ymm")
        s_yv = sem("s_yv")
        s_ge = sem("s_ge")
        s_gl = sem("s_gl")
        s_g2 = sem("s_g2")
        s_mixs = sem("s_mixs")
        s_rope = sem("s_rope")
        s_smax = sem("s_smax")
        s_exp = sem("s_exp")
        s_comb = sem("s_comb")
        s_attn = sem("s_attn")
        s_hms = sem("s_hms")
        s_hrt = sem("s_hrt")
        s_xmax = sem("s_xmax")
        s_xexp = sem("s_xexp")
        s_xpn = sem("s_xpn")
        s_oxl = sem("s_oxl")
        s_pick = sem("s_pick")
        s_pexp = sem("s_pexp")
        s_idx = sem("s_idx")
        s_scat = sem("s_scat")
        s_ugelu = sem("s_ugelu")
        s_store = sems("s_store", 2)
        s_slab = sems("s_slab", 2)
        s_wmul = sem("s_wmul")
        s_w = sem("s_w")
        s_acc = sem("s_acc")
        s_fin = sem("s_fin")
        s_fo = sem("s_fo")
        s_out = sem("s_out")
        s_zr = sem("s_zr")
        s_ubank = sem("s_ubank")

        def fill_done(eng, name):
            b, _ = plan.at[name]
            if name in plan.unit:
                eng.wait_ge(s_used, plan.unit[name] + 1)
            else:
                eng.wait_ge(full[b], plan.fills[name])
            return ps[b]

        def stored(eng, name):
            b, n = plan.at[name]
            eng.wait_ge(taken[b], n + 1)

        def took(ins, name):
            return ins.then_inc(taken[plan.at[name][0]], 1)

        block = ctx.enter_context(nc.Block())

        @block.sync
        def _(sp):
            sp.dma_start(nat[:, :, :], T["mem"]).then_inc(s_mem, 16)

            def load(src, k):
                sp.dma_start(raw[k][:, :], src).then_inc(s_raw[k], 16)

            def segment(name, first, n):
                for j in range(n):
                    u = first + j
                    if u >= SLOTS:
                        sp.wait_ge(s_used, u - SLOTS + 1)
                    load(T[name][j], u % SLOTS)
                    if u == 0:
                        sp.dma_start(H[:, :, :], T["x"]).then_inc(s_x, 16)
                    if 4 <= u < 36:
                        if u == 4:
                            sp.wait_ge(s_zero, 1)
                        sp.dma_start(gd_zero[u - 4], zero[:, :]).then_inc(s_gz, 16)

            segment("w_mk", 0, 4)
            segment("w_mv", 4, 4)
            segment("w_u", UW0, 8)
            segment("w_qkv", QKV0, 24)
            segment("w_glu", GLU0, 4)
            segment("w_wo", WO0, 16)
            segment("w_xq", XQ0, 4)
            segment("w_xo", XO0, 4)
            sp.dma_start(keys[:, :, :], T["keys"]).then_inc(s_keys, 16)
            segment("w_pq", PQ0, 16)
            with sp.Fori(0, KEYS // 4) as i:
                for j in range(4):
                    sp.wait_ge(s_used, i * 4 + (U0 + j - SLOTS + 1))
                    load(T["u"][bass.ds(i * 4 + j, 1)].rearrange("a p n -> p (a n)"), j)
            for j in range(8):
                sp.wait_ge(s_used, V0 + j - SLOTS + 1)
                load(T["v"][j], j % 4)
                if j != 3:
                    continue
                sp.wait_ge(s_store[0], 16 * (KEYS // 8))
                sp.wait_ge(s_store[1], 16 * (KEYS // 8))
                sp.wait_ge(s_scat, 16 * NT * PH * TOPK)
                for g in range(2):
                    sp.dma_start(As[:, g], ACTS[4 * g:4 * g + 4].rearrange("n p t -> p n t")).then_inc(s_slab[g], 16)
                    sp.dma_start(Gs[:, g], gd_slab[4 * g:4 * g + 4].rearrange("n p t -> p n t")).then_inc(s_slab[g], 16)
            sp.dma_start(g_fin[:, :], T["g_fin"].to_broadcast([P, D])).then_inc(s_gf, 16)
            with sp.Fori(0, KEYS // 8 - 1) as i:
                for g in range(2):
                    sp.wait_ge(s_wmul, i * 2 + (g + 1))
                    n0 = i * 8 + (8 + 4 * g)
                    sp.dma_start(As[:, g], ACTS[bass.ds(n0, 4)].rearrange("n p t -> p n t")).then_inc(s_slab[g], 16)
                    sp.dma_start(Gs[:, g], gd_slab[bass.ds(n0, 4)].rearrange("n p t -> p n t")).then_inc(s_slab[g], 16)
                    for j in range(4):
                        sp.wait_ge(s_used, i * 8 + (V0 + 8 + 4 * g + j - SLOTS + 1))
                        load(T["v"][bass.ds(n0 + j, 1)].rearrange("a p n -> p (a n)"), j)
            for t in range(NT):
                sp.wait_ge(s_fo, t + 1)
                sp.dma_start(T["out"][t * P:(t + 1) * P, :], H[:, t]).then_inc(s_out, 16)
            sp.wait_ge(s_out, 16 * NT)

        @block.gpsimd
        def _(pool):
            G = nc.gpsimd
            G.memset(ident[:, :], 0.0).then_inc(s_cst, 1)
            G.memset(maskd[:, :, :], 0.0).then_inc(s_cst, 1)
            G.memset(zero[:, :], 0.0).then_inc(s_zero, 1)
            pool.wait_ge(s_cst, 2)
            G.affine_select(out=ident[:, :], in_=ident[:, :], compare_op=ALU.not_equal, fill=1.0,
                            base=0, pattern=[[-1, P]], channel_multiplier=1).then_inc(s_cst, 1)
            G.affine_select(out=maskd[:, 1, :], in_=maskd[:, 1, :], compare_op=ALU.is_ge, fill=NEG,
                            base=0, pattern=[[-1, P]], channel_multiplier=1).then_inc(s_cst, 1)
            G.iota(iota_t[:, :], [[1, S]], base=0, channel_multiplier=0,
                   allow_small_or_imprecise_dtypes=True).then_inc(s_cst, 1)
            for j in range(8):
                G.memset(freq[:, j:j + 1], ROPE[j]).then_inc(s_cst, 1)
            G.memset(eps[:, :], EPS).then_inc(s_cst, 1)
            G.memset(magic[:, :], ROUND).then_inc(s_cst, 1)
            G.memset(ones[:, :], 1.0).then_inc(s_cst, 1)
            G.memset(one[:, :], 1.0).then_inc(s_cst, 1)
            with pool.Fori(0, POOL_UNITS // SLOTS) as i:
                for j in range(SLOTS):
                    pool.wait_ge(s_hi, i * SLOTS + (j + 1))
                    G.tensor_tensor(lo[j][:, :], raw[j][:, :], hi[j][:, :].bitcast(F32),
                                    ALU.subtract).then_inc(s_lo_pool, 1)
            pool.wait_ge(s_idx, NT)
            pool.wait_ge(s_gz, 16 * 32)
            for h in range(PH):
                if h:
                    pool.wait_ge(s_scat, 16 * NT * TOPK * h)
                for t in range(NT):
                    for r in range(TOPK):
                        G.indirect_dma_start(GD, bass.IndirectOffsetOnAxis(ap=eidx[:, t, h, r:r + 1], axis=0),
                                             gate[:, t, h, r:r + 1], None,
                                             compute_op=ALU.add).then_inc(s_scat, 16)

        @block.scalar
        def _(act):
            A = nc.scalar
            own = Chain(act, s_act)
            smalls = [
                (gains[:, :, :], T["gains"]), (g_att[:, :], T["g_att"]), (g_ssm[:, :], T["g_ssm"]),
                (glu_b[:, :], T["glu_b"]), (d_skip[:, :], T["d_skip"]),
                (lamv[:, :, :], T["lam"].unsqueeze(0).to_broadcast([P, 4, QK])),
                (posi[:, :], T["pos"]), (prm[:, 0, :], T["a_re"]), (prm[:, 1, :], T["a_im"]),
                (prm[0:64, 2, :], T["log_dt"][0:1, :].to_broadcast([64, NBLK])),
                (prm[64:128, 2, :], T["log_dt"][1:2, :].to_broadcast([64, NBLK])),
            ]
            for dst, src in smalls:
                act.dma_start(dst, src).then_inc(s_small, 16)
            act.dma_start(braw[:, :, :, :], T["bT"]).then_inc(s_bc, 16)
            act.dma_start(craw[:, :, :, :], T["cT"]).then_inc(s_bc, 16)

            def split(u):
                act.wait_ge(s_raw[u % SLOTS], 16 * (u // SLOTS + 1))
                A.activation(hi[u % SLOTS][:, :], raw[u % SLOTS][:, :], ACT.Copy).then_inc(s_hi, 1)

            def norm_stats(kk, X):
                for t in range(NT):
                    if t or kk:
                        act.wait_ge(s_sq, NT * kk + t)
                    A.activation(junk[:, :], X[:, t], ACT.Square,
                                 accum_out=stat[:, 4 * (kk % 2) + t:4 * (kk % 2) + t + 1]).then_inc(s_sq, 1)
                act.wait_ge(s_ms, kk + 1)
                A.activation(stat[:, 8:8 + NT], stat[:, 4 * (kk % 2) + 2:4 * (kk % 2) + 4],
                             ACT.Sqrt).then_inc(s_rt, 1)

            def norm_hi(kk, g):
                for cp in range(8):
                    b = fill_done(act, ("norm", kk, cp))
                    for c in range(2):
                        A.activation(XTh[:, 2 * cp + c], b[:, 256 * c:256 * c + 256], ACT.Copy,
                                     scale=gains[:, g, 2 * cp + c:2 * cp + c + 1]).then_inc(s_hc, 1)

            act.wait_ge(s_small, 16 * len(smalls))
            act.wait_ge(s_cst, 17)
            own(A.activation(prm[:, 3, :], prm[:, 2, :], ACT.Exp))
            act.wait_ge(s_par, 1)
            own(A.activation(prm[:, 6, :], prm[:, 4, :], ACT.Exp))
            A.activation(lams[:, 2:4], lams[:, 0:2], ACT.Exp).then_inc(s_parv, 1)
            act.wait_ge(s_par, 2)
            own(A.activation(prm[:, 8, :], prm[:, 7, :], ACT.Sin))
            own(A.activation(prm[:, 9, :], prm[:, 7, :], ACT.Sin, scale=0.5))
            own(A.activation(rsin[:, :, :], rcos[:, :, :], ACT.Sin))
            own(A.activation(rcos[:, :, :], rcos[:, :, :], ACT.Sin, scale=0.5))
            own.settle()
            own(A.activation(prm[:, 9, :], prm[:, 9, :], ACT.Square, scale=math.sqrt(2.0)))
            own(A.activation(rcos[:, :, :], rcos[:, :, :], ACT.Square, scale=math.sqrt(2.0)))
            own.settle()
            A.activation(prm[:, 9, :], prm[:, 9, :], ACT.Identity, scale=-1.0, bias=one[:, 0:1]).then_inc(s_parv, 1)
            A.activation(rcos[:, :, :], rcos[:, :, :], ACT.Identity, scale=-1.0, bias=one[:, 0:1]).then_inc(s_parv, 1)

            act.wait_ge(s_mem, 16)
            norm_stats(0, nat)
            for u in range(3):
                split(u)
            norm_hi(0, 0)

            def phase_a(b):
                if b >= NBLK:
                    return
                if b == 0:
                    act.wait_ge(s_par, 3)
                    act.wait_ge(s_bw, 2)
                else:
                    act.wait_ge(s_tB, b)
                own(A.activation(phA[:, :], iota_t[:, :], ACT.Copy, scale=prm[:, 11, b:b + 1]))
                A.activation(phR[:, :], iota_t[:, :], ACT.Identity, scale=prm[:, 10, b:b + 1],
                             bias=magic[:, 0:1]).then_inc(s_tA, 1)

            def phase_c(b):
                if b >= NBLK:
                    return
                act.wait_ge(s_tB, b + 1)
                if b >= 2:
                    act.wait_ge(s_dem, b - 1)
                A.activation(tab[:, b % 2, 1], phF[:, :], ACT.Sin, scale=2 * PI_IN).then_inc(s_tC, 1)
                own(A.activation(phS[:, :], phF[:, :], ACT.Sin, scale=PI_IN))
                own.settle()
                own(A.activation(phS[:, :], phS[:, :], ACT.Square, scale=math.sqrt(2.0)))
                own.settle()
                A.activation(tab[:, b % 2, 0], phS[:, :], ACT.Identity, scale=-1.0,
                             bias=one[:, 0:1]).then_inc(s_tC, 1)

            def evac(name, dst, cols=slice(0, 256)):
                b = fill_done(act, name)
                took(A.activation(dst, b[:, cols], ACT.Copy), name)

            for j in range(4):
                split(j + 3)
                evac(("mk", j), kxT[:, j])
            act.wait_ge(s_x, 16)
            norm_stats(1, H)
            for j in range(4):
                split(j + 7)
            for t in range(2):
                evac(("mv", t), vx[:, t], slice(0, 512))
            norm_hi(1, 1)
            for j in range(8):
                split(UW0 + j + 3)
                evac(("uw", j), uT[:, j])
            phase_a(0)
            phase_c(0)
            phase_a(1)
            for cb in range(6):
                for j in range(4):
                    split(QKV0 + 4 * cb + j + 3)
                    if j == 3:
                        for t in range(2):
                            dst = zqk[:, t, 512 * cb:512 * cb + 512] if cb < 4 else \
                                vnat[:, t, 512 * (cb - 4):512 * (cb - 4) + 512]
                            evac(("qkv", cb, t), dst, slice(0, 512))
                    phase_c(4 * cb + j + 1)
                    phase_a(4 * cb + j + 2)

            def ssm_slot(s):
                phase_c(s + 1)
                phase_a(s + 2)

            for i in range(8):
                dst = (qT if i < 4 else kT)[:, 4 * (i % 2):4 * (i % 2) + 4, P * (i // 2 % 2):P * (i // 2 % 2) + P]
                b = fill_done(act, ("qkT", i))
                took(A.activation(dst, b[:, :].rearrange("p (h t) -> p h t", h=4), ACT.Copy), ("qkT", i))
            ssm_slot(24)
            ssm_slot(25)

            act.wait_ge(s_smax, 1)
            for i in range(2 * HEADS):
                A.activation(p0[:, i], p0[:, i], ACT.Exp, bias=st_max[:, i:i + 1],
                             accum_out=st_sum[:, i:i + 1]).then_inc(s_exp, 1)
            ssm_slot(26)
            ssm_slot(27)
            act.wait_ge(s_smax, 2)
            for i in range(2 * HEADS):
                A.activation(p1[:, i], p1[:, i], ACT.Exp, bias=st_max[:, 16 + i:17 + i],
                             accum_out=st_sum[:, 16 + i:17 + i]).then_inc(s_exp, 1)
            ssm_slot(28)
            ssm_slot(29)
            for i in range(6):
                b = fill_done(act, ("aT", i))
                dst = aT0[:, 4 * i:4 * i + 4] if i < 2 else aT1[:, 2 * (i - 2):2 * (i - 2) + 2]
                src = b[:, :].rearrange("p (h t) -> p h t", h=4) if i < 2 else \
                    b[:, :].rearrange("p (h k t) -> p h k t", h=2, k=2)
                took(A.activation(dst, src, ACT.Copy), ("aT", i))
            ssm_slot(30)
            ssm_slot(31)
            act.wait_ge(s_hms, 1)
            A.activation(head_ms[:, :], head_ms[:, :], ACT.Sqrt).then_inc(s_hrt, 1)
            for i in range(4):
                b = fill_done(act, ("oT", i))
                A.activation(mixh[:, 2 * i:2 * i + 2], b[:, :].rearrange("p (h t) -> p h t", h=2), ACT.Copy,
                             scale=g_att8[:, 0:1]).then_inc(s_hc, 1)

            for j in range(SSM_C):
                act.wait_ge(s_yv, j + 1)
                A.activation(yT[:, j], yT[:, j], ACT.Gelu).then_inc(s_ge, 1)
                act.wait_ge(s_ge, j + 1)
                A.activation(gTh[:, j], yT[:, j], ACT.Copy).then_inc(s_gl, 1)
            for j in range(4):
                split(GLU0 + j + 3)
                for c in range(2):
                    b = fill_done(act, ("glu", 2 * j + c))
                    took(A.activation(sig[:, 2 * j + c], b[:, 0:256], ACT.Sigmoid,
                                      bias=glu_b[:, 2 * j + c:2 * j + c + 1]), ("glu", 2 * j + c))
            for j in range(SSM_C):
                act.wait_ge(s_g2, j + 1)
                A.activation(sqb[:, j], yT[:, j], ACT.Square).then_inc(s_mixs, 1)
            b = fill_done(act, ("ssq", 0))
            took(A.activation(sig[:, 0], b[:, 0:256], ACT.Sqrt, scale=1.0 / SSM_W, bias=eps[:, 0:1]), ("ssq", 0))
            for j in range(SSM_C):
                act.wait_ge(s_g2, SSM_C + 1 + j)
                A.activation(mixh[:, SSM_C + j], yT[:, j], ACT.Copy).then_inc(s_hc, 1)
            for u in range(WO0, WO0 + 16):
                split(u + 3)

            for cb in range(4):
                for t in range(NT):
                    stored(act, ("wo", cb, t))
            norm_stats(2, H)
            norm_hi(2, 2)
            for j in range(4):
                split(XQ0 + j + 3)
                evac(("xq", j), qxT[:, j])
            act.wait_ge(s_xmax, 1)
            for t in range(NT):
                for h in range(XH):
                    A.activation(px[:, t, h], px[:, t, h], ACT.Exp, bias=st_max[:, 4 * t + h:4 * t + h + 1],
                                 accum_out=st_sum[:, 4 * t + h:4 * t + h + 1]).then_inc(s_xexp, 1)
            for h in range(XH):
                evac(("xp", h), pxT[:, h].rearrange("p k t -> p (k t)"), slice(0, 512))
            for h in range(XH):
                b = fill_done(act, ("xo", h))
                A.activation(oxh[:, h], b[:, 0:256], ACT.Copy).then_inc(s_hc, 1)
            for u in range(XO0, XO0 + 4):
                split(u + 3)

            for cb in range(4):
                for t in range(NT):
                    stored(act, ("xw", cb, t))
            norm_stats(3, H)
            norm_hi(3, 3)
            for c in range(16):
                split(PQ0 + c + 3)
                evac(("pq", c), qP[:, c])
            for i in range(8):
                t, c = i // 4, 4 * (i % 4)
                b = fill_done(act, ("ps", i))
                took(A.activation(sc[:, t, c:c + 4], b[:, :].rearrange("p (c n) -> p c n", c=4), ACT.Copy), ("ps", i))

            def unit_gelu(i, jj, u_base):
                g, j = jj // 4, jj % 4
                act.wait_ge(s_raw[(jj + 3) % SLOTS], i * 32 + 16 * ((u_base + jj + 3) // SLOTS + 1))
                A.activation(hi[(jj + 3) % SLOTS][:, :], raw[(jj + 3) % SLOTS][:, :], ACT.Copy).then_inc(s_hi, 1)
                if j == 0:
                    act.wait_ge(s_store[g], i * 16 + 16 * ((u_base - U0) // 8))
                act.wait_ge(s_used, i * 8 + (u_base + jj + 1))
                A.activation(gbuf[:, g, j], ps[j][:, 0:256], ACT.Gelu).then_inc(s_ubank, 1)
                if j == 3:
                    act.wait_ge(s_ubank, i * 8 + (u_base - U0 + jj + 1 + 4))
                    n0 = i * 8 + (u_base - U0 + 4 * g)
                    act.dma_start(ACTS[bass.ds(n0, 4)].rearrange("n p t -> p n t"), gbuf[:, g]).then_inc(s_store[g], 16)

            for t in range(NT):
                for i in range(2):
                    for jj in range(8):
                        unit_gelu(2 * t + i, jj, U0)
                act.wait_ge(s_pick, t + 1)
                A.activation(gate[:, t], gate[:, t], ACT.Exp).then_inc(s_pexp, 1)
            with act.Fori(0, KEYS // 8 - 4) as i:
                for jj in range(8):
                    unit_gelu(i, jj, U0 + 32)
            for u in range(V0 + 3, V0 + 8):
                split(u)
            with act.Fori(0, KEYS // 8 - 1) as i:
                for j in range(8):
                    act.wait_ge(s_raw[j % SLOTS], i * 32 + 16 * ((V0 + 8 + j) // SLOTS + 1))
                    A.activation(hi[j % SLOTS][:, :], raw[j % SLOTS][:, :], ACT.Copy).then_inc(s_hi, 1)
            for t in range(NT):
                act.wait_ge(s_acc, 1)
                act.wait_ge(s_fin, 4 * (t + 1))
                A.activation(raw[0][:, :], H[:, t], ACT.Square, accum_out=stat[:, t:t + 1]).then_inc(s_sq, 1)
                act.wait_ge(s_ms, 5 + t)
                A.activation(stat[:, 8 + t:9 + t], stat[:, 2 + t:3 + t], ACT.Sqrt).then_inc(s_rt, 1)

        @block.vector
        def _(dve):
            V = nc.vector
            own = Chain(dve, s_dve)

            def pr(n):
                return prm[:, n, :]

            dve.wait_ge(s_small, 16 * 11)
            dve.wait_ge(s_act, 1)
            own(V.tensor_tensor(pr(4), pr(0), pr(3), ALU.mult))
            own(V.tensor_tensor(pr(5), pr(1), pr(3), ALU.mult))
            own(V.tensor_tensor_reduce(lamv[:, 0], lamv[:, 0], lamv[:, 1], 1.0, 0.0, ALU.mult, ALU.add, lams[:, 0:1]))
            own(V.tensor_tensor_reduce(lamv[:, 2], lamv[:, 2], lamv[:, 3], 1.0, 0.0, ALU.mult, ALU.add, lams[:, 1:2]))
            own.settle()
            V.tensor_copy(posf[:, :], posi[:, :]).then_inc(s_par, 1)
            dve.wait_ge(s_par, 1)
            dve.wait_ge(s_cst, 17)

            def reduce_angle(x, kk, tmp):
                own(V.tensor_scalar(kk, x, 1.0 / TWO_PI, ROUND, ALU.mult, ALU.add))
                own.settle()
                own(V.tensor_scalar(kk, kk, -ROUND, None, ALU.add))
                own.settle()
                for c in (C1, C2, C3):
                    own(V.tensor_scalar(tmp, kk, -c, None, ALU.mult))
                    own.settle()
                    own(V.tensor_tensor(x, x, tmp, ALU.add))
                    own.settle()
                own(V.tensor_scalar(x, x, PI_IN, -PI_IN, ALU.min, ALU.max))
                own.settle()

            own(V.tensor_copy(pr(7), pr(5)))
            for t in range(NT):
                own(V.tensor_scalar(rcos[:, t], freq[:, :], posf[:, t:t + 1], None, ALU.mult))
            own.settle()
            rc = rcos[:, :, :].rearrange("p t j -> p (t j)")
            rs = rsin[:, :, :].rearrange("p t j -> p (t j)")
            reduce_angle(rc, rs, pr(18)[:, 0:16])
            reduce_angle(pr(7), pr(18), pr(19))
            dve.wait_ge(s_parv, 1)
            own(V.tensor_tensor(lams[:, 4:5], lams[:, 3:4], lams[:, 2:3], ALU.subtract))
            V.tensor_scalar(g_att8[:, :], g_att[:, :], 1.0 - LAM_INIT, None, ALU.mult).then_inc(s_par, 1)
            own.settle()
            own(V.tensor_scalar(lams[:, 5:6], lams[:, 4:5], -LAM_INIT, None, ALU.add))
            own(V.tensor_scalar(pr(10), pr(7), 1.0 / TWO_PI, None, ALU.mult))
            own.settle()
            own(V.tensor_scalar(pr(11), pr(10), ROUND15, None, ALU.add))
            own.settle()
            own(V.tensor_scalar(pr(11), pr(11), -ROUND15, None, ALU.add))
            own.settle()
            V.tensor_tensor(pr(12), pr(10), pr(11), ALU.subtract).then_inc(s_par, 1)
            dve.wait_ge(s_bc, 32)
            odd = ident[:, :].rearrange("p (q g h) -> p q g h", q=4, g=2)
            for g in range(2):
                own(V.tensor_reduce(half_mask[:, g:g + 1], odd[:, :, g, :], AX.XY, ALU.add))
            own.settle()
            for c in range(2):
                for g in range(2):
                    last = V.tensor_scalar(BW[:, c, :, 64 * g:64 * g + 64], braw[:, c], half_mask[:, g:g + 1],
                                           None, ALU.mult)
                    own(last)
            dve.wait_ge(s_parv, 3)
            own(V.tensor_tensor(pr(13), pr(6), pr(9), ALU.mult))
            own(V.tensor_tensor(pr(14), pr(6), pr(8), ALU.mult))
            own(V.tensor_tensor(pr(15), pr(0), pr(0), ALU.mult))
            own(V.tensor_tensor(pr(16), pr(1), pr(1), ALU.mult))
            own.settle()
            own(V.tensor_tensor(pr(15), pr(15), pr(16), ALU.add))
            own(V.tensor_scalar(pr(13), pr(13), -1.0, None, ALU.add))
            own.settle()
            own(V.reciprocal(pr(15), pr(15)))
            own(V.tensor_tensor(pr(16), pr(13), pr(0), ALU.mult))
            own(V.tensor_tensor(pr(17), pr(14), pr(1), ALU.mult))
            own(V.tensor_tensor(pr(18), pr(14), pr(0), ALU.mult))
            own(V.tensor_tensor(pr(19), pr(13), pr(1), ALU.mult))
            own.settle()
            own(V.tensor_tensor(pr(16), pr(16), pr(17), ALU.add))
            own(V.tensor_tensor(pr(18), pr(18), pr(19), ALU.subtract))
            own.settle()
            own(V.tensor_tensor(pr(16), pr(16), pr(15), ALU.mult))
            own(V.tensor_tensor(pr(18), pr(18), pr(15), ALU.mult))
            own(V.memset(CW[:, :, :, :], 0.0))
            own.settle()
            fre = pr(16).unsqueeze(2).to_broadcast([P, NBLK, 16])
            fim = pr(18).unsqueeze(2).to_broadcast([P, NBLK, 16])
            own(V.tensor_tensor(ctmp[:, 0], craw[:, 0], fre, ALU.mult))
            own(V.tensor_tensor(ctmp[:, 1], craw[:, 1], fim, ALU.mult))
            own.settle()
            for g in range(2):
                r = slice(64 * g, 64 * g + 64)
                own(V.tensor_tensor(CW[r, :, 0, 16 * g:16 * g + 16], ctmp[r, 0], ctmp[r, 1], ALU.subtract))
            own.settle()
            own(V.scalar_tensor_tensor(ctmp[:, 0], craw[:, 0], -1.0, fim, ALU.mult, ALU.mult))
            own(V.tensor_tensor(ctmp[:, 1], craw[:, 1], fre, ALU.mult))
            own.settle()
            for g in range(2):
                r = slice(64 * g, 64 * g + 64)
                V.tensor_tensor(CW[r, :, 1, 16 * g:16 * g + 16], ctmp[r, 0], ctmp[r, 1],
                                ALU.subtract).then_inc(s_bw, 1)

            def norm_rows(kk, X, dst):
                o = 4 * (kk % 2)
                dve.wait_ge(s_sq, NT * (kk + 1))
                V.tensor_scalar(stat[:, o + 2:o + 4], stat[:, o:o + 2], 1.0 / D, EPS, ALU.mult,
                                ALU.add).then_inc(s_ms, 1)
                dve.wait_ge(s_rt, kk + 1)
                own(V.reciprocal(stat[:, 12:14], stat[:, 8:10]))
                own.settle()
                for t in range(NT):
                    V.tensor_scalar(dst[:, t], X[:, t], stat[:, 12 + t:13 + t], None, ALU.mult).then_inc(s_xn, 1)

            def norm_lo(kk, g, hc0):
                for cp in range(8):
                    dve.wait_ge(s_hc, hc0 + 2 * cp + 2)
                    for c in range(2):
                        ins = V.scalar_tensor_tensor(XTl[:, 2 * cp + c], fill_done(dve, ("norm", kk, cp))[:, 256 * c:256 * c + 256],
                                                     gains[:, g, 2 * cp + c:2 * cp + c + 1],
                                                     XTh[:, 2 * cp + c].bitcast(F32), ALU.mult, ALU.subtract)
                        if c == 0:
                            own(ins)
                        else:
                            took(ins, ("norm", kk, cp))

            norm_rows(0, nat, nat)
            norm_lo(0, 0, 0)
            stored(dve, ("norm", 0, 7))
            norm_rows(1, H, nat)
            norm_lo(1, 1, 16)

            def phase_b(b):
                if b >= NBLK:
                    return
                dve.wait_ge(s_tA, b + 1)
                if b >= 1:
                    dve.wait_ge(s_tC, 2 * b)
                own(V.scalar_tensor_tensor(phR[:, :], phR[:, :], ROUND, phA[:, :], ALU.subtract, ALU.subtract))
                own.settle()
                own(V.scalar_tensor_tensor(phF[:, :], iota_t[:, :], prm[:, 12, b:b + 1], phR[:, :],
                                           ALU.mult, ALU.subtract))
                own.settle()
                V.tensor_scalar(phF[:, :], phF[:, :], 0.5, -0.5, ALU.min, ALU.max).then_inc(s_tB, 1)

            def scan_block(b):
                if b >= NBLK:
                    return
                bank = fill_done(dve, ("bu", b))[:, :].rearrange("p (c t) -> p c t", c=2)
                dve.wait_ge(s_tC, 2 * b + 2)
                if b:
                    dve.wait_ge(s_xs, 2 * b)
                cos = tab[:, b % 2, 0:1].to_broadcast([P, 2, S])
                sin = tab[:, b % 2, 1:2].to_broadcast([P, 2, S])
                own(V.tensor_tensor(m1[:, :, :], bank, cos, ALU.mult))
                took(V.tensor_tensor(m2[:, :, :], bank, sin, ALU.mult), ("bu", b))
                own.settle()
                stored(dve, ("bu", b))
                own(V.tensor_tensor(wmod[:, 0], m1[:, 0], m2[:, 1], ALU.add))
                own(V.tensor_tensor(wmod[:, 1], m1[:, 1], m2[:, 0], ALU.subtract))
                own.settle()
                r = prm[:, 6, b:b + 1].to_broadcast([P, S])
                for c in range(2):
                    own(V.tensor_tensor_scan(sst[:, c], r, wmod[:, c], 0.0, ALU.mult, ALU.add))
                own.settle()
                own(V.tensor_tensor(m1[:, :, :], sst[:, :, :], cos, ALU.mult))
                V.tensor_tensor(m2[:, :, :], sst[:, :, :], sin, ALU.mult).then_inc(s_dem, 1)
                own.settle()
                dve.wait_ge(s_dem, b + 1)
                if b >= 1:
                    dve.wait_ge(s_ymm, b)
                V.tensor_tensor(xst[:, 0], m1[:, 0], m2[:, 1], ALU.subtract).then_inc(s_xs, 1)
                V.tensor_tensor(xst[:, 1], m1[:, 1], m2[:, 0], ALU.add).then_inc(s_xs, 1)

            def y_out(j):
                dve.wait_ge(s_ymm, 4 * j + 4)
                V.scalar_tensor_tensor(yT[:, j], uT[:, j], d_skip[:, j:j + 1], ps[6 + j % 2][:, 0:256],
                                       ALU.mult, ALU.add).then_inc(s_yv, 1)

            def slot(s):
                phase_b(s + 1)
                scan_block(s)
                if s % 4 == 2 and s >= 6:
                    y_out(s // 4 - 1)

            def rope(t, kq):
                z = zqk[:, t, ATT * kq:ATT * kq + ATT].rearrange("p (h d) -> p h d", d=QK)
                r1, r2 = z[:, :, 0:8], z[:, :, 8:16]
                c = rcos[:, t:t + 1].to_broadcast([P, 16, 8])
                s = rsin[:, t:t + 1].to_broadcast([P, 16, 8])
                a = m1[:, :, :].rearrange("p a (b h d) -> p (a b) h d", b=2, d=8)
                if t or kq:
                    dve.wait_ge(s_rope, 2 * (2 * kq + t))
                own(V.tensor_tensor(a[:, 0], r1, c, ALU.mult))
                own(V.tensor_tensor(a[:, 1], r2, s, ALU.mult))
                own(V.tensor_tensor(a[:, 2], r1, s, ALU.mult))
                own(V.tensor_tensor(a[:, 3], r2, c, ALU.mult))
                own.settle()
                V.tensor_tensor(r1, a[:, 0], a[:, 1], ALU.subtract).then_inc(s_rope, 1)
                V.tensor_tensor(r2, a[:, 2], a[:, 3], ALU.add).then_inc(s_rope, 1)

            phase_b(0)
            for s in range(24):
                slot(s)
                if s in (8, 16):
                    dve.wait_ge(s_xs, 2 * s + 2)
                if s == 8:
                    for t in range(NT):
                        stored(dve, ("qkv", 1, t))
                        rope(t, 0)
                if s == 16:
                    for t in range(NT):
                        stored(dve, ("qkv", 3, t))
                        rope(t, 1)

            for i in range(4):
                b = fill_done(dve, ("s0", i))
                o = 8 * (i % 2) + i // 2
                took(V.scalar_tensor_tensor(p0[:, o:o + 7:2], b[:, :].rearrange("p (c n) -> p c n", c=4), QK ** -0.5,
                                            maskd[:, 1:2].to_broadcast([P, 4, P]), ALU.mult, ALU.add), ("s0", i))
            for i in range(4):
                stored(dve, ("s0", i))
            own(V.tensor_reduce(st_max[:, 0:16], p0[:, :, :], AX.X, ALU.max))
            own.settle()
            V.tensor_scalar(st_max[:, 0:16], st_max[:, 0:16], -1.0, None, ALU.mult).then_inc(s_smax, 1)
            for h in range(HEADS):
                b = fill_done(dve, ("s1", h))
                o = 4 * (h // 2) + h % 2
                took(V.scalar_tensor_tensor(p1[:, o:o + 3:2], b[:, :].rearrange("p (c n) -> p c n", c=2), QK ** -0.5,
                                            maskd[:, :, :].rearrange("p a n -> p (a n)").unsqueeze(1).to_broadcast([P, 2, S]),
                                            ALU.mult, ALU.add), ("s1", h))
            for h in range(4, 8):
                stored(dve, ("s1", h))
            own(V.tensor_reduce(st_max[:, 16:32], p1[:, :, :], AX.X, ALU.max))
            own.settle()
            V.tensor_scalar(st_max[:, 16:32], st_max[:, 16:32], -1.0, None, ALU.mult).then_inc(s_smax, 1)
            slot(24)
            slot(25)

            def combine(p, o):
                dve.wait_ge(s_exp, o + 16)
                own(V.reciprocal(st_rec[:, o:o + 16], st_sum[:, o:o + 16]))
                own.settle()
                own(V.tensor_scalar(st_rec[:, o + 1:o + 16:2], st_rec[:, o + 1:o + 16:2], lams[:, 5:6], None, ALU.mult))
                own.settle()
                for h in range(HEADS):
                    own(V.tensor_scalar(p[:, 2 * h + 1], p[:, 2 * h + 1], st_rec[:, o + 2 * h + 1:o + 2 * h + 2], None, ALU.mult))
                own.settle()
                for h in range(HEADS):
                    V.scalar_tensor_tensor(p[:, 2 * h], p[:, 2 * h], st_rec[:, o + 2 * h:o + 2 * h + 1],
                                           p[:, 2 * h + 1], ALU.mult, ALU.add).then_inc(s_comb, 1)

            combine(p0, 0)
            slot(26)
            slot(27)
            combine(p1, 16)
            slot(28)
            slot(29)
            slot(30)
            slot(31)
            y_out(7)
            sq = [m1, m2, wmod, sst]
            for i in range(4):
                b = fill_done(dve, ("av", i))
                own(V.tensor_copy(xst[:, :, :].rearrange("p a n -> p (a n)") if i % 2 else
                                  tab[:, 0].rearrange("p a n -> p (a n)"), b[:, :]))
                own.settle()
                src = xst[:, :, :].rearrange("p a n -> p (a n)") if i % 2 else tab[:, 0].rearrange("p a n -> p (a n)")
                own(V.tensor_tensor(sq[i][:, :, :].rearrange("p a n -> p (a n)"), src, src, ALU.mult))
                own.settle()
                own(V.tensor_reduce(head_ms[:, 4 * i:4 * i + 4],
                                    sq[i][:, :, :].rearrange("p a (h e) -> p (a h) e", e=P), AX.X, ALU.add))
            own.settle()
            V.tensor_scalar(head_ms[:, :], head_ms[:, :], 1.0 / P, EPS, ALU.mult, ALU.add).then_inc(s_hms, 1)
            dve.wait_ge(s_hrt, 1)
            own(V.reciprocal(head_ms[:, :], head_ms[:, :]))
            own.settle()
            for i in range(4):
                t, hf = i // 2, i % 2
                b = fill_done(dve, ("av", i))
                took(V.tensor_tensor(att_n[:, t, 512 * hf:512 * hf + 512].rearrange("p (h e) -> p h e", h=4),
                                     b[:, :].rearrange("p (h e) -> p h e", h=4),
                                     head_ms[:, 4 * i:4 * i + 4].unsqueeze(2).to_broadcast([P, 4, P]), ALU.mult), ("av", i))
            for i in range(4):
                dve.wait_ge(s_hc, 32 + i + 1)
                b = fill_done(dve, ("oT", i))
                took(V.scalar_tensor_tensor(mixl[:, 2 * i:2 * i + 2], b[:, :].rearrange("p (h t) -> p h t", h=2),
                                            g_att8[:, 0:1], mixh[:, 2 * i:2 * i + 2].bitcast(F32),
                                            ALU.mult, ALU.subtract), ("oT", i))

            for j in range(SSM_C):
                dve.wait_ge(s_gl, j + 1)
                V.tensor_tensor(gTl[:, j], yT[:, j], gTh[:, j].bitcast(F32), ALU.subtract).then_inc(s_bw, 1)
            for j in range(SSM_C):
                stored(dve, ("glu", j))
                V.tensor_tensor(yT[:, j], yT[:, j], sig[:, j], ALU.mult).then_inc(s_g2, 1)
            stored(dve, ("ssq", 0))
            own(V.reciprocal(sig[:, 0], sig[:, 0]))
            own.settle()
            for j in range(SSM_C):
                V.scalar_tensor_tensor(yT[:, j], yT[:, j], g_ssm[:, j:j + 1], sig[:, 0], ALU.mult,
                                       ALU.mult).then_inc(s_g2, 1)
            for j in range(SSM_C):
                dve.wait_ge(s_hc, 36 + j + 1)
                V.tensor_tensor(mixl[:, SSM_C + j], yT[:, j], mixh[:, SSM_C + j].bitcast(F32),
                                ALU.subtract).then_inc(s_mixs, 1)

            def residual(name, cb, t):
                b = fill_done(dve, (name, cb, t))
                took(V.tensor_tensor(H[:, t, 512 * cb:512 * cb + 512], b[:, :], H[:, t, 512 * cb:512 * cb + 512],
                                     ALU.add), (name, cb, t))

            for cb in range(4):
                for t in range(NT):
                    residual("wo", cb, t)
            norm_rows(2, H, nat)
            norm_lo(2, 2, 44)
            for i in range(4):
                t, hp = i // 2, i % 2
                b = fill_done(dve, ("xs", i))
                took(V.tensor_scalar(px[:, t, 2 * hp:2 * hp + 2], b[:, :].rearrange("p (h m) -> p h m", h=2),
                                     P ** -0.5, None, ALU.mult), ("xs", i))
            for i in range(4):
                stored(dve, ("xs", i))
            own(V.tensor_reduce(st_max[:, 0:8], px[:, :, :, :].rearrange("p t h m -> p (t h) m"), AX.X, ALU.max))
            own.settle()
            V.tensor_scalar(st_max[:, 0:8], st_max[:, 0:8], -1.0, None, ALU.mult).then_inc(s_xmax, 1)
            dve.wait_ge(s_xexp, 8)
            own(V.reciprocal(st_rec[:, 0:8], st_sum[:, 0:8]))
            own.settle()
            for h in range(XH):
                for t in range(NT):
                    V.tensor_scalar(px[:, t, h], px[:, t, h], st_rec[:, 4 * t + h:4 * t + h + 1], None,
                                    ALU.mult).then_inc(s_xpn, 1)
            for h in range(XH):
                dve.wait_ge(s_hc, 60 + h + 1)
                b = fill_done(dve, ("xo", h))
                took(V.tensor_tensor(oxl[:, h], b[:, 0:256], oxh[:, h].bitcast(F32), ALU.subtract), ("xo", h))
            for cb in range(4):
                for t in range(NT):
                    residual("xw", cb, t)
            norm_rows(3, H, nat)
            norm_lo(3, 3, 64)

            own(V.tensor_copy(io16[:, :], iota_t[:, 0:TOPK]))
            own(V.tensor_tensor_reduce(repl[:, 0:P], ident[:, :], iota_t[:, 0:P], 1.0, 0.0, ALU.mult, ALU.add,
                                       tokf[:, 0:1]))
            own.settle()
            own(V.tensor_scalar(tokf[:, 1:2], tokf[:, 0:1], float(P), None, ALU.add))

            def top16(vals, idx, x):
                n = x.shape[1]
                own(V.max(vals[:, 0:8], x))
                own.settle()
                own(V.max_index(idx[:, 0:8], vals[:, 0:8], x))
                own(V.match_replace(repl[:, 0:n], vals[:, 0:8], x, -3e38))
                own.settle()
                own(V.max(vals[:, 8:16], repl[:, 0:n]))
                own.settle()
                own(V.max_index(idx[:, 8:16], vals[:, 8:16], repl[:, 0:n]))

            for t in range(NT):
                for i in range(8):
                    stored(dve, ("ps", i))
                for c in range(2 * PH):
                    top16(tv[:, c], ti[:, c], sc[:, t, c])
                own.settle()
                own(V.tensor_copy(tif[:, :, :], ti[:, :, :]))
                tv4 = tv[:, :, :].rearrange("p (h s) a -> p h s a", s=2)
                own(V.tensor_tensor(cand[:, :, :, :], tv4[:, :, 0].unsqueeze(3).to_broadcast([P, PH, TOPK, TOPK]),
                                    tv4[:, :, 1].unsqueeze(2).to_broadcast([P, PH, TOPK, TOPK]), ALU.add))
                own.settle()
                for h in range(PH):
                    top16(ts[:, h], ic[:, h], cand[:, h].rearrange("p a b -> p (a b)"))
                own.settle()
                own(V.tensor_tensor(gate[:, t], ts[:, :, :], ts[:, :, 0:1].to_broadcast([P, PH, TOPK]), ALU.subtract))
                own(V.tensor_single_scalar(icx[:, 0], ic[:, :, :], 4, ALU.logical_shift_right))
                own(V.tensor_single_scalar(icx[:, 1], ic[:, :, :], 15, ALU.bitwise_and))
                own.settle()
                V.tensor_copy(icf[:, :, :, :], icx[:, :, :, :]).then_inc(s_pick, 1)
                dve.wait_ge(s_pick, t + 1)
                tif4 = tif[:, :, :].rearrange("p (h s) a -> p h s a", s=2)
                for x in range(2):
                    own(V.tensor_tensor(eq[:, :, :, :], icf[:, x].unsqueeze(3).to_broadcast([P, PH, TOPK, TOPK]),
                                        io16[:, :].unsqueeze(1).unsqueeze(1).to_broadcast([P, PH, TOPK, TOPK]), ALU.is_equal))
                    own.settle()
                    own(V.tensor_tensor(eqv[:, :, :, :], eq[:, :, :, :],
                                        tif4[:, :, x].unsqueeze(2).to_broadcast([P, PH, TOPK, TOPK]), ALU.mult))
                    own.settle()
                    own(V.tensor_reduce(ef[:, x], eqv[:, :, :, :], AX.X, ALU.add))
                own.settle()
                own(V.scalar_tensor_tensor(ei[:, :, :], ef[:, 1], float(KEYS), ef[:, 0], ALU.mult, ALU.add))
                own.settle()
                own(V.tensor_scalar(ei[:, :, :], ei[:, :, :], float(S), tokf[:, t:t + 1], ALU.mult, ALU.add))
                dve.wait_ge(s_pexp, t + 1)
                own(V.tensor_reduce(g1[:, :], gate[:, t], AX.X, ALU.add))
                own.settle()
                own(V.reciprocal(g2[:, :], g1[:, :]))
                own.settle()
                own(V.tensor_tensor(gate[:, t], gate[:, t], g2[:, :].unsqueeze(2).to_broadcast([P, PH, TOPK]), ALU.mult))
                own.settle()
                V.tensor_copy(eidx[:, t], ei[:, :, :]).then_inc(s_idx, 1)

            def rest(i, j, base_hi, per):
                dve.wait_ge(s_hi, i * per + (base_hi + j + 1))
                V.tensor_tensor(lo[j % SLOTS][:, :], raw[j % SLOTS][:, :], hi[j % SLOTS][:, :].bitcast(F32),
                                ALU.subtract).then_inc(s_lo_vec, 1)

            with dve.Fori(0, (KEYS - UA) // 4) as i:
                for j in range(4):
                    rest(i, j, POOL_UNITS, 4)
            V.memset(zr[:, :].bitcast(F32), 0.0).then_inc(s_zr, 1)
            with dve.Fori(0, KEYS // 8) as i:
                for g in range(2):
                    dve.wait_ge(s_slab[g], i * 32 + 32)
                    dve.wait_ge(s_used, i * 8 + (V0 + 4 * g - 4))
                    dve.wait_ge(s_w, i * 4 + 2 * g)
                    V.tensor_tensor(Wf[:, :, :], As[:, g], Gs[:, g], ALU.mult).then_inc(s_wmul, 1)
                    dve.wait_ge(s_wmul, i * 2 + (g + 1))
                    V.tensor_copy(Wh[:, g], Wf[:, :, :]).then_inc(s_w, 1)
                    dve.wait_ge(s_w, i * 4 + (2 * g + 1))
                    V.tensor_tensor(Wl[:, g], Wf[:, :, :], Wh[:, g].bitcast(F32), ALU.subtract).then_inc(s_w, 1)
                    for j in range(4):
                        rest(i, 4 * g + j, V0, 8)
            dve.wait_ge(s_acc, 1)
            dve.wait_ge(s_gf, 16)
            for t in range(NT):
                for c in range(4):
                    V.tensor_tensor(H[:, t, 512 * c:512 * c + 512], ps[4 * t + c][:, :],
                                    H[:, t, 512 * c:512 * c + 512], ALU.add).then_inc(s_fin, 1)
            for t in range(NT):
                dve.wait_ge(s_sq, 2 * 4 + t + 1)
                V.tensor_scalar(stat[:, 2 + t:3 + t], stat[:, t:t + 1], 1.0 / D, EPS, ALU.mult, ALU.add).then_inc(s_ms, 1)
                dve.wait_ge(s_rt, 4 + t + 1)
                own(V.reciprocal(stat[:, 12 + t:13 + t], stat[:, 8 + t:9 + t]))
                own.settle()
                dve.wait_ge(s_fin, 4 * (t + 1))
                V.scalar_tensor_tensor(H[:, t], H[:, t], stat[:, 12 + t:13 + t], g_fin[:, :], ALU.mult,
                                       ALU.mult).then_inc(s_fo, 1)

        @block.tensor
        def _(pe):
            M = nc.tensor

            def bank(name):
                b, n = plan.at[name]
                if n:
                    pe.wait_ge(taken[b], n)
                return ps[b]

            def filled(ins, name):
                ins.then_inc(full[plan.at[name][0]], 1)

            def used(ins):
                ins.then_inc(s_used, 1)

            def unit(u):
                pe.wait_ge(s_lo_pool, u + 1)

            def three(out, wh, wl, xh, xl, start, stop):
                M.matmul(out, wh, xh, start=start, stop=False)
                M.matmul(out, wh, xl, start=False, stop=False)
                return M.matmul(out, wl, xh, start=False, stop=stop)

            def norm(kk):
                for cp in range(8):
                    b = bank(("norm", kk, cp))
                    if cp == 0:
                        pe.wait_ge(s_xn, NT * (kk + 1))
                    for c in range(2):
                        for t in range(NT):
                            ins = M.transpose(b[:, 256 * c + P * t:256 * c + P * t + P],
                                              nat[:, t, P * (2 * cp + c):P * (2 * cp + c) + P], ident[:, :])
                    filled(ins, ("norm", kk, cp))

            def cols_unit(name, u, xh=XTh, xl=XTl):
                b = bank(name)
                unit(u)
                s = u % SLOTS
                for c in range(DC):
                    ins = three(b[:, 0:256], hi[s][:, P * c:P * c + P], lo[s][:, P * c:P * c + P],
                                xh[:, c], xl[:, c], c == 0, c == DC - 1)
                ins.then_inc(s_used, 1)

            def rows_block(name, u0, n, xh, xl, after=None):
                b = [bank((*name, t)) for t in range(NT)]
                for q in range(n):
                    unit(u0 + q)
                    s = (u0 + q) % SLOTS
                    for c in range(4):
                        for t in range(NT):
                            k = 4 * q + c
                            x_h, x_l = xh[:, k, P * t:P * t + P], xl[:, k, P * t:P * t + P]
                            w_h, w_l = hi[s][:, 512 * c:512 * c + 512], lo[s][:, 512 * c:512 * c + 512]
                            M.matmul(b[t][:, :], x_h, w_h, start=k == 0, stop=False)
                            M.matmul(b[t][:, :], x_h, w_l, start=False, stop=False)
                            ins = M.matmul(b[t][:, :], x_l, w_h, start=False, stop=k == 4 * n - 1)
                    used(ins)
                    if after:
                        after(q)

            pe.wait_ge(s_cst, 17)
            norm(0)
            for cp in range(8):
                stored(pe, ("norm", 0, cp))
            for j in range(4):
                cols_unit(("mk", j), j)
            rows_block(("mv",), 4, 4, XTh, XTl)
            norm(1)
            for cp in range(8):
                stored(pe, ("norm", 1, cp))
            for j in range(8):
                cols_unit(("uw", j), UW0 + j)
            for j in range(8):
                stored(pe, ("uw", j))
            pe.wait_ge(s_bw, 2)

            def bu(b):
                if b >= NBLK:
                    return
                j, q = b // 4, b % 4
                r = slice(32 * q, 32 * q + 32)
                out = bank(("bu", b))
                for c in range(2):
                    ins = M.matmul(out[:, 256 * c:256 * c + 256], BW[r, c, j], uT[r, j], start=True, stop=True,
                                   skip_group_check=True)
                filled(ins, ("bu", b))

            def y(b):
                if b < 0:
                    return
                j, q = b // 4, b % 4
                if q == 0 and j >= 2:
                    pe.wait_ge(s_yv, j - 1)
                pe.wait_ge(s_xs, 2 * b + 2)
                out = ps[6 + j % 2][32 * q:32 * q + 32, 0:256]
                M.matmul(out, CW[:, b, 0], xst[:, 0], start=True, stop=False, skip_group_check=True)
                M.matmul(out, CW[:, b, 1], xst[:, 1], start=False, stop=True,
                         skip_group_check=True).then_inc(s_ymm, 1)

            def slot(s):
                bu(s)
                y(s - 1)

            for cb in range(6):
                def after(q, cb=cb):
                    slot(4 * cb + q)
                rows_block(("qkv", cb), QKV0 + 4 * cb, 4, XTh, XTl, after)

            for i in range(8):
                kq, t, hf = i // 4, i // 2 % 2, i % 2
                b = bank(("qkT", i))
                pe.wait_ge(s_rope, 4 * kq + 4)
                for x in range(4):
                    col = ATT * kq + P * (4 * hf + x)
                    ins = M.transpose(b[:, P * x:P * x + P], zqk[:, t, col:col + P], ident[:, :])
                filled(ins, ("qkT", i))
            for i in range(8):
                stored(pe, ("qkT", i))
            for i in range(4):
                b = bank(("s0", i))
                c = i // 2
                r = slice(64 * c, 64 * c + 64)
                for x in range(4):
                    h = 4 * (i % 2) + x
                    ins = M.matmul(b[:, P * x:P * x + P], qT[r, h, 0:P], kT[r, h, 0:P], start=True, stop=True,
                                   skip_group_check=True)
                filled(ins, ("s0", i))
            for i in range(8):
                b = bank(("s1", i))
                c = i % 2
                r = slice(64 * c, 64 * c + 64)
                for x in range(2):
                    h = 2 * (i // 2) + x
                    ins = M.matmul(b[:, S * x:S * x + S], qT[r, h, P:S], kT[r, h, 0:S], start=True, stop=True,
                                   skip_group_check=True)
                filled(ins, ("s1", i))
            slot(24)
            slot(25)
            slot(26)
            for i in range(2):
                b = bank(("aT", i))
                pe.wait_ge(s_comb, 4 * i + 4)
                for x in range(4):
                    ins = M.transpose(b[:, P * x:P * x + P], p0[:, 2 * (4 * i + x)], ident[:, :])
                filled(ins, ("aT", i))
            slot(27)
            slot(28)
            for i in range(4):
                b = bank(("aT", 2 + i))
                pe.wait_ge(s_comb, 8 + 2 * i + 2)
                for x in range(2):
                    for kk in range(2):
                        ins = M.transpose(b[:, P * (2 * x + kk):P * (2 * x + kk) + P],
                                          p1[:, 2 * (2 * i + x), P * kk:P * kk + P], ident[:, :])
                filled(ins, ("aT", 2 + i))
            for i in range(4):
                t, hf = i // 2, i % 2
                b = bank(("av", i))
                if t == 0:
                    stored(pe, ("aT", hf))
                else:
                    stored(pe, ("aT", 2 + 2 * hf))
                    stored(pe, ("aT", 3 + 2 * hf))
                for x in range(4):
                    h = 4 * hf + x
                    out = b[:, P * x:P * x + P]
                    if t == 0:
                        ins = M.matmul(out, aT0[:, h], vnat[:, 0, P * h:P * h + P], start=True, stop=True,
                                       skip_group_check=True)
                    else:
                        for kk in range(2):
                            ins = M.matmul(out, aT1[:, h, kk], vnat[:, kk, P * h:P * h + P],
                                           start=kk == 0, stop=kk == 1, skip_group_check=True)
                filled(ins, ("av", i))
            slot(29)
            slot(30)
            slot(31)
            y(31)
            for i in range(4):
                b = bank(("oT", i))
                for t in range(NT):
                    stored(pe, ("av", 2 * t + i // 2))
                    for x in range(2):
                        h = 2 * i + x
                        ins = M.transpose(b[:, S * x + P * t:S * x + P * t + P], att_n[:, t, P * h:P * h + P], ident[:, :])
                filled(ins, ("oT", i))

            pe.wait_ge(s_bw, 2 + SSM_C)
            for j in range(4):
                unit(GLU0 + j)
                s = (GLU0 + j) % SLOTS
                for c in range(2):
                    b = bank(("glu", 2 * j + c))
                    for kk in range(SSM_C):
                        o = 1024 * c + P * kk
                        ins = three(b[:, 0:256], hi[s][:, o:o + P], lo[s][:, o:o + P], gTh[:, kk], gTl[:, kk],
                                    kk == 0, kk == SSM_C - 1)
                used(ins)
            b = bank(("ssq", 0))
            for j in range(SSM_C):
                pe.wait_ge(s_mixs, j + 1)
                ins = M.matmul(b[:, 0:256], ones[:, :], sqb[:, j], start=j == 0, stop=j == SSM_C - 1)
            filled(ins, ("ssq", 0))
            for i in range(4):
                stored(pe, ("oT", i))
            pe.wait_ge(s_mixs, 2 * SSM_C)
            for cb in range(4):
                rows_block(("wo", cb), WO0 + 4 * cb, 4, mixh, mixl)

            norm(2)
            for cp in range(8):
                stored(pe, ("norm", 2, cp))
            for j in range(4):
                cols_unit(("xq", j), XQ0 + j)
            for i in range(4):
                t, hp = i // 2, i % 2
                b = bank(("xs", i))
                for x in range(2):
                    h = 2 * hp + x
                    stored(pe, ("xq", h))
                    ins = M.matmul(b[:, S * x:S * x + S], qxT[:, h, P * t:P * t + P], kxT[:, h], start=True,
                                   stop=True, skip_group_check=True)
                filled(ins, ("xs", i))
            for h in range(XH):
                b = bank(("xp", h))
                pe.wait_ge(s_xpn, 2 * h + 2)
                for kk in range(2):
                    for t in range(NT):
                        ins = M.transpose(b[:, S * kk + P * t:S * kk + P * t + P], px[:, t, h, P * kk:P * kk + P], ident[:, :])
                filled(ins, ("xp", h))
            for h in range(XH):
                b = bank(("xo", h))
                stored(pe, ("xp", h))
                for kk in range(2):
                    ins = M.matmul(b[:, 0:256], vx[:, kk, P * h:P * h + P], pxT[:, h, kk], start=kk == 0, stop=kk == 1)
                filled(ins, ("xo", h))
            for h in range(XH):
                stored(pe, ("xo", h))
            for cb in range(4):
                rows_block(("xw", cb), XO0 + cb, 1, oxh, oxl)

            norm(3)
            for cp in range(8):
                stored(pe, ("norm", 3, cp))
            for c in range(16):
                cols_unit(("pq", c), PQ0 + c)
            pe.wait_ge(s_keys, 16)
            for i in range(8):
                t = i // 4
                b = bank(("ps", i))
                for x in range(4):
                    c = 4 * (i % 4) + x
                    stored(pe, ("pq", c))
                    ins = M.matmul(b[:, P * x:P * x + P], qP[:, c, P * t:P * t + P], keys[:, c], start=True,
                                   stop=True, skip_group_check=True)
                filled(ins, ("ps", i))
            for i in range(4, 8):
                stored(pe, ("ps", i))
            pe.sem_inc(s_ubank, 4)

            def expert_unit(i, j, gu0, lo_sem, lo0, per):
                pe.wait_ge(lo_sem, i * per + (lo0 + j + 1))
                pe.wait_ge(s_ubank, i * per + (gu0 + j + 1))
                s = j % SLOTS
                for c in range(DC):
                    ins = three(ps[s][:, 0:256], hi[s][:, P * c:P * c + P], lo[s][:, P * c:P * c + P],
                                XTh[:, c], XTl[:, c], c == 0, c == DC - 1)
                used(ins)

            with pe.Fori(0, UA // 4) as i:
                for j in range(4):
                    expert_unit(i, j, 0, s_lo_pool, U0, 4)
            with pe.Fori(0, (KEYS - UA) // 4) as i:
                for j in range(4):
                    expert_unit(i, j, UA, s_lo_vec, 0, 4)
            pe.wait_ge(s_zr, 1)
            pe.wait_ge(s_ubank, KEYS + 4)
            for b in range(8):
                M.matmul(ps[b][:, :], zr[:, 0:P], zr[:, :], start=True, stop=False, skip_group_check=True)
            with pe.Fori(0, KEYS // 8) as i:
                for g in range(2):
                    pe.wait_ge(s_w, i * 4 + (2 * g + 2))
                    for j in range(4):
                        pe.wait_ge(s_lo_vec, i * 8 + (KEYS - UA + 4 * g + j + 1))
                        for t in range(NT):
                            wh, wl = Wh[:, g, j, P * t:P * t + P], Wl[:, g, j, P * t:P * t + P]
                            for x, v in ((wh, hi), (wh, lo), (wl, hi)):
                                for c in range(4):
                                    ins = M.matmul(ps[4 * t + c][:, :], x, v[j][:, 512 * c:512 * c + 512],
                                                   start=False, stop=False, skip_group_check=True)
                        ins.then_inc(s_used, 1)
            for b in range(8):
                ins = M.matmul(ps[b][:, :], zr[:, 0:P], zr[:, :], start=False, stop=True, skip_group_check=True)
            ins.then_inc(s_acc, 1)


def kernel(**inputs):
    import numpy as np
    import concourse.bacc as bacc
    from concourse.bass_utils import run_bass_kernel_spmd

    a = {k: np.asarray(v) for k, v in inputs.items()}

    def cont(x):
        return np.ascontiguousarray(x)

    def cols(v):
        return cont(v.reshape(-1, P).T)

    def by_cols(w):
        kc, n = w.shape[0] // P, w.shape[1] // P
        return cont(w.reshape(kc, P, n, P).transpose(2, 1, 0, 3)).reshape(-1, P, kc * P)

    def by_rows(w):
        q, n = w.shape[0] // (4 * P), w.shape[1] // 512
        return cont(w.reshape(q, 4, P, n, 512).transpose(3, 0, 2, 1, 4)).reshape(-1, P, D)

    w_in, w_kv = a["w_in"][0], a["xattn_wkv"][0]
    glu = by_cols(a["glu_w"][0]).reshape(4, 2, P, SSM_W).transpose(0, 2, 1, 3)
    b_all = np.stack([a["ssm_b_re"][0], a["ssm_b_im"][0]])
    c_all = np.stack([a["ssm_c_re"][0], a["ssm_c_im"][0]])
    keys = np.stack([a["peer_k1"][0], a["peer_k2"][0]], axis=1)
    arrays = {
        "x": a["x"][0], "mem": a["mem"][0],
        "w_mk": by_cols(w_kv[:, :XW]), "w_mv": by_rows(w_kv[:, XW:]),
        "w_u": by_cols(w_in[:, 3 * ATT:]), "w_qkv": by_rows(w_in[:, :3 * ATT]),
        "w_glu": cont(glu).reshape(4, P, D), "w_wo": by_rows(a["w_out"][0]),
        "w_xq": by_cols(a["xattn_wq"][0]), "w_xo": by_rows(a["xattn_wo"][0]),
        "w_pq": by_cols(a["peer_wq"][0]),
        "u": cont(a["peer_u"][0].reshape(KEYS, KEYS, DC, P).transpose(1, 3, 2, 0)).reshape(KEYS, P, D),
        "v": cont(a["peer_v"][0].reshape(KEYS, KEYS, D).transpose(1, 0, 2)),
        "gains": cont(np.stack([cols(a[n][0]) for n in ("mem_norm_g", "mix_norm_g", "xattn_norm_g", "ffn_norm_g")], 1)),
        "g_att": cols(a["attn_head_g"][0]), "g_ssm": cols(a["ssm_out_g"][0]), "glu_b": cols(a["glu_b"][0]),
        "d_skip": cols(a["ssm_d"][0].reshape(-1)),
        "lam": np.concatenate([a["lam_q1"], a["lam_k1"], a["lam_q2"], a["lam_k2"]]),
        "pos": cols(a["positions"][0]), "a_re": cols(a["ssm_a_re"][0].reshape(-1)),
        "a_im": cols(a["ssm_a_im"][0].reshape(-1)), "log_dt": cont(a["ssm_log_dt"].reshape(NBLK, 2).T),
        "bT": cont(b_all.reshape(2, SSM_C, 8, QK, 16).transpose(2, 4, 0, 1, 3)).reshape(P, 2, SSM_C, QK),
        "cT": cont(c_all.reshape(2, NBLK, 2, 16, QK).transpose(2, 4, 0, 1, 3)).reshape(P, 2, NBLK, 16),
        "keys": cont(keys.reshape(2 * PH, KEYS, P).transpose(2, 0, 1)),
        "g_fin": a["final_norm_g"].reshape(1, D),
    }
    arrays = {f"in_{n}": cont(v) for n, v in arrays.items()}
    nc = bacc.Bacc("TRN2", target_bir_lowering=False, num_devices=1)
    T = {n[3:]: nc.dram_tensor(n, v.shape, mybir.dt.from_np(v.dtype), kind="ExternalInput").ap()
         for n, v in arrays.items()}
    for n in ("x", "mem"):
        T[n] = T[n].rearrange("(t p) d -> p t d", p=P)
    T["out"] = nc.dram_tensor("out", (S, D), F32, kind="ExternalOutput").ap()
    hymba_peer(nc, T)
    r = run_bass_kernel_spmd(nc, [arrays], core_ids=[0])
    return r.results[0]["out"].reshape(1, S, D)
```

```python
import math
from contextlib import ExitStack

import concourse.bass as bass
from concourse import mybir

F32 = mybir.dt.float32
F32R = mybir.dt.float32r
I32 = mybir.dt.int32
U32 = mybir.dt.uint32
BF16 = mybir.dt.bfloat16
ALU = mybir.AluOpType
ACT = mybir.ActivationFunctionType
AX = mybir.AxisListType

P = 128
D = 2048
S = 256
NT = S // P
DC = D // P
HEADS = 8
ATT = 1024
QK = 64
SSM_W = 1024
SSM_C = SSM_W // P
NBLK = 32
XH = 4
XW = 512
PH = 8
KEYS = 128
TOPK = 16
EPS = 1e-6
LAM_INIT = 0.8 - 0.6 * math.exp(-0.3 * 0)
TWO_PI = 2 * math.pi
PI_IN = 3.1415925
C1 = 6.28125
C2 = float(int((TWO_PI - C1) * 2 ** 20)) / 2 ** 20
C3 = TWO_PI - C1 - C2
ROUND = 1.5 * 2 ** 23
ROUND15 = 1.5 * 2 ** 8
NEG = -1e30
ROPE = [500000.0 ** (-j / 16.0) for j in range(0, 16, 2)]

UW0 = 8
QKV0 = 16
GLU0 = 40
WO0 = 44
XQ0 = 60
XO0 = 64
PQ0 = 68
U0 = 84
V0 = U0 + KEYS
END = V0 + KEYS
UA = 32
POOL_UNITS = U0 + UA
PICKS_AT = [13, 26]
SLOTS = 4
CST = 18
QKV_ORDER = [0, 2, 1, 3, 4, 5]
STEPS = 4 * 24
ZERO_AT = 46
TABLES_AT = 10
BLOCK_EVERY = 3
BLOCKS_BEFORE = [-(-4 * n // BLOCK_EVERY) for n in range(25)]
HALF_AT = [STEPS // 3, 2 * STEPS // 3]
ROPE_AT, QKT_AT, S0_AT, S1_AT, MAX_AT, EXP_AT, COMB_AT, AT_AT = 1, 4, 9, 11, 16, 17, 20, 23
WO_ORDER = [0, 1, 4, 5, 2, 3, 6, 7] + list(range(8, 16))
assert BLOCKS_BEFORE[24] == NBLK
GELU_AT = [min(n for n in range(25) if BLOCKS_BEFORE[n] >= 4 * j + 4) + 2 for j in range(6)] + [23]
NAT_AT = {6: range(4), 9: range(4, 8)}
GLU_HI_AT = [80, 81, 82, 85, 86, 87, 95]
GLU_LO_AT = [83, 84, 85, 89, 90, 91]
GROUPS = NBLK // 4


VEC_AT = {"gains": (0, 4 * DC), "g_att": (64, 1), "g_ssm": (72, SSM_C), "glu_b": (80, SSM_C), "d_skip": (88, SSM_C),
          "lam": (96, 4 * QK)}
VECS = 96 + 4 * QK


class Banks:

    def __init__(self):
        self.uses = [0] * 8
        self.at = {}
        self.unit = {}

    def add(self, name, bank, unit=None):
        self.at[name] = (bank, self.uses[bank])
        self.uses[bank] += 1
        if unit is not None:
            self.unit[name] = unit


def plan_banks():
    b = Banks()

    def norm(k, bank0=0):
        for cp in range(8):
            b.add(("norm", k, cp), bank0 + cp % 4)

    norm(0)
    for j in range(4):
        b.add(("mk", j), j, j)
        if j == 1:
            b.add(("rb", 0), 4)
            norm(1, 4)
    b.add(("rb", 1), 4)
    for t in range(2):
        b.add(("mv", t), t, 7)
    for j in range(8):
        b.add(("uw", j), (j + 2) % 4, UW0 + j)
    for s in range(NBLK):
        b.add(("bu", s), 4 + s % 2)
    jobs = [(QKT_AT + i, ("qkT", i)) for i in range(4)] + [(S0_AT + i, ("s0", i)) for i in range(2)] + \
        [(S1_AT + i, ("s1", i)) for i in range(4)] + [(AT_AT + i, ("aT", i)) for i in range(3)]
    for cb in range(6):
        for t in range(2):
            b.add(("qkv", cb, t), 2 * (cb % 2) + t, QKV0 + 4 * cb + 3)
        for x, at in enumerate(HALF_AT):
            for step, (name, i) in jobs:
                if (at + step) // 16 == cb:
                    b.add((name, x, i), 2 * (1 - cb % 2) + i % 2)
    for i in range(4):
        b.add(("av", i), 4 + i)
    for ct in range(8):
        b.add(("glu", ct), ct % 4, GLU0 + ct // 2)
    for i in range(4):
        b.add(("oT", i), 4 + i)
    b.add(("ssq", 0), 4)
    for cb in range(4):
        for t in range(2):
            b.add(("wo", cb, t), 2 * (cb % 2) + t, WO0 + (5 if cb == 0 else 4 * cb + 3))
    norm(2, 4)
    for j in range(4):
        b.add(("xq", j), j, XQ0 + j)
        if j == 1:
            b.add(("rb", 2), 4)
    for name, bank0 in (("xs", 4), ("xp", 0), ("xo", 4)):
        for h in range(4):
            b.add((name, h), bank0 + h)
    for cb in range(4):
        for t in range(2):
            b.add(("xw", cb, t), 2 * (cb % 2) + t, XO0 + cb)
    norm(3, 4)
    b.add(("rb", 3), 4)
    norm(4, 4)
    for c in range(16):
        b.add(("pq", c), c % 4, PQ0 + c)
    for i in range(8):
        b.add(("ps", i), i % 4)
    count, b.fills = [0] * 8, {}
    for name, (bank, _) in b.at.items():
        if name not in b.unit:
            count[bank] += 1
            b.fills[name] = count[bank]
    return b


class Chain:

    def __init__(self, eng, sem):
        self.eng, self.sem, self.n = eng, sem, 0

    def __call__(self, ins):
        ins.then_inc(self.sem, 1)
        self.n += 1
        return self.n

    def settle(self):
        self.eng.wait_ge(self.sem, self.n)


def hymba_peer(nc, T):
    ctx = ExitStack()
    with ctx:
        base = 16512

        def at(name, kb, shape, dt=F32):
            return nc.alloc_sbuf_tensor_at(name, shape, dt, offset=base + int(kb * 1024))

        def sem(name):
            return ctx.enter_context(nc.semaphore(name))

        def sems(name, n):
            return [sem(f"{name}{i}") for i in range(n)]

        raw = [at(f"raw{i}", 8 * i, [P, 2048]) for i in range(SLOTS)]
        lo = [at(f"lo{i}", 8 * i, [P, 2048], F32R) for i in range(SLOTS)]
        hi = [at(f"hi{i}", 32 + 8 * i, [P, 2048], F32R) for i in range(SLOTS)]
        H = at("H", 64, [P, NT, D])
        k = 80.0
        small = {}

        def sm(name, shape, dt=F32):
            nonlocal k
            n = 4
            for x in shape[1:]:
                n *= x
            small[name] = at(name, k, shape, dt)
            k += max(n, 32) / 1024
            k = math.ceil(k * 32) / 32
            return small[name]

        ident = sm("ident", [P, P])
        maskd = sm("maskd", [P, 2, P])
        vecs = sm("vecs", [P, VECS])
        vec = {n: vecs[:, o:o + c] for n, (o, c) in VEC_AT.items()}
        gains = vec["gains"].rearrange("p (n c) -> p n c", n=4)
        g_att, g_ssm, glu_b, d_skip = (vec[n] for n in ("g_att", "g_ssm", "glu_b", "d_skip"))
        lamv = vec["lam"].rearrange("p (n d) -> p n d", n=4)
        g_att8 = sm("g_att8", [P, 1])
        lams = sm("lams", [P, 8])
        posi = sm("posi", [P, NT], I32)
        posf = sm("posf", [P, NT])
        freq = sm("freq", [P, 8])
        rcos = sm("rcos", [P, NT, 8])
        rsin = sm("rsin", [P, NT, 8])
        stat = sm("stat", [P, 16])
        rstd = sm("rstd", [P, 8])
        assert k <= 84.1, k
        k = 84.25
        prm = at("prm", k, [P, 20, NBLK])
        k += 2.5
        st_max = at("st_max", k, [P, 32])
        st_sum = at("st_sum", k + 0.125, [P, 32])
        st_rec = at("st_rec", k + 0.25, [P, 32])
        head_ms = at("head_ms", k + 0.375, [P, 16])
        ones = at("ones", 207, [P, P])
        eps = at("eps", k + 0.5, [P, 1])
        magic = at("magic", k + 0.53125, [P, 1])
        one = at("one", k + 0.5625, [P, 1])
        half_mask = at("half_mask", k + 0.59375, [P, 2])
        quarter = at("quarter", k + 0.625, [P, 1])

        XTh = at("XTh", 88, [P, DC, S], F32R)
        XTl = at("XTl", 104, [P, DC, S], F32R)
        p0 = at("p0", 64, [P, HEADS, P])
        p1 = at("p1", 68, [P, HEADS, S])
        aT0 = at("aT0", 76, [P, HEADS, P])
        aT1 = at("aT1", 168, [P, HEADS, 2, P])
        zqk = at("zqk", 128, [P, NT, ATT])
        qkT = at("qkT", 136, [P, 2, HEADS // 2, S])
        mixh = at("mixh", 88, [P, DC, S], F32R)
        mixl = at("mixl", 104, [P, DC, S], F32R)
        uT = at("uT", 120, [P, SSM_C, S])
        sig = at("sig", 160, [P, SSM_C, S])
        nat = at("nat", 176, [P, NT, D])
        mem = at("mem", 152, [P, NT, D])
        memh = at("memh", 120, [P, DC, S], F32R)
        meml = at("meml", 136, [P, DC, S], F32R)
        XT2h = at("XT2h", 128, [P, DC, S], F32R)
        XT2l = at("XT2l", 144, [P, DC, S], F32R)
        att_n = at("att_n", 152, [P, NT, ATT])
        vnat = at("vnat", 144, [P, NT, ATT])
        junk = at("junk", 176, [P, D], BF16)
        hjunk = at("hjunk", 87.5, [P, P], BF16)
        BW = at("BW", 152, [P, 2, SSM_C, P])
        CW = at("CW", 160, [P, NBLK, 2, 32])
        yT = uT
        tab = [at(f"tab{i}", o, [P, 2, S]) for i, o in enumerate((176, 178, 190, 192))]
        tgrp = at("tgrp", 128, [P, 2, 2, 4, S])
        phF = at("phF", 168, [P, 2, 4, S])
        m1 = at("m1", 180, [P, 2, S])
        m2 = at("m2", 182, [P, 2, S])
        dem = at("dem", 184, [P, 2, S])
        xst = at("xst", 186, [P, 2, 2, S])
        phA = at("phA", 180, [P, 4, S])
        phR = at("phR", 184, [P, 4, S])
        kxT = at("kxT", 194, [P, XH, S])
        vx = at("vx", 198, [P, NT, XW])
        iota_t = at("iota_t", 202, [P, S])
        zero = at("zero", 203, [P, 512])
        diag = at("diag", 205, [P, NT, P])
        Rb = at("Rb", 206, [P, S])
        braw = at("braw", 180, [P, 2, SSM_C, 64])
        craw = at("craw", 184, [P, 2, NBLK, 16])
        ctmp = at("ctmp", 188, [P, 2, NBLK, 16])
        gTh = at("gTh", 128, [P, SSM_C, S], F32R)
        gTl = at("gTl", 136, [P, SSM_C, S], F32R)
        sqb = at("sqb", 176, [P, SSM_C, S])
        qxT = at("qxT", 88, [P, XH, S])
        px = at("px", 92, [P, NT, XH, S])
        pxT = at("pxT", 100, [P, XH, 2, S])
        oxh = at("oxh", 108, [P, XH, S], F32R)
        oxl = at("oxl", 112, [P, XH, S], F32R)
        keys = at("keys", 120, [P, 2 * PH, KEYS])
        qP = at("qP", 160, [P, 2 * PH, S])
        sc = at("sc", 144, [P, NT, 2 * PH, KEYS])
        cand = at("cand", 176, [P, PH, TOPK, TOPK])
        repl = at("repl", 184, [P, 256])
        k = 185.0
        tv = at("tv", k, [P, 2 * PH, TOPK])
        ti = at("ti", k + 1, [P, 2 * PH, TOPK], U32)
        tif = at("tif", k + 2, [P, 2 * PH, TOPK])
        ts = at("ts", k + 3, [P, PH, TOPK])
        ic = at("ic", k + 3.5, [P, PH, TOPK], U32)
        icx = at("icx", k + 4, [P, 2, PH, TOPK], U32)
        icf = at("icf", k + 5, [P, 2, PH, TOPK])
        ef = at("ef", k + 6, [P, 2, PH, TOPK])
        ei = at("ei", k + 7, [P, PH, TOPK])
        gate = at("gate", k + 7.5, [P, NT, PH, TOPK])
        eidx = at("eidx", k + 8.5, [P, NT, PH, TOPK], I32)
        io16 = at("io16", k + 9.5, [P, TOPK])
        tokf = at("tokf", k + 9.5625, [P, NT])
        g1 = at("g1", k + 9.625, [P, PH])
        g2 = at("g2", k + 9.6875, [P, PH])
        eq = at("eq", 160, [P, PH, TOPK, TOPK])
        eqv = at("eqv", 168, [P, PH, TOPK, TOPK])
        gbuf = at("gbuf", 128, [P, 2, 4, S])
        As = at("As", 144, [P, 2, 4, S])
        Gs = at("Gs", 152, [P, 2, 4, S])
        Wf = at("Wf", 160, [P, 4, S])
        Wh = at("Wh", 164, [P, 2, 4, S], F32R)
        Wl = at("Wl", 172, [P, 2, 4, S], F32R)
        zr = at("zr", 195, [P, 512], F32R)
        sqs = at("sqs", 160, [P, NT, D], BF16)
        sums = at("sums", 180, [P, NT, 4])
        g_fin = at("g_fin", 197, [P, D])

        ps = [ctx.enter_context(nc.psum_tensor(f"ps{i}", [P, 512], F32)) for i in range(8)]
        ACTS = nc.dram_tensor("acts_dram", (KEYS, P, S), F32, kind="Internal").ap()
        TABD = nc.dram_tensor("tables_dram", (GROUPS, P, 2, 4, S), F32, kind="Internal").ap()
        GD = nc.dram_tensor("gates_dram", (KEYS * P * S, 1), F32, kind="Internal").ap()
        gd_zero = GD.rearrange("(z p n) o -> z p (n o)", p=P, n=512)
        gd_slab = GD.rearrange("(n p t) o -> n p (t o)", p=P, t=S)

        plan = plan_banks()
        full = sems("full", 8)
        taken = sems("taken", 8)

        s_small = sem("s_small")
        s_gain = sem("s_gain")
        s_bc = sem("s_bc")
        s_mem = sems("s_mem", 4)
        s_x = sem("s_x")
        s_keys = sem("s_keys")
        s_gf = sem("s_gf")
        s_raw = sems("s_raw", SLOTS)
        s_hi = sem("s_hi")
        s_lo_pool = sem("s_lo_pool")
        s_lo_vec = sem("s_lo_vec")
        s_lo_first = sem("s_lo_first")
        s_used = sem("s_used")
        s_cst = sem("s_cst")
        s_zero = sem("s_zero")
        s_gz = sem("s_gz")
        s_sq = sem("s_sq")
        s_ms = sem("s_ms")
        s_rt = sem("s_rt")
        s_xn = sem("s_xn")
        s_hc = sem("s_hc")
        s_dve = sem("s_dve")
        s_act = sem("s_act")
        s_par = sem("s_par")
        s_parv = sem("s_parv")
        s_bw = sem("s_bw")
        s_hc0 = sem("s_hc0")
        s_phase = sem("s_phase")
        s_sin = sem("s_sin")
        s_tst = sems("s_tst", 2)
        s_tab = sems("s_tab", 4)
        s_dg = sem("s_dg")
        s_dem = sem("s_dem")
        s_xs = sem("s_xs")
        s_ymm = sem("s_ymm")
        s_yv = sem("s_yv")
        s_ge = sem("s_ge")
        s_gl = sem("s_gl")
        s_g2 = sem("s_g2")
        s_mixs = sem("s_mixs")
        s_rope = sem("s_rope")
        s_smax = sem("s_smax")
        s_exp = sem("s_exp")
        s_comb = sem("s_comb")
        s_rec = sem("s_rec")
        s_second = sem("s_second")
        s_attn = sem("s_attn")
        s_hms = sem("s_hms")
        s_hsq = sem("s_hsq")
        s_hrt = sem("s_hrt")
        s_xmax = sem("s_xmax")
        s_xexp = sem("s_xexp")
        s_xpn = sem("s_xpn")
        s_oxl = sem("s_oxl")
        s_pick = sem("s_pick")
        s_pexp = sem("s_pexp")
        s_idx = sem("s_idx")
        s_scat = sem("s_scat")
        s_ugelu = sem("s_ugelu")
        s_store = sems("s_store", 2)
        s_slab = sems("s_slab", 2)
        s_wmul = sem("s_wmul")
        s_w = sem("s_w")
        s_fin = sem("s_fin")
        s_fo = sem("s_fo")
        s_out = sem("s_out")
        s_zr = sem("s_zr")
        s_ubank = sem("s_ubank")

        def fill_done(eng, name):
            b, _ = plan.at[name]
            if name in plan.unit:
                eng.wait_ge(s_used, plan.unit[name] + 1)
            else:
                eng.wait_ge(full[b], plan.fills[name])
            return ps[b]

        def stored(eng, name):
            b, n = plan.at[name]
            eng.wait_ge(taken[b], n + 1)

        def took(ins, name):
            return ins.then_inc(taken[plan.at[name][0]], 1)

        block = ctx.enter_context(nc.Block())

        @block.sync
        def _(sp):
            sp.dma_start(vecs[:, :], T["vecs"]).then_inc(s_gain, 16)
            for x in range(4):
                part = slice(512 * x, 512 * x + 512)
                sp.dma_start(mem[:, :, part], T["mem"][:, :, part]).then_inc(s_mem[x], 16)

            def load(src, k):
                sp.dma_start(raw[k][:, :], src).then_inc(s_raw[k], 16)

            def tables(j):
                return 0 if j < 0 else NBLK if j == 23 else min(NBLK, BLOCKS_BEFORE[max(0, j - 3)] + 2)

            def segment(name, first, n):
                for j in range(n):
                    u = first + j
                    if u >= SLOTS:
                        sp.wait_ge(s_used, u - SLOTS + 1)
                    load(T[name][j], u % SLOTS)
                    if u == WO0 + 1:
                        for x in range(2):
                            for i in range(3):
                                stored(sp, ("aT", x, i))
                        for i in range(4):
                            fill_done(sp, ("av", i))
                        sp.dma_start(H[:, :, :], T["x"]).then_inc(s_x, 16)
                    if u == 1:
                        sp.dma_start(H[:, :, :], T["x"]).then_inc(s_x, 16)
                    if ZERO_AT <= u < ZERO_AT + 32:
                        if u == ZERO_AT:
                            sp.wait_ge(s_zero, 1)
                        for z in range(2):
                            sp.dma_start(gd_zero[2 * (u - ZERO_AT) + z], zero[:, :]).then_inc(s_gz, 16)
                    if name == "w_qkv":
                        for b in range(tables(j - 1), tables(j)):
                            sp.wait_ge(s_tst[b // 4 % 2], 16 * (b // 8 + 1))
                            if b >= 4:
                                sp.wait_ge(s_dem, b - 3)
                            sp.dma_start(tab[b % 4][:, :, :], TABD[b // 4, :, :, b % 4]).then_inc(s_tab[b % 4], 16)

            segment("w_mk", 0, 4)
            segment("w_mv", 4, 4)
            segment("w_u", UW0, 8)
            segment("w_qkv", QKV0, 24)
            segment("w_glu", GLU0, 4)
            segment("w_wo", WO0, 16)
            segment("w_xq", XQ0, 4)
            segment("w_xo", XO0, 4)
            sp.dma_start(keys[:, :, :], T["keys"]).then_inc(s_keys, 16)
            segment("w_pq", PQ0, 16)
            with sp.Fori(0, KEYS // 4) as i:
                for j in range(4):
                    sp.wait_ge(s_used, i * 4 + (U0 + j - SLOTS + 1))
                    load(T["u"][bass.ds(i * 4 + j, 1)].rearrange("a p n -> p (a n)"), j)
            sp.wait_ge(s_scat, 16 * NT * PH * TOPK)
            for g in range(2):
                sp.wait_ge(s_store[g], 16)
                sp.dma_start(As[:, g], ACTS[4 * g:4 * g + 4].rearrange("n p t -> p n t")).then_inc(s_slab[g], 16)
                sp.dma_start(Gs[:, g], gd_slab[4 * g:4 * g + 4].rearrange("n p t -> p n t")).then_inc(s_slab[g], 16)
            for j in range(8):
                sp.wait_ge(s_used, V0 + j - SLOTS + 1)
                load(T["v"][j], j % 4)
            for g in range(2):
                sp.wait_ge(s_store[g], 16 * (KEYS // 8))
            sp.dma_start(g_fin[:, :], T["g_fin"].to_broadcast([P, D])).then_inc(s_gf, 16)
            with sp.Fori(0, KEYS // 8 - 1) as i:
                for g in range(2):
                    sp.wait_ge(s_wmul, i * 2 + (g + 1))
                    n0 = i * 8 + (8 + 4 * g)
                    sp.dma_start(As[:, g], ACTS[bass.ds(n0, 4)].rearrange("n p t -> p n t")).then_inc(s_slab[g], 16)
                    sp.dma_start(Gs[:, g], gd_slab[bass.ds(n0, 4)].rearrange("n p t -> p n t")).then_inc(s_slab[g], 16)
                    for j in range(4):
                        sp.wait_ge(s_used, i * 8 + (V0 + 8 + 4 * g + j - SLOTS + 1))
                        load(T["v"][bass.ds(n0 + j, 1)].rearrange("a p n -> p (a n)"), j)
            for t in range(NT):
                for x in range(2):
                    sp.wait_ge(s_fo, 2 * t + x + 1)
                    half = slice(D // 2 * x, D // 2 * x + D // 2)
                    sp.dma_start(T["out"][t * P:(t + 1) * P, half], H[:, t, half]).then_inc(s_out, 16)
            sp.wait_ge(s_out, 16 * 2 * NT)

        @block.gpsimd
        def _(pool):
            G = nc.gpsimd
            G.memset(ident[:, :], 0.0).then_inc(s_cst, 1)
            G.memset(maskd[:, :, :], 0.0).then_inc(s_cst, 1)
            G.memset(zero[:, :], 0.0).then_inc(s_zero, 1)
            pool.wait_ge(s_cst, 2)
            G.affine_select(out=ident[:, :], in_=ident[:, :], compare_op=ALU.not_equal, fill=1.0,
                            base=0, pattern=[[-1, P]], channel_multiplier=1).then_inc(s_cst, 1)
            G.affine_select(out=maskd[:, 1, :], in_=maskd[:, 1, :], compare_op=ALU.is_ge, fill=NEG,
                            base=0, pattern=[[-1, P]], channel_multiplier=1).then_inc(s_cst, 1)
            G.iota(iota_t[:, :], [[1, S]], base=0, channel_multiplier=0,
                   allow_small_or_imprecise_dtypes=True).then_inc(s_cst, 1)
            for j in range(8):
                G.memset(freq[:, j:j + 1], ROPE[j]).then_inc(s_cst, 1)
            G.memset(eps[:, :], EPS).then_inc(s_cst, 1)
            G.memset(magic[:, :], ROUND).then_inc(s_cst, 1)
            G.memset(ones[:, :], 1.0).then_inc(s_cst, 1)
            G.memset(one[:, :], 1.0).then_inc(s_cst, 1)
            G.memset(quarter[:, :], PI_IN / 2).then_inc(s_cst, 1)

            def rest(j, hi_count):
                pool.wait_ge(s_hi, hi_count)
                G.tensor_tensor(lo[j][:, :], raw[j][:, :], hi[j][:, :].bitcast(F32), ALU.subtract).then_inc(s_lo_pool, 1)

            for j in range(1, SLOTS):
                rest(j, j + 1)
            with pool.Fori(1, POOL_UNITS // SLOTS) as i:
                for j in range(SLOTS):
                    rest(j, i * SLOTS + (j + 1))
            pool.wait_ge(s_idx, NT)
            pool.wait_ge(s_gz, 16 * 64)
            for h in range(PH):
                if h:
                    pool.wait_ge(s_scat, 16 * NT * TOPK * h)
                for t in range(NT):
                    for r in range(TOPK):
                        G.indirect_dma_start(GD, bass.IndirectOffsetOnAxis(ap=eidx[:, t, h, r:r + 1], axis=0),
                                             gate[:, t, h, r:r + 1], None,
                                             compute_op=ALU.add).then_inc(s_scat, 16)

        @block.scalar
        def _(act):
            A = nc.scalar
            own = Chain(act, s_act)
            act.dma_start(prm[:, 0:3, :], T["ssm"]).then_inc(s_small, 16)
            act.dma_start(posi[:, :], T["pos"]).then_inc(s_small, 16)

            def gelu(j):
                act.wait_ge(s_yv, j + 1)
                A.activation(yT[:, j], yT[:, j], ACT.Gelu).then_inc(s_ge, 1)

            def glu_hi(j):
                act.wait_ge(s_ge, j + 1)
                A.activation(gTh[:, j], yT[:, j], ACT.Copy).then_inc(s_gl, 1)

            def split(u):
                act.wait_ge(s_raw[u % SLOTS], 16 * (u // SLOTS + 1))
                A.activation(hi[u % SLOTS][:, :], raw[u % SLOTS][:, :], ACT.Copy).then_inc(s_hi, 1)

            def norm_stats(kk, X):
                for t in range(NT):
                    if t or kk:
                        act.wait_ge(s_sq, NT * kk + t)
                    A.activation(junk[:, :], X[:, t], ACT.Square,
                                 accum_out=stat[:, 4 * (kk % 2) + t:4 * (kk % 2) + t + 1]).then_inc(s_sq, 1)

            def norm_root(kk):
                act.wait_ge(s_ms, kk + 1)
                A.activation(stat[:, 8:8 + NT], stat[:, 4 * (kk % 2) + 2:4 * (kk % 2) + 4],
                             ACT.Sqrt).then_inc(s_rt, 1)

            def norm_hi(kk, g, cps=range(8)):
                dst = (memh, XTh, XT2h, XT2h, XTh)[kk]
                for cp in cps:
                    b = fill_done(act, ("norm", kk, cp))
                    for c in range(2):
                        A.activation(dst[:, 2 * cp + c], b[:, 256 * c:256 * c + 256], ACT.Copy,
                                     scale=gains[:, g, 2 * cp + c:2 * cp + c + 1]).then_inc(s_hc, 1)

            def evac(name, dst, cols=slice(0, 256), scale=1.0, by=1):
                src = fill_done(act, name)[:, cols]
                if by > 1:
                    src = src.rearrange("p (x t) -> p x t", x=by)
                took(A.activation(dst, src, ACT.Copy, scale=scale), name)

            def table_group(g):
                act.wait_ge(s_phase, g + 1)
                if g == 0:
                    act.wait_ge(s_used, 8)
                if g > 1:
                    act.wait_ge(s_tst[g % 2], 16 * (g // 2))
                cos, sin, ph = tgrp[:, g % 2, 0], tgrp[:, g % 2, 1], phF[:, g % 2]
                A.activation(sin, ph, ACT.Sin, scale=2 * PI_IN).then_inc(s_sin, 1)
                A.activation(cos, ph, ACT.Abs).then_inc(s_sin, 1)
                act.wait_ge(s_sin, 2 * g + 2)
                own(A.activation(cos, cos, ACT.Sin, scale=-2 * PI_IN, bias=quarter[:, 0:1]))
                own.settle()
                act.dma_start(TABD[g], tgrp[:, g % 2]).then_inc(s_tst[g % 2], 16)

            act.wait_ge(s_cst, CST)
            act.wait_ge(s_gain, 16)
            norm_hi(0, 0)
            act.dma_start(braw[:, :, :, :], T["bT"]).then_inc(s_bc, 16)
            act.dma_start(craw[:, :, :, :], T["cT"]).then_inc(s_bc, 16)
            split(0)
            split(1)
            for x in range(4):
                act.wait_ge(s_mem[x], 16)
            norm_stats(0, mem)
            norm_root(0)
            act.wait_ge(s_x, 16)
            split(2)
            split(3)
            split(4)
            norm_hi(1, 1)
            norm_stats(1, H)
            norm_root(1)
            act.wait_ge(s_small, 32)
            own(A.activation(prm[:, 3, :], prm[:, 2, :], ACT.Exp))
            act.wait_ge(s_par, 1)
            own(A.activation(prm[:, 6, :], prm[:, 4, :], ACT.Exp))
            A.activation(lams[:, 2:4], lams[:, 0:2], ACT.Exp).then_inc(s_parv, 1)
            split(5)
            act.wait_ge(s_par, 2)
            own(A.activation(prm[:, 8, :], prm[:, 7, :], ACT.Sin))
            own(A.activation(prm[:, 9, :], prm[:, 7, :], ACT.Sin, scale=0.5))
            own(A.activation(rsin[:, :, :], rcos[:, :, :], ACT.Sin))
            own(A.activation(rcos[:, :, :], rcos[:, :, :], ACT.Sin, scale=0.5))
            own.settle()
            own(A.activation(prm[:, 9, :], prm[:, 9, :], ACT.Square, scale=math.sqrt(2.0)))
            own(A.activation(rcos[:, :, :], rcos[:, :, :], ACT.Square, scale=math.sqrt(2.0)))
            own.settle()
            A.activation(prm[:, 9, :], prm[:, 9, :], ACT.Identity, scale=-1.0, bias=one[:, 0:1]).then_inc(s_parv, 1)
            A.activation(rcos[:, :, :], rcos[:, :, :], ACT.Identity, scale=-1.0, bias=one[:, 0:1]).then_inc(s_parv, 1)

            def weights(u):
                split(u)
                if TABLES_AT <= u < TABLES_AT + GROUPS:
                    table_group(u - TABLES_AT)

            for u in range(6, 10):
                split(u)
            for t in range(2):
                evac(("mv", t), vx[:, t], slice(0, 512), scale=rstd[:, t:t + 1])
            for u in range(10, 19):
                weights(u)
            def attention_step(g, hf):
                x = g - HALF_AT[hf]
                if 0 <= x - QKT_AT - 1 < 4:
                    i = x - QKT_AT - 1
                    evac(("qkT", hf, i), qkT[:, i // 2, :, P * (i % 2):P * (i % 2) + P], slice(0, 512), by=4)
                if x in (EXP_AT, EXP_AT + 1):
                    k = x - EXP_AT
                    p, o = (p0, p1)[k], 16 * hf + 8 * k
                    act.wait_ge(s_smax, 2 * hf + k + 1)
                    for i in range(HEADS):
                        A.activation(p[:, i], p[:, i], ACT.Exp, bias=st_max[:, o + i:o + i + 1],
                                     accum_out=st_sum[:, o + i:o + i + 1]).then_inc(s_exp, 1)
                if x in (COMB_AT, COMB_AT + 1):
                    k = x - COMB_AT
                    p, o = (p0, p1)[k], 16 * hf + 8 * k
                    act.wait_ge(s_rec, 2 * hf + k + 1)
                    for h in range(4):
                        A.activation(p[:, 2 * h + 1], p[:, 2 * h + 1], ACT.Copy,
                                     scale=st_rec[:, o + 2 * h + 1:o + 2 * h + 2]).then_inc(s_second, 1)
                if 0 <= x - AT_AT - 1 < 3:
                    i = x - AT_AT - 1
                    if i == 0:
                        evac(("aT", hf, i), aT0[:, 4 * hf:4 * hf + 4], slice(0, 512), by=4)
                    else:
                        h = 4 * hf + 2 * (i - 1)
                        evac(("aT", hf, i), aT1[:, h:h + 2].rearrange("p h k t -> p (h k) t"), slice(0, 512), by=4)

            for n in range(24):
                for c in range(4):
                    if c == 2:
                        weights(QKV0 + n + 3)
                    for hf in range(2):
                        attention_step(4 * n + c, hf)
                    if c == 3:
                        for j in range(SSM_C - 1):
                            if n == GELU_AT[j]:
                                gelu(j)
                    if 4 * n + c in GLU_HI_AT:
                        glu_hi(GLU_HI_AT.index(4 * n + c))
                if n % 4 == 3:
                    cb = n // 4
                    for x in range(2):
                        act.wait_ge(s_tst[x], 16 * GROUPS // 2)
                    for t in range(2):
                        dst = zqk[:, t, 512 * (cb % 2):512 * (cb % 2) + 512] if cb < 4 else \
                            vnat[:, t, 512 * (cb - 4):512 * (cb - 4) + 512]
                        evac(("qkv", cb, t), dst, slice(0, 512), scale=rstd[:, 2 + t:3 + t])

            gelu(SSM_C - 1)
            glu_hi(SSM_C - 1)
            for j in range(4):
                split(GLU0 + j + 3)
                for c in range(2):
                    b = fill_done(act, ("glu", 2 * j + c))
                    took(A.activation(sig[:, 2 * j + c], b[:, 0:256], ACT.Sigmoid,
                                      bias=glu_b[:, 2 * j + c:2 * j + c + 1]), ("glu", 2 * j + c))
                if j == 0:
                    for i in range(4):
                        b = fill_done(act, ("av", i))
                        for x in range(4):
                            if 4 * i + x:
                                act.wait_ge(s_hsq, 4 * i + x)
                            A.activation(hjunk[:, :], b[:, P * x:P * x + P], ACT.Square,
                                         accum_out=head_ms[:, 4 * i + x:4 * i + x + 1]).then_inc(s_hsq, 1)
                    act.wait_ge(s_hms, 1)
                    A.activation(head_ms[:, :], head_ms[:, :], ACT.Sqrt).then_inc(s_hrt, 1)
                if j == 2:
                    for i in range(4):
                        b = fill_done(act, ("oT", i))
                        A.activation(mixh[:, 2 * i:2 * i + 2], b[:, :].rearrange("p (h t) -> p h t", h=2), ACT.Copy,
                                     scale=g_att8[:, 0:1]).then_inc(s_hc, 1)
            for j in range(SSM_C):
                act.wait_ge(s_g2, j + 1)
                A.activation(sqb[:, j], yT[:, j], ACT.Square).then_inc(s_mixs, 1)
            split(WO0 + 3)
            b = fill_done(act, ("ssq", 0))
            took(A.activation(sig[:, 0], b[:, 0:256], ACT.Sqrt, scale=1.0 / SSM_W, bias=eps[:, 0:1]), ("ssq", 0))
            for j in range(SSM_C):
                act.wait_ge(s_g2, SSM_C + 1 + j)
                A.activation(mixh[:, SSM_C + j], yT[:, j], ACT.Copy).then_inc(s_hc, 1)
            for n in range(1, 16):
                split(WO0 + n + 3)
                if n == 10:
                    norm_hi(2, 2, range(4))
                if n == 14:
                    norm_hi(2, 2, (4, 5))

            norm_hi(2, 2, (6, 7))
            for cb in range(4):
                for t in range(NT):
                    stored(act, ("wo", cb, t))
            norm_stats(2, H)
            norm_root(2)
            def exps(h):
                act.wait_ge(s_xmax, h + 1)
                b = fill_done(act, ("xs", h))
                for t in range(NT):
                    i = 2 * h + t
                    ins = A.activation(px[:, t, h], b[:, S * t:S * t + S], ACT.Exp, bias=st_max[:, i:i + 1],
                                       scale=P ** -0.5, accum_out=st_sum[:, i:i + 1])
                    if t == 0:
                        own(ins)
                    else:
                        took(ins, ("xs", h))

            def probs_out(h):
                evac(("xp", h), pxT[:, h].rearrange("p k t -> p (k t)"), slice(0, 512))

            def output_hi(h):
                b = fill_done(act, ("xo", h))
                A.activation(oxh[:, h], b[:, 0:256], ACT.Copy).then_inc(s_hc, 1)

            split(XQ0 + 3)
            split(XO0)
            for heads in ((0, 1), (2, 3)):
                for h in heads:
                    exps(h)
                if heads[0] == 0:
                    split(XO0 + 1)
                    for h in heads:
                        probs_out(h)
            for heads in ((0, 1), (2, 3)):
                for h in heads:
                    output_hi(h)
                if heads[0] == 0:
                    for h in (2, 3):
                        probs_out(h)
            for u in range(XO0 + 2, XO0 + 5):
                split(u)
            norm_hi(3, 3, (0, 1))
            split(XO0 + 5)
            norm_hi(3, 3, (2, 3))
            split(XO0 + 6)
            norm_hi(3, 3, range(4, 8))

            for cb in range(4):
                for t in range(NT):
                    stored(act, ("xw", cb, t))
            norm_stats(3, H)
            norm_root(3)
            for c in range(16):
                split(PQ0 + c + 3)
                if c in NAT_AT:
                    norm_hi(4, 3, NAT_AT[c])
            for i in range(8):
                t, c = i // 4, 4 * (i % 4)
                b = fill_done(act, ("ps", i))
                took(A.activation(sc[:, t, c:c + 4], b[:, :].rearrange("p (c n) -> p c n", c=4), ACT.Copy), ("ps", i))

            def unit_gelu(i, jj, u_base):
                g, j = jj // 4, jj % 4
                act.wait_ge(s_raw[(jj + 3) % SLOTS], i * 32 + 16 * ((u_base + jj + 3) // SLOTS + 1))
                A.activation(hi[(jj + 3) % SLOTS][:, :], raw[(jj + 3) % SLOTS][:, :], ACT.Copy).then_inc(s_hi, 1)
                if j == 0:
                    act.wait_ge(s_store[g], i * 16 + 16 * ((u_base - U0) // 8))
                act.wait_ge(s_used, i * 8 + (u_base + jj + 1))
                A.activation(gbuf[:, g, j], ps[j][:, 0:256], ACT.Gelu).then_inc(s_ubank, 1)
                if j == 3:
                    act.wait_ge(s_ubank, i * 8 + (u_base - U0 + jj + 1 + 4))
                    n0 = i * 8 + (u_base - U0 + 4 * g)
                    act.dma_start(ACTS[bass.ds(n0, 4)].rearrange("n p t -> p n t"), gbuf[:, g]).then_inc(s_store[g], 16)

            for n in range(UA):
                if n in PICKS_AT:
                    t = PICKS_AT.index(n)
                    act.wait_ge(s_pick, t + 1)
                    A.activation(gate[:, t], gate[:, t], ACT.Exp).then_inc(s_pexp, 1)
                unit_gelu(n // 8, n % 8, U0)
            with act.Fori(0, KEYS // 8 - 4) as i:
                for jj in range(8):
                    unit_gelu(i, jj, U0 + 32)
            for u in range(V0 + 3, V0 + 8):
                split(u)
            with act.Fori(0, KEYS // 8 - 1) as i:
                for j in range(8):
                    act.wait_ge(s_raw[j % SLOTS], i * 32 + 16 * ((V0 + 8 + j) // SLOTS + 1))
                    A.activation(hi[j % SLOTS][:, :], raw[j % SLOTS][:, :], ACT.Copy).then_inc(s_hi, 1)
            for t in range(NT):
                for c in range(4):
                    act.wait_ge(s_fin, 4 * t + c + 1)
                    A.activation(sqs[:, t, 512 * c:512 * c + 512], H[:, t, 512 * c:512 * c + 512], ACT.Square,
                                 accum_out=sums[:, t, c:c + 1]).then_inc(s_sq, 1)
                act.wait_ge(s_ms, 5 + t)
                A.activation(stat[:, 8 + t:9 + t], stat[:, 2 + t:3 + t], ACT.Sqrt).then_inc(s_rt, 1)

        @block.vector
        def _(dve):
            V = nc.vector
            own = Chain(dve, s_dve)

            def pr(n):
                return prm[:, n, :]

            def reduce_angle(x, kk, tmp):
                own(V.tensor_scalar(kk, x, 1.0 / TWO_PI, ROUND, ALU.mult, ALU.add))
                own.settle()
                own(V.tensor_scalar(kk, kk, -ROUND, None, ALU.add))
                own.settle()
                for c in (C1, C2, C3):
                    own(V.tensor_scalar(tmp, kk, -c, None, ALU.mult))
                    own.settle()
                    own(V.tensor_tensor(x, x, tmp, ALU.add))
                    own.settle()
                own(V.tensor_scalar(x, x, PI_IN, -PI_IN, ALU.min, ALU.max))
                own.settle()

            def ssm_weights():
                dve.wait_ge(s_bc, 32)
                odd = ident[:, :].rearrange("p (q g h) -> p q g h", q=4, g=2)
                for g in range(2):
                    own(V.tensor_reduce(half_mask[:, g:g + 1], odd[:, :, g, :], AX.XY, ALU.add))
                own.settle()
                for c in range(2):
                    for g in range(2):
                        last = V.tensor_scalar(BW[:, c, :, 64 * g:64 * g + 64], braw[:, c], half_mask[:, g:g + 1],
                                               None, ALU.mult)
                        own(last)
                dve.wait_ge(s_parv, 3)
                own(V.tensor_tensor(pr(13), pr(6), pr(9), ALU.mult))
                own(V.tensor_tensor(pr(14), pr(6), pr(8), ALU.mult))
                own(V.tensor_tensor(pr(15), pr(0), pr(0), ALU.mult))
                own(V.tensor_tensor(pr(16), pr(1), pr(1), ALU.mult))
                own.settle()
                own(V.tensor_tensor(pr(15), pr(15), pr(16), ALU.add))
                own(V.tensor_scalar(pr(13), pr(13), -1.0, None, ALU.add))
                own.settle()
                own(V.reciprocal(pr(15), pr(15)))
                own(V.tensor_tensor(pr(16), pr(13), pr(0), ALU.mult))
                own(V.tensor_tensor(pr(17), pr(14), pr(1), ALU.mult))
                own(V.tensor_tensor(pr(18), pr(14), pr(0), ALU.mult))
                own(V.tensor_tensor(pr(19), pr(13), pr(1), ALU.mult))
                own.settle()
                own(V.tensor_tensor(pr(16), pr(16), pr(17), ALU.add))
                own(V.tensor_tensor(pr(18), pr(18), pr(19), ALU.subtract))
                own.settle()
                own(V.tensor_tensor(pr(16), pr(16), pr(15), ALU.mult))
                own(V.tensor_tensor(pr(18), pr(18), pr(15), ALU.mult))
                own(V.memset(CW[:, :, :, :], 0.0))
                own.settle()
                fre = pr(16).unsqueeze(2).to_broadcast([P, NBLK, 16])
                fim = pr(18).unsqueeze(2).to_broadcast([P, NBLK, 16])
                own(V.tensor_tensor(ctmp[:, 0], craw[:, 0], fre, ALU.mult))
                own(V.tensor_tensor(ctmp[:, 1], craw[:, 1], fim, ALU.mult))
                own.settle()
                for g in range(2):
                    r = slice(64 * g, 64 * g + 64)
                    own(V.tensor_tensor(CW[r, :, 0, 16 * g:16 * g + 16], ctmp[r, 0], ctmp[r, 1], ALU.subtract))
                own.settle()
                own(V.scalar_tensor_tensor(ctmp[:, 0], craw[:, 0], -1.0, fim, ALU.mult, ALU.mult))
                own(V.tensor_tensor(ctmp[:, 1], craw[:, 1], fre, ALU.mult))
                own.settle()
                for g in range(2):
                    r = slice(64 * g, 64 * g + 64)
                    V.tensor_tensor(CW[r, :, 1, 16 * g:16 * g + 16], ctmp[r, 0], ctmp[r, 1],
                                    ALU.subtract).then_inc(s_bw, 1)

            def norm_rstd(kk):
                o = 4 * (kk % 2)
                dve.wait_ge(s_sq, NT * (kk + 1))
                V.tensor_scalar(stat[:, o + 2:o + 4], stat[:, o:o + 2], 1.0 / D, EPS, ALU.mult,
                                ALU.add).then_inc(s_ms, 1)
                dve.wait_ge(s_rt, kk + 1)
                own(V.reciprocal(rstd[:, 2 * kk:2 * kk + 2], stat[:, 8:10]))
                own.settle()

            def norm_diag(kk):
                norm_rstd(kk)
                for t in range(NT):
                    V.tensor_scalar(diag[:, t], ident[:, :], rstd[:, 2 * kk + t:2 * kk + t + 1], None,
                                    ALU.mult).then_inc(s_dg, 1)

            def norm_spread(kk):
                took(V.tensor_copy(Rb[:, :], fill_done(dve, ("rb", kk))[:, 0:256]), ("rb", kk))
                stored(dve, ("rb", kk))

            def evac(name, dst):
                took(V.tensor_tensor(dst, fill_done(dve, name)[:, 0:256], Rb[:, :], ALU.mult), name)

            def norm_lo(kk, g, hc0, cps=range(8)):
                dh, dl = ((memh, meml), (XTh, XTl), (XT2h, XT2l), (XT2h, XT2l), (XTh, XTl))[kk]
                for cp in cps:
                    dve.wait_ge(s_hc, hc0 + 2 * cp + 2)
                    for c in range(2):
                        ins = V.scalar_tensor_tensor(dl[:, 2 * cp + c], fill_done(dve, ("norm", kk, cp))[:, 256 * c:256 * c + 256],
                                                     gains[:, g, 2 * cp + c:2 * cp + c + 1],
                                                     dh[:, 2 * cp + c].bitcast(F32), ALU.mult, ALU.subtract)
                        if c == 0:
                            own(ins)
                        else:
                            took(ins, ("norm", kk, cp))

            def phases(g):
                if g == 0:
                    dve.wait_ge(s_bw, 2)
                if g > 1:
                    dve.wait_ge(s_sin, 2 * g - 2)
                blocks = [(x, 4 * g + x) for x in range(4)]
                for x, b in blocks:
                    own(V.tensor_scalar(phR[:, x], iota_t[:, :], prm[:, 10, b:b + 1], ROUND, ALU.mult, ALU.add))
                for x, b in blocks:
                    own(V.tensor_scalar(phA[:, x], iota_t[:, :], prm[:, 11, b:b + 1], None, ALU.mult))
                own.settle()
                for x, b in blocks:
                    own(V.scalar_tensor_tensor(phR[:, x], phR[:, x], ROUND, phA[:, x], ALU.subtract, ALU.subtract))
                own.settle()
                for x, b in blocks:
                    own(V.scalar_tensor_tensor(phF[:, g % 2, x], iota_t[:, :], prm[:, 12, b:b + 1], phR[:, x],
                                               ALU.mult, ALU.subtract))
                own.settle()
                V.tensor_scalar(phF[:, g % 2], phF[:, g % 2], 0.5, -0.5, ALU.min, ALU.max).then_inc(s_phase, 1)

            norm_lo(0, 0, 0)
            dve.wait_ge(s_hi, 1)
            V.tensor_tensor(lo[0][:, :], raw[0][:, :], hi[0][:, :].bitcast(F32), ALU.subtract).then_inc(s_lo_first, 1)
            norm_diag(0)
            norm_spread(0)
            for j in range(2):
                evac(("mk", j), kxT[:, j])
            norm_lo(1, 1, 16)
            norm_diag(1)
            dve.wait_ge(s_small, 32)
            dve.wait_ge(s_act, 1)
            own(V.tensor_tensor(pr(4), pr(0), pr(3), ALU.mult))
            own(V.tensor_tensor(pr(5), pr(1), pr(3), ALU.mult))
            own(V.tensor_tensor_reduce(lamv[:, 0], lamv[:, 0], lamv[:, 1], 1.0, 0.0, ALU.mult, ALU.add, lams[:, 0:1]))
            own(V.tensor_tensor_reduce(lamv[:, 2], lamv[:, 2], lamv[:, 3], 1.0, 0.0, ALU.mult, ALU.add, lams[:, 1:2]))
            own.settle()
            V.tensor_copy(posf[:, :], posi[:, :]).then_inc(s_par, 1)
            dve.wait_ge(s_par, 1)
            dve.wait_ge(s_cst, CST)

            for j in range(2, 4):
                evac(("mk", j), kxT[:, j])
            own(V.tensor_copy(pr(7), pr(5)))
            for t in range(NT):
                own(V.tensor_scalar(rcos[:, t], freq[:, :], posf[:, t:t + 1], None, ALU.mult))
            own.settle()
            rc = rcos[:, :, :].rearrange("p t j -> p (t j)")
            rs = rsin[:, :, :].rearrange("p t j -> p (t j)")
            reduce_angle(rc, rs, pr(18)[:, 0:16])
            reduce_angle(pr(7), pr(18), pr(19))
            dve.wait_ge(s_parv, 1)
            own(V.tensor_tensor(lams[:, 4:5], lams[:, 3:4], lams[:, 2:3], ALU.subtract))
            V.tensor_scalar(g_att8[:, :], g_att[:, :], 1.0 - LAM_INIT, None, ALU.mult).then_inc(s_par, 1)
            own.settle()
            own(V.tensor_scalar(lams[:, 5:6], lams[:, 4:5], -LAM_INIT, None, ALU.add))
            own(V.tensor_scalar(pr(10), pr(7), 1.0 / TWO_PI, None, ALU.mult))
            own.settle()
            own(V.tensor_scalar(pr(11), pr(10), ROUND15, None, ALU.add))
            own.settle()
            own(V.tensor_scalar(pr(11), pr(11), -ROUND15, None, ALU.add))
            own.settle()
            V.tensor_tensor(pr(12), pr(10), pr(11), ALU.subtract).then_inc(s_par, 1)
            norm_spread(1)
            ssm_weights()
            phases(0)
            for j in range(8):
                if j < 7:
                    phases(1 + j)
                evac(("uw", j), uT[:, j])

            def turn_back(b):
                bank = fill_done(dve, ("bu", b))[:, :].rearrange("p (c t) -> p c t", c=2)
                dve.wait_ge(s_tab[b % 4], 16 * (b // 4 + 1))
                if b:
                    dve.wait_ge(s_dem, b)
                cos = tab[b % 4][:, 0:1].to_broadcast([P, 2, S])
                sin = tab[b % 4][:, 1:2].to_broadcast([P, 2, S])
                own(V.tensor_tensor(m1[:, :, :], bank, cos, ALU.mult))
                took(V.tensor_tensor(m2[:, :, :], bank, sin, ALU.mult), ("bu", b))

            def scan(b):
                own.settle()
                stored(dve, ("bu", b))
                re_in = own(V.tensor_tensor(m1[:, 0], m1[:, 0], m2[:, 1], ALU.add))
                im_in = own(V.tensor_tensor(m1[:, 1], m1[:, 1], m2[:, 0], ALU.subtract))
                r = prm[:, 6, b:b + 1].to_broadcast([P, S])
                for c, n in ((0, re_in), (1, im_in)):
                    dve.wait_ge(s_dve, n)
                    own(V.tensor_tensor_scan(m1[:, c], r, m1[:, c], 0.0, ALU.mult, ALU.add))
                own.settle()
                if b >= 2:
                    dve.wait_ge(s_ymm, b - 1)
                if b:
                    dve.wait_ge(s_xs, 2 * b)
                cos = tab[b % 4][:, 0:1].to_broadcast([P, 2, S])
                sin = tab[b % 4][:, 1:2].to_broadcast([P, 2, S])
                own(V.tensor_tensor(xst[:, b % 2], m1[:, :, :], cos, ALU.mult))
                V.tensor_tensor(dem[:, :, :], m1[:, :, :], sin, ALU.mult).then_inc(s_dem, 1)

            def states(b):
                x = xst[:, b % 2]
                own.settle()
                dve.wait_ge(s_dem, b + 1)
                V.tensor_tensor(x[:, 0], x[:, 0], dem[:, 1], ALU.subtract).then_inc(s_xs, 1)
                V.tensor_tensor(x[:, 1], x[:, 1], dem[:, 0], ALU.add).then_inc(s_xs, 1)

            def y_out(j):
                dve.wait_ge(s_ymm, 4 * j + 4)
                V.scalar_tensor_tensor(yT[:, j], uT[:, j], d_skip[:, j:j + 1], ps[6 + j % 2][:, 0:256],
                                       ALU.mult, ALU.add).then_inc(s_yv, 1)

            def slot(s):
                turn_back(s)
                if s:
                    states(s - 1)
                scan(s)
                if s % 4 == 2 and s >= 6:
                    y_out(s // 4 - 1)

            def rope(hf, t):
                z = zqk[:, t].rearrange("p (h d) -> p h d", d=QK)
                r1, r2 = z[:, :, 0:8], z[:, :, 8:16]
                c = rcos[:, t:t + 1].to_broadcast([P, 16, 8])
                s = rsin[:, t:t + 1].to_broadcast([P, 16, 8])
                a = m1[:, :, :].rearrange("p a (b h d) -> p (a b) h d", b=2, d=8)
                if t or hf:
                    dve.wait_ge(s_rope, 2 * (2 * hf + t))
                own(V.tensor_tensor(a[:, 0], r1, c, ALU.mult))
                own(V.tensor_tensor(a[:, 1], r2, s, ALU.mult))
                own(V.tensor_tensor(a[:, 2], r1, s, ALU.mult))
                own(V.tensor_tensor(a[:, 3], r2, c, ALU.mult))
                own.settle()
                V.tensor_tensor(r1, a[:, 0], a[:, 1], ALU.subtract).then_inc(s_rope, 1)
                V.tensor_tensor(r2, a[:, 2], a[:, 3], ALU.add).then_inc(s_rope, 1)

            def glu_lo(j):
                dve.wait_ge(s_gl, j + 1)
                V.tensor_tensor(gTl[:, j], yT[:, j], gTh[:, j].bitcast(F32), ALU.subtract).then_inc(s_bw, 1)

            def combine(hf, k):
                p, o = (p0, p1)[k], 16 * hf + 8 * k
                dve.wait_ge(s_exp, o + 8)
                own(V.reciprocal(st_rec[:, o:o + 8], st_sum[:, o:o + 8]))
                own.settle()
                V.tensor_scalar(st_rec[:, o + 1:o + 8:2], st_rec[:, o + 1:o + 8:2], lams[:, 5:6], None,
                                ALU.mult).then_inc(s_rec, 1)

            def difference(hf, k):
                p, o = (p0, p1)[k], 16 * hf + 8 * k
                dve.wait_ge(s_second, o // 2 + 4)
                for h in range(4):
                    V.scalar_tensor_tensor(p[:, 2 * h], p[:, 2 * h], st_rec[:, o + 2 * h:o + 2 * h + 1],
                                           p[:, 2 * h + 1], ALU.mult, ALU.add).then_inc(s_comb, 1)

            def attention_step(g, hf):
                x = g - HALF_AT[hf]
                if x == ROPE_AT:
                    dve.wait_ge(s_dem, -(-g // BLOCK_EVERY))
                    for t in range(NT):
                        for kq in range(2):
                            stored(dve, ("qkv", 2 * hf + kq, t))
                        rope(hf, t)
                    dve.wait_ge(s_rope, 4 * hf + 4)
                if 0 <= x - S0_AT - 1 < 2:
                    i = x - S0_AT - 1
                    if hf and i == 0:
                        for j in range(3):
                            fill_done(dve, ("aT", 0, j))
                    b = fill_done(dve, ("s0", hf, i))
                    took(V.scalar_tensor_tensor(p0[:, i:i + 7:2], b[:, :].rearrange("p (c n) -> p c n", c=4), QK ** -0.5,
                                                maskd[:, 1:2].to_broadcast([P, 4, P]), ALU.mult, ALU.add), ("s0", hf, i))
                if 0 <= x - S1_AT - 1 < 4:
                    i = x - S1_AT - 1
                    b = fill_done(dve, ("s1", hf, i))
                    o = 4 * (i // 2) + i % 2
                    took(V.scalar_tensor_tensor(p1[:, o:o + 3:2], b[:, :].rearrange("p (c n) -> p c n", c=2), QK ** -0.5,
                                                maskd[:, :, :].rearrange("p a n -> p (a n)").unsqueeze(1).to_broadcast([P, 2, S]),
                                                ALU.mult, ALU.add), ("s1", hf, i))
                if x == MAX_AT:
                    for i in range(2, 4):
                        stored(dve, ("s1", hf, i))
                    o = 16 * hf
                    own(V.tensor_reduce(st_max[:, o:o + 8], p0[:, :, :], AX.X, ALU.max))
                    own(V.tensor_reduce(st_max[:, o + 8:o + 16], p1[:, :, :], AX.X, ALU.max))
                    own.settle()
                    for k in range(2):
                        V.tensor_scalar(st_max[:, o + 8 * k:o + 8 * k + 8], st_max[:, o + 8 * k:o + 8 * k + 8], -1.0,
                                        None, ALU.mult).then_inc(s_smax, 1)
                if x in (COMB_AT, COMB_AT + 1):
                    combine(hf, x - COMB_AT)
                if x in (COMB_AT + 1, COMB_AT + 2):
                    difference(hf, x - COMB_AT - 1)

            for g in range(STEPS):
                for hf in range(2):
                    attention_step(g, hf)
                if g % BLOCK_EVERY == 0:
                    slot(g // BLOCK_EVERY)
                if g in GLU_LO_AT:
                    glu_lo(GLU_LO_AT.index(g))
            states(NBLK - 1)
            y_out(7)

            for j in range(len(GLU_LO_AT), SSM_C):
                glu_lo(j)
            dve.wait_ge(s_hsq, 16)
            V.tensor_scalar(head_ms[:, :], head_ms[:, :], 1.0 / P, EPS, ALU.mult, ALU.add).then_inc(s_hms, 1)
            dve.wait_ge(s_hrt, 1)
            own(V.reciprocal(head_ms[:, :], head_ms[:, :]))
            own.settle()
            for i in range(4):
                t, hf = i // 2, i % 2
                b = fill_done(dve, ("av", i))
                took(V.tensor_tensor(att_n[:, t, 512 * hf:512 * hf + 512].rearrange("p (h e) -> p h e", h=4),
                                     b[:, :].rearrange("p (h e) -> p h e", h=4),
                                     head_ms[:, 4 * i:4 * i + 4].unsqueeze(2).to_broadcast([P, 4, P]), ALU.mult), ("av", i))

            def gated(j):
                stored(dve, ("glu", j))
                V.tensor_tensor(yT[:, j], yT[:, j], sig[:, j], ALU.mult).then_inc(s_g2, 1)

            for j in range(6):
                gated(j)
            for i in range(4):
                dve.wait_ge(s_hc, 32 + i + 1)
                b = fill_done(dve, ("oT", i))
                took(V.scalar_tensor_tensor(mixl[:, 2 * i:2 * i + 2], b[:, :].rearrange("p (h t) -> p h t", h=2),
                                            g_att8[:, 0:1], mixh[:, 2 * i:2 * i + 2].bitcast(F32),
                                            ALU.mult, ALU.subtract), ("oT", i))
            for j in range(6, SSM_C):
                gated(j)

            stored(dve, ("ssq", 0))
            own(V.reciprocal(sig[:, 0], sig[:, 0]))
            own.settle()
            for j in range(SSM_C):
                V.scalar_tensor_tensor(yT[:, j], yT[:, j], g_ssm[:, j:j + 1], sig[:, 0], ALU.mult,
                                       ALU.mult).then_inc(s_g2, 1)
            for j in range(SSM_C):
                dve.wait_ge(s_hc, 36 + j + 1)
                V.tensor_tensor(mixl[:, SSM_C + j], yT[:, j], mixh[:, SSM_C + j].bitcast(F32),
                                ALU.subtract).then_inc(s_mixs, 1)

            def residual(name, cb, t):
                b = fill_done(dve, (name, cb, t))
                took(V.tensor_tensor(H[:, t, 512 * cb:512 * cb + 512], b[:, :], H[:, t, 512 * cb:512 * cb + 512],
                                     ALU.add), (name, cb, t))

            dve.wait_ge(s_x, 32)
            for cb in range(4):
                for t in range(NT):
                    residual("wo", cb, t)
                if cb in (1, 2):
                    norm_lo(2, 2, 44, range(4) if cb == 1 else (4, 5))
            norm_lo(2, 2, 44, (6, 7))
            norm_diag(2)
            norm_spread(2)

            def head_max(h):
                b = fill_done(dve, ("xs", h))
                own(V.tensor_reduce(st_max[:, 2 * h:2 * h + 2], b[:, :].rearrange("p (t m) -> p t m", t=NT), AX.X, ALU.max))
                own.settle()
                V.tensor_scalar(st_max[:, 2 * h:2 * h + 2], st_max[:, 2 * h:2 * h + 2], -P ** -0.5, None,
                                ALU.mult).then_inc(s_xmax, 1)

            def head_norm(h):
                stored(dve, ("xs", h))
                own(V.reciprocal(st_rec[:, 2 * h:2 * h + 2], st_sum[:, 2 * h:2 * h + 2]))
                own.settle()
                for t in range(NT):
                    V.tensor_scalar(px[:, t, h], px[:, t, h], st_rec[:, 2 * h + t:2 * h + t + 1], None,
                                    ALU.mult).then_inc(s_xpn, 1)

            for j in range(3):
                evac(("xq", j), qxT[:, j])
            for h in (0, 1):
                head_max(h)
            evac(("xq", 3), qxT[:, 3])
            for h in (0, 1):
                head_norm(h)
            for h in (2, 3):
                head_max(h)
            for h in (2, 3):
                head_norm(h)
            for h in range(XH):
                dve.wait_ge(s_hc, 60 + h + 1)
                b = fill_done(dve, ("xo", h))
                took(V.tensor_tensor(oxl[:, h], b[:, 0:256], oxh[:, h].bitcast(F32), ALU.subtract), ("xo", h))
            for cb in range(4):
                for t in range(NT):
                    residual("xw", cb, t)
                if cb:
                    norm_lo(3, 3, 64, (2 * cb - 2, 2 * cb - 1))
            norm_lo(3, 3, 64, (6, 7))
            V.memset(zr[:, :].bitcast(F32), 0.0).then_inc(s_zr, 1)
            norm_diag(3)
            norm_spread(3)
            for c in range(16):
                evac(("pq", c), qP[:, c])
                if c == 1:
                    for t in range(NT):
                        V.tensor_scalar(nat[:, t], H[:, t], rstd[:, 6 + t:7 + t], None, ALU.mult).then_inc(s_xn, 1)
                if c in NAT_AT:
                    norm_lo(4, 3, 80, NAT_AT[c])

            own(V.tensor_copy(io16[:, :], iota_t[:, 0:TOPK]))
            own(V.tensor_tensor_reduce(repl[:, 0:P], ident[:, :], iota_t[:, 0:P], 1.0, 0.0, ALU.mult, ALU.add,
                                       tokf[:, 0:1]))
            own.settle()
            own(V.tensor_scalar(tokf[:, 1:2], tokf[:, 0:1], float(P), None, ALU.add))

            def top16(vals, idx, x):
                n = x.shape[1]
                own(V.max(vals[:, 0:8], x))
                own.settle()
                own(V.max_index(idx[:, 0:8], vals[:, 0:8], x))
                own(V.match_replace(repl[:, 0:n], vals[:, 0:8], x, -3e38))
                own.settle()
                own(V.max(vals[:, 8:16], repl[:, 0:n]))
                own.settle()
                own(V.max_index(idx[:, 8:16], vals[:, 8:16], repl[:, 0:n]))

            for t in range(NT):
                for i in range(8):
                    stored(dve, ("ps", i))
                for c in range(2 * PH):
                    top16(tv[:, c], ti[:, c], sc[:, t, c])
                own.settle()
                own(V.tensor_copy(tif[:, :, :], ti[:, :, :]))
                tv4 = tv[:, :, :].rearrange("p (h s) a -> p h s a", s=2)
                own(V.tensor_tensor(cand[:, :, :, :], tv4[:, :, 0].unsqueeze(3).to_broadcast([P, PH, TOPK, TOPK]),
                                    tv4[:, :, 1].unsqueeze(2).to_broadcast([P, PH, TOPK, TOPK]), ALU.add))
                own.settle()
                for h in range(PH):
                    top16(ts[:, h], ic[:, h], cand[:, h].rearrange("p a b -> p (a b)"))
                own.settle()
                own(V.tensor_tensor(gate[:, t], ts[:, :, :], ts[:, :, 0:1].to_broadcast([P, PH, TOPK]), ALU.subtract))
                own(V.tensor_single_scalar(icx[:, 0], ic[:, :, :], 4, ALU.logical_shift_right))
                own(V.tensor_single_scalar(icx[:, 1], ic[:, :, :], 15, ALU.bitwise_and))
                own.settle()
                V.tensor_copy(icf[:, :, :, :], icx[:, :, :, :]).then_inc(s_pick, 1)
                dve.wait_ge(s_pick, t + 1)
                tif4 = tif[:, :, :].rearrange("p (h s) a -> p h s a", s=2)
                for x in range(2):
                    own(V.tensor_tensor(eq[:, :, :, :], icf[:, x].unsqueeze(3).to_broadcast([P, PH, TOPK, TOPK]),
                                        io16[:, :].unsqueeze(1).unsqueeze(1).to_broadcast([P, PH, TOPK, TOPK]), ALU.is_equal))
                    own.settle()
                    own(V.tensor_tensor(eqv[:, :, :, :], eq[:, :, :, :],
                                        tif4[:, :, x].unsqueeze(2).to_broadcast([P, PH, TOPK, TOPK]), ALU.mult))
                    own.settle()
                    own(V.tensor_reduce(ef[:, x], eqv[:, :, :, :], AX.X, ALU.add))
                own.settle()
                own(V.scalar_tensor_tensor(ei[:, :, :], ef[:, 1], float(KEYS), ef[:, 0], ALU.mult, ALU.add))
                own.settle()
                own(V.tensor_scalar(ei[:, :, :], ei[:, :, :], float(S), tokf[:, t:t + 1], ALU.mult, ALU.add))
                dve.wait_ge(s_pexp, t + 1)
                own(V.tensor_reduce(g1[:, :], gate[:, t], AX.X, ALU.add))
                own.settle()
                own(V.reciprocal(g2[:, :], g1[:, :]))
                own.settle()
                own(V.tensor_tensor(gate[:, t], gate[:, t], g2[:, :].unsqueeze(2).to_broadcast([P, PH, TOPK]), ALU.mult))
                own.settle()
                V.tensor_copy(eidx[:, t], ei[:, :, :]).then_inc(s_idx, 1)

            def rest(i, j, base_hi, per):
                dve.wait_ge(s_hi, i * per + (base_hi + j + 1))
                V.tensor_tensor(lo[j % SLOTS][:, :], raw[j % SLOTS][:, :], hi[j % SLOTS][:, :].bitcast(F32),
                                ALU.subtract).then_inc(s_lo_vec, 1)

            with dve.Fori(0, (KEYS - UA) // 4) as i:
                for j in range(4):
                    rest(i, j, POOL_UNITS, 4)
            with dve.Fori(0, KEYS // 8) as i:
                for g in range(2):
                    dve.wait_ge(s_slab[g], i * 32 + 32)
                    dve.wait_ge(s_used, i * 8 + (V0 + 4 * g - 4))
                    dve.wait_ge(s_w, i * 4 + 2 * g)
                    V.tensor_tensor(Wf[:, :, :], As[:, g], Gs[:, g], ALU.mult).then_inc(s_wmul, 1)
                    dve.wait_ge(s_wmul, i * 2 + (g + 1))
                    V.tensor_copy(Wh[:, g], Wf[:, :, :]).then_inc(s_w, 1)
                    dve.wait_ge(s_w, i * 4 + (2 * g + 1))
                    V.tensor_tensor(Wl[:, g], Wf[:, :, :], Wh[:, g].bitcast(F32), ALU.subtract).then_inc(s_w, 1)
                    for j in range(4):
                        rest(i, 4 * g + j, V0, 8)
            dve.wait_ge(s_gf, 16)
            dve.wait_ge(s_used, END)

            def add(t):
                for c in range(4):
                    V.tensor_tensor(H[:, t, 512 * c:512 * c + 512], ps[4 * t + c][:, :],
                                    H[:, t, 512 * c:512 * c + 512], ALU.add).then_inc(s_fin, 1)

            def mean(t):
                dve.wait_ge(s_sq, 2 * 4 + 4 * (t + 1))
                own(V.tensor_reduce(stat[:, t:t + 1], sums[:, t], AX.X, ALU.add))
                own.settle()
                V.tensor_scalar(stat[:, 2 + t:3 + t], stat[:, t:t + 1], 1.0 / D, EPS, ALU.mult, ALU.add).then_inc(s_ms, 1)

            def out(t):
                dve.wait_ge(s_rt, 5 + t)
                own(V.reciprocal(stat[:, 12 + t:13 + t], stat[:, 8 + t:9 + t]))
                own.settle()
                dve.wait_ge(s_fin, 4 * (t + 1))
                for x in range(2):
                    half = slice(D // 2 * x, D // 2 * x + D // 2)
                    V.scalar_tensor_tensor(H[:, t, half], H[:, t, half], stat[:, 12 + t:13 + t], g_fin[:, half], ALU.mult,
                                           ALU.mult).then_inc(s_fo, 1)

            add(0)
            add(1)
            mean(0)
            out(0)
            mean(1)
            out(1)

        @block.tensor
        def _(pe):
            M = nc.tensor

            def bank(name):
                b, n = plan.at[name]
                if n:
                    pe.wait_ge(taken[b], n)
                return ps[b]

            def filled(ins, name):
                ins.then_inc(full[plan.at[name][0]], 1)

            def used(ins):
                ins.then_inc(s_used, 1)

            def unit(u):
                if u == 0:
                    pe.wait_ge(s_lo_first, 1)
                else:
                    pe.wait_ge(s_lo_pool, u)

            def three(out, wh, wl, xh, xl, start, stop):
                M.matmul(out, wh, xh, start=start, stop=False)
                M.matmul(out, wh, xl, start=False, stop=False)
                return M.matmul(out, wl, xh, start=False, stop=stop)

            def norm(kk, src, cps=range(8)):
                for cp in cps:
                    b = bank(("norm", kk, cp))
                    for c in range(2):
                        for t in range(NT):
                            ins = M.transpose(b[:, 256 * c + P * t:256 * c + P * t + P],
                                              src[:, t, P * (2 * cp + c):P * (2 * cp + c) + P], ident[:, :])
                    filled(ins, ("norm", kk, cp))

            def spread(kk):
                b = bank(("rb", kk))
                pe.wait_ge(s_dg, NT * (kk + 1))
                filled(M.matmul(b[:, 0:256], ones[:, :], diag[:, :, :].rearrange("p t n -> p (t n)"),
                                start=True, stop=True), ("rb", kk))

            def cols_unit(name, u, xh=XTh, xl=XTl, ready=None):
                b = bank(name)
                unit(u)
                s = u % SLOTS
                for c in range(DC):
                    if ready is not None and c % 2 == 0:
                        stored(pe, ("norm", ready, c // 2))
                    ins = three(b[:, 0:256], hi[s][:, P * c:P * c + P], lo[s][:, P * c:P * c + P],
                                xh[:, c], xl[:, c], c == 0, c == DC - 1)
                ins.then_inc(s_used, 1)

            def rows_unit(name, u, q, n, xh, xl, step=None, ready=False):
                if q == 0:
                    b = [bank((*name, t)) for t in range(NT)]
                else:
                    b = [ps[plan.at[(*name, t)][0]] for t in range(NT)]
                unit(u)
                s = u % SLOTS
                for c in range(4):
                    if ready:
                        stored(pe, ("xo", c))
                    for t in range(NT):
                        k = 4 * q + c
                        x_h, x_l = xh[:, k, P * t:P * t + P], xl[:, k, P * t:P * t + P]
                        w_h, w_l = hi[s][:, 512 * c:512 * c + 512], lo[s][:, 512 * c:512 * c + 512]
                        M.matmul(b[t][:, :], x_h, w_h, start=k == 0, stop=False)
                        M.matmul(b[t][:, :], x_h, w_l, start=False, stop=False)
                        ins = M.matmul(b[t][:, :], x_l, w_h, start=False, stop=k == 4 * n - 1)
                    if c == 3:
                        used(ins)
                    if step:
                        step(4 * q + c)

            def rows_block(name, u0, n, xh, xl, step=None):
                for q in range(n):
                    rows_unit(name, u0 + q, q, n, xh, xl, step)

            pe.wait_ge(s_cst, CST)
            for x in range(4):
                pe.wait_ge(s_mem[x], 16)
                norm(0, mem, (2 * x, 2 * x + 1))
            for j in range(4):
                cols_unit(("mk", j), j, memh, meml, 0 if j == 0 else None)
                if j == 1:
                    spread(0)
                    pe.wait_ge(s_x, 16)
                    norm(1, H)
            spread(1)
            rows_block(("mv",), 4, 4, memh, meml)
            for cp in range(8):
                stored(pe, ("norm", 1, cp))
            for j in range(8):
                cols_unit(("uw", j), UW0 + j)
            pe.wait_ge(s_bw, 2)

            def bu(b):
                if b >= NBLK:
                    return
                j, q = b // 4, b % 4
                r = slice(32 * q, 32 * q + 32)
                out = bank(("bu", b))
                if q == 0:
                    stored(pe, ("uw", j))
                for c in range(2):
                    ins = M.matmul(out[:, 256 * c:256 * c + 256], BW[r, c, j], uT[r, j], start=True, stop=True,
                                   skip_group_check=True)
                filled(ins, ("bu", b))

            def y(b):
                if b < 0:
                    return
                j, q = b // 4, b % 4
                if q == 0 and j >= 2:
                    pe.wait_ge(s_yv, j - 1)
                pe.wait_ge(s_xs, 2 * b + 2)
                out = ps[6 + j % 2][32 * q:32 * q + 32, 0:256]
                M.matmul(out, CW[:, b, 0], xst[:, b % 2, 0], start=True, stop=False, skip_group_check=True)
                M.matmul(out, CW[:, b, 1], xst[:, b % 2, 1], start=False, stop=True,
                         skip_group_check=True).then_inc(s_ymm, 1)

            def slot(s):
                bu(s)
                y(s - 2)

            def glu(j):
                unit(GLU0 + j)
                s = (GLU0 + j) % SLOTS
                for c in range(2):
                    b = bank(("glu", 2 * j + c))
                    for kk in range(SSM_C):
                        if j == 0 and c == 0:
                            pe.wait_ge(s_bw, 2 + kk + 1)
                        o = 1024 * c + P * kk
                        ins = three(b[:, 0:256], hi[s][:, o:o + P], lo[s][:, o:o + P], gTh[:, kk], gTl[:, kk],
                                    kk == 0, kk == SSM_C - 1)
                used(ins)

            def attention_step(g, hf):
                x = g - HALF_AT[hf]
                if 0 <= x - QKT_AT < 4:
                    i = x - QKT_AT
                    kq, t = i // 2, i % 2
                    b = bank(("qkT", hf, i))
                    pe.wait_ge(s_rope, 4 * hf + 4)
                    for h in range(4):
                        col = 512 * kq + P * h
                        ins = M.transpose(b[:, P * h:P * h + P], zqk[:, t, col:col + P], ident[:, :])
                    filled(ins, ("qkT", hf, i))
                if 0 <= x - S0_AT < 2:
                    i = x - S0_AT
                    b = bank(("s0", hf, i))
                    if i == 0:
                        for k in range(4):
                            stored(pe, ("qkT", hf, k))
                    r = slice(64 * i, 64 * i + 64)
                    for h in range(4):
                        ins = M.matmul(b[:, P * h:P * h + P], qkT[r, 0, h, 0:P], qkT[r, 1, h, 0:P], start=True, stop=True,
                                       skip_group_check=True)
                    filled(ins, ("s0", hf, i))
                if 0 <= x - S1_AT < 4:
                    i = x - S1_AT
                    b = bank(("s1", hf, i))
                    c = i % 2
                    r = slice(64 * c, 64 * c + 64)
                    for k in range(2):
                        h = 2 * (i // 2) + k
                        ins = M.matmul(b[:, S * k:S * k + S], qkT[r, 0, h, P:S], qkT[r, 1, h, 0:S], start=True, stop=True,
                                       skip_group_check=True)
                    filled(ins, ("s1", hf, i))
                if x == AT_AT:
                    b = bank(("aT", hf, 0))
                    pe.wait_ge(s_comb, 8 * hf + 4)
                    for h in range(4):
                        ins = M.transpose(b[:, P * h:P * h + P], p0[:, 2 * h], ident[:, :])
                    filled(ins, ("aT", hf, 0))
                if 1 <= x - AT_AT < 3:
                    i = x - AT_AT
                    b = bank(("aT", hf, i))
                    pe.wait_ge(s_comb, 8 * hf + 4 + 2 * i)
                    for k in range(2):
                        for kk in range(2):
                            ins = M.transpose(b[:, P * (2 * k + kk):P * (2 * k + kk) + P],
                                              p1[:, 2 * (2 * (i - 1) + k), P * kk:P * kk + P], ident[:, :])
                    filled(ins, ("aT", hf, i))

            for cb in range(6):
                def step(x, cb=cb):
                    g = 16 * cb + x
                    if g % BLOCK_EVERY == 0:
                        slot(g // BLOCK_EVERY)
                    for hf in range(2):
                        attention_step(g, hf)
                rows_block(("qkv", cb), QKV0 + 4 * cb, 4, XTh, XTl, step)

            y(NBLK - 2)
            y(NBLK - 1)

            for hf in range(2):
                for i in range(3):
                    stored(pe, ("aT", hf, i))
                for t in range(NT):
                    stored(pe, ("qkv", 4 + hf, t))
            for i in range(4):
                t, hf = i // 2, i % 2
                b = bank(("av", i))
                if i >= 2:
                    pe.wait_ge(s_yv, SSM_C - 3 + i)
                for x in range(4):
                    h = 4 * hf + x
                    out = b[:, P * x:P * x + P]
                    if t == 0:
                        ins = M.matmul(out, aT0[:, h], vnat[:, 0, P * h:P * h + P], start=True, stop=True,
                                       skip_group_check=True)
                    else:
                        for kk in range(2):
                            ins = M.matmul(out, aT1[:, h, kk], vnat[:, kk, P * h:P * h + P],
                                           start=kk == 0, stop=kk == 1, skip_group_check=True)
                filled(ins, ("av", i))
            for j in range(3):
                glu(j)
            for i in range(4):
                b = bank(("oT", i))
                for t in range(NT):
                    stored(pe, ("av", 2 * t + i // 2))
                    for x in range(2):
                        h = 2 * i + x
                        ins = M.transpose(b[:, S * x + P * t:S * x + P * t + P], att_n[:, t, P * h:P * h + P], ident[:, :])
                filled(ins, ("oT", i))
            glu(3)
            for i in range(4):
                stored(pe, ("oT", i))
            for n in range(16):
                cb, q = WO_ORDER[n] // 4, WO_ORDER[n] % 4
                if n == 4:
                    pe.wait_ge(s_mixs, 2 * SSM_C)
                rows_unit(("wo", cb), WO0 + n, q, 4, mixh, mixl)
                if n == 0:
                    b = bank(("ssq", 0))
                    for j in range(SSM_C):
                        pe.wait_ge(s_mixs, j + 1)
                        ins = M.matmul(b[:, 0:256], ones[:, :], sqb[:, j], start=j == 0, stop=j == SSM_C - 1)
                    filled(ins, ("ssq", 0))
                if n == 9:
                    for c in range(2):
                        for t in range(NT):
                            stored(pe, ("wo", c, t))
                    norm(2, H, range(4))
                if n == 13:
                    for t in range(NT):
                        stored(pe, ("wo", 2, t))
                    norm(2, H, (4, 5))

            for t in range(NT):
                stored(pe, ("wo", 3, t))
            norm(2, H, (6, 7))
            def scores(h):
                b = bank(("xs", h))
                stored(pe, ("xq", h))
                for t in range(NT):
                    ins = M.matmul(b[:, S * t:S * t + S], qxT[:, h, P * t:P * t + P], kxT[:, h], start=True,
                                   stop=True, skip_group_check=True)
                filled(ins, ("xs", h))

            def probs(h):
                b = bank(("xp", h))
                pe.wait_ge(s_xpn, 2 * h + 2)
                for kk in range(2):
                    for t in range(NT):
                        ins = M.transpose(b[:, S * kk + P * t:S * kk + P * t + P], px[:, t, h, P * kk:P * kk + P], ident[:, :])
                filled(ins, ("xp", h))

            def output(h):
                b = bank(("xo", h))
                stored(pe, ("xp", h))
                for kk in range(2):
                    ins = M.matmul(b[:, 0:256], vx[:, kk, P * h:P * h + P], pxT[:, h, kk], start=kk == 0, stop=kk == 1)
                filled(ins, ("xo", h))

            for j in range(4):
                cols_unit(("xq", j), XQ0 + j, XT2h, XT2l, 2 if j == 0 else None)
                if j == 1:
                    spread(2)
                if j == 2:
                    scores(0)
                    scores(1)
            for job, heads in ((probs, (0, 1)), (scores, (2, 3)), (output, (0, 1)), (probs, (2, 3)), (output, (2, 3))):
                for h in heads:
                    job(h)
            for cb in range(4):
                rows_unit(("xw", cb), XO0 + cb, 0, 1, oxh, oxl, ready=cb == 0)
                if cb:
                    for t in range(NT):
                        stored(pe, ("xw", cb - 1, t))
                    norm(3, H, (2 * cb - 2, 2 * cb - 1))
            for t in range(NT):
                stored(pe, ("xw", 3, t))
            norm(3, H, (6, 7))

            for c in range(16):
                cols_unit(("pq", c), PQ0 + c, XT2h, XT2l, 3 if c == 0 else None)
                if c == 1:
                    spread(3)
                if c in NAT_AT:
                    pe.wait_ge(s_xn, NT)
                    norm(4, nat, NAT_AT[c])
            for cp in range(8):
                stored(pe, ("norm", 4, cp))
            pe.wait_ge(s_keys, 16)
            for i in range(8):
                t = i // 4
                b = bank(("ps", i))
                for x in range(4):
                    c = 4 * (i % 4) + x
                    stored(pe, ("pq", c))
                    ins = M.matmul(b[:, P * x:P * x + P], qP[:, c, P * t:P * t + P], keys[:, c], start=True,
                                   stop=True, skip_group_check=True)
                filled(ins, ("ps", i))
            for i in range(4, 8):
                stored(pe, ("ps", i))
            pe.sem_inc(s_ubank, 4)

            def expert_unit(i, j, gu0, lo_sem, lo0, per):
                pe.wait_ge(lo_sem, i * per + (lo0 + j + 1))
                pe.wait_ge(s_ubank, i * per + (gu0 + j + 1))
                s = j % SLOTS
                for c in range(DC):
                    ins = three(ps[s][:, 0:256], hi[s][:, P * c:P * c + P], lo[s][:, P * c:P * c + P],
                                XTh[:, c], XTl[:, c], c == 0, c == DC - 1)
                used(ins)

            def clear(b):
                M.matmul(ps[b][:, :], zr[:, 0:P], zr[:, :], start=True, stop=False, skip_group_check=True)

            pe.wait_ge(s_zr, 1)
            for b in range(4, 8):
                clear(b)
            with pe.Fori(0, UA // 4) as i:
                for j in range(4):
                    expert_unit(i, j, 0, s_lo_pool, U0 - 1, 4)
            with pe.Fori(0, (KEYS - UA) // 4) as i:
                for j in range(4):
                    expert_unit(i, j, UA, s_lo_vec, 0, 4)
            for b in range(4):
                pe.wait_ge(s_ubank, KEYS + 1 + b)
                clear(b)
            with pe.Fori(0, KEYS // 8) as i:
                for g in range(2):
                    pe.wait_ge(s_w, i * 4 + (2 * g + 2))
                    for j in range(4):
                        pe.wait_ge(s_lo_vec, i * 8 + (KEYS - UA + 4 * g + j + 1))
                        for t in range(NT):
                            wh, wl = Wh[:, g, j, P * t:P * t + P], Wl[:, g, j, P * t:P * t + P]
                            for x, v in ((wh, hi), (wh, lo), (wl, hi)):
                                for c in range(4):
                                    ins = M.matmul(ps[4 * t + c][:, :], x, v[j][:, 512 * c:512 * c + 512],
                                                   start=False, stop=True, skip_group_check=True)
                        ins.then_inc(s_used, 1)


def kernel(**inputs):
    import numpy as np
    import concourse.bacc as bacc
    from concourse.bass_utils import run_bass_kernel_spmd

    a = {k: np.asarray(v) for k, v in inputs.items()}

    def cont(x):
        return np.ascontiguousarray(x)

    def cols(v):
        return cont(v.reshape(-1, P).T)

    def by_cols(w):
        kc, n = w.shape[0] // P, w.shape[1] // P
        return cont(w.reshape(kc, P, n, P).transpose(2, 1, 0, 3)).reshape(-1, P, kc * P)

    def by_rows(w, order=None):
        q, n = w.shape[0] // (4 * P), w.shape[1] // 512
        return cont(w.reshape(q, 4, P, n, 512).transpose(3, 0, 2, 1, 4)[order or list(range(n))]).reshape(-1, P, D)

    w_in, w_kv = a["w_in"][0], a["xattn_wkv"][0]
    glu = by_cols(a["glu_w"][0]).reshape(4, 2, P, SSM_W).transpose(0, 2, 1, 3)
    b_all = np.stack([a["ssm_b_re"][0], a["ssm_b_im"][0]])
    c_all = np.stack([a["ssm_c_re"][0], a["ssm_c_im"][0]])
    keys = np.stack([a["peer_k1"][0], a["peer_k2"][0]], axis=1)
    vecs = np.zeros((P, VECS), np.float32)
    for n, v in (("gains", np.concatenate([cols(a[m][0]) for m in ("mem_norm_g", "mix_norm_g", "xattn_norm_g",
                                                                  "ffn_norm_g")], 1)),
                 ("g_att", cols(a["attn_head_g"][0])), ("g_ssm", cols(a["ssm_out_g"][0])), ("glu_b", cols(a["glu_b"][0])),
                 ("d_skip", cols(a["ssm_d"][0].reshape(-1))),
                 ("lam", np.concatenate([a[m].reshape(1, QK) for m in ("lam_q1", "lam_k1", "lam_q2", "lam_k2")], 1))):
        o, c = VEC_AT[n]
        vecs[:, o:o + c] = v
    arrays = {
        "x": a["x"][0], "mem": a["mem"][0],
        "w_mk": by_cols(w_kv[:, :XW]), "w_mv": by_rows(w_kv[:, XW:]),
        "w_u": by_cols(w_in[:, 3 * ATT:]), "w_qkv": by_rows(w_in[:, :3 * ATT], QKV_ORDER),
        "w_glu": cont(glu).reshape(4, P, D), "w_wo": by_rows(a["w_out"][0])[WO_ORDER],
        "w_xq": by_cols(a["xattn_wq"][0]), "w_xo": by_rows(a["xattn_wo"][0]),
        "w_pq": by_cols(a["peer_wq"][0]),
        "u": cont(a["peer_u"][0].reshape(KEYS, KEYS, DC, P).transpose(1, 3, 2, 0)).reshape(KEYS, P, D),
        "v": cont(a["peer_v"][0].reshape(KEYS, KEYS, D).transpose(1, 0, 2)),
        "vecs": vecs, "pos": cols(a["positions"][0]),
        "ssm": np.stack([cols(a["ssm_a_re"][0].reshape(-1)), cols(a["ssm_a_im"][0].reshape(-1)),
                         np.repeat(a["ssm_log_dt"].reshape(NBLK, 2).T, P // 2, axis=0)], 1),
        "bT": cont(b_all.reshape(2, SSM_C, 8, QK, 16).transpose(2, 4, 0, 1, 3)).reshape(P, 2, SSM_C, QK),
        "cT": cont(c_all.reshape(2, NBLK, 2, 16, QK).transpose(2, 4, 0, 1, 3)).reshape(P, 2, NBLK, 16),
        "keys": cont(keys.reshape(2 * PH, KEYS, P).transpose(2, 0, 1)),
        "g_fin": a["final_norm_g"].reshape(1, D),
    }
    arrays = {f"in_{n}": cont(v) for n, v in arrays.items()}
    nc = bacc.Bacc("TRN2", target_bir_lowering=False, num_devices=1)
    T = {n[3:]: nc.dram_tensor(n, v.shape, mybir.dt.from_np(v.dtype), kind="ExternalInput").ap()
         for n, v in arrays.items()}
    for n in ("x", "mem"):
        T[n] = T[n].rearrange("(t p) d -> p t d", p=P)
    T["out"] = nc.dram_tensor("out", (S, D), F32, kind="ExternalOutput").ap()
    hymba_peer(nc, T)
    r = run_bass_kernel_spmd(nc, [arrays], core_ids=[0])
    return r.results[0]["out"].reshape(1, S, D)
```

```python
import math
from contextlib import ExitStack

import concourse.bass as bass
from concourse import mybir

F32 = mybir.dt.float32
F32R = mybir.dt.float32r
I32 = mybir.dt.int32
U32 = mybir.dt.uint32
BF16 = mybir.dt.bfloat16
ALU = mybir.AluOpType
ACT = mybir.ActivationFunctionType
AX = mybir.AxisListType

P = 128
D = 2048
S = 256
NT = S // P
DC = D // P
HEADS = 8
ATT = 1024
QK = 64
SSM_W = 1024
SSM_C = SSM_W // P
NBLK = 32
XH = 4
XW = 512
PH = 8
KEYS = 128
TOPK = 16
EPS = 1e-6
LAM_INIT = 0.8 - 0.6 * math.exp(-0.3 * 0)
TWO_PI = 2 * math.pi
PI_IN = 3.1415925
C1 = 6.28125
C2 = float(int((TWO_PI - C1) * 2 ** 20)) / 2 ** 20
C3 = TWO_PI - C1 - C2
ROUND = 1.5 * 2 ** 23
ROUND15 = 1.5 * 2 ** 8
NEG = -1e30
ROPE = [500000.0 ** (-j / 16.0) for j in range(0, 16, 2)]

UW0 = 8
QKV0 = 16
GLU0 = 40
WO0 = 44
XQ0 = 60
XO0 = 64
PQ0 = 68
U0 = 84
V0 = U0 + KEYS
END = V0 + KEYS
UA = 32
POOL_UNITS = U0 + UA
PICKS_AT = [13, 26]
SLOTS = 4
CST = 18
QKV_ORDER = [0, 2, 1, 3, 4, 5]
STEPS = 4 * 24
ZERO_AT = 46
TABLES_AT = 10
BLOCK_EVERY = 3
BLOCKS_BEFORE = [-(-4 * n // BLOCK_EVERY) for n in range(25)]
HALF_AT = [STEPS // 3, 2 * STEPS // 3]
ROPE_AT, QKT_AT, S0_AT, S1_AT, MAX_AT, EXP_AT, COMB_AT, AT_AT = 1, 4, 9, 11, 16, 17, 20, 23
WO_ORDER = [0, 1, 4, 5, 2, 3, 6, 7] + list(range(8, 16))
assert BLOCKS_BEFORE[24] == NBLK
GELU_AT = [min(n for n in range(25) if BLOCKS_BEFORE[n] >= 4 * j + 4) + 2 for j in range(6)] + [23]
NAT_AT = {6: range(4), 9: range(4, 8)}
GLU_HI_AT = [80, 81, 82, 85, 86, 87, 95]
GLU_LO_AT = [83, 84, 85, 89, 90, 91]
GROUPS = NBLK // 4


VEC_AT = {"gains": (0, 4 * DC), "g_att": (64, 1), "g_ssm": (72, SSM_C), "glu_b": (80, SSM_C), "d_skip": (88, SSM_C),
          "lam": (96, 4 * QK)}
VECS = 96 + 4 * QK


class Banks:

    def __init__(self):
        self.uses = [0] * 8
        self.at = {}
        self.unit = {}

    def add(self, name, bank, unit=None):
        self.at[name] = (bank, self.uses[bank])
        self.uses[bank] += 1
        if unit is not None:
            self.unit[name] = unit


def plan_banks():
    b = Banks()

    def norm(k, bank0=0):
        for cp in range(8):
            b.add(("norm", k, cp), bank0 + cp % 4)

    norm(0)
    for j in range(4):
        b.add(("mk", j), j, j)
        if j == 1:
            b.add(("rb", 0), 4)
            norm(1, 4)
    b.add(("rb", 1), 4)
    for t in range(2):
        b.add(("mv", t), t, 7)
    for j in range(8):
        b.add(("uw", j), (j + 2) % 4, UW0 + j)
    for s in range(NBLK):
        b.add(("bu", s), 4 + s % 2)
    jobs = [(QKT_AT + i, ("qkT", i)) for i in range(4)] + [(S0_AT + i, ("s0", i)) for i in range(2)] + \
        [(S1_AT + i, ("s1", i)) for i in range(4)] + [(AT_AT + i, ("aT", i)) for i in range(3)]
    for cb in range(6):
        for t in range(2):
            b.add(("qkv", cb, t), 2 * (cb % 2) + t, QKV0 + 4 * cb + 3)
        for x, at in enumerate(HALF_AT):
            for step, (name, i) in jobs:
                if (at + step) // 16 == cb:
                    b.add((name, x, i), 2 * (1 - cb % 2) + i % 2)
    for i in range(4):
        b.add(("av", i), 4 + i)
    for ct in range(8):
        b.add(("glu", ct), ct % 4, GLU0 + ct // 2)
    for i in range(4):
        b.add(("oT", i), 4 + i)
    b.add(("ssq", 0), 4)
    for cb in range(4):
        for t in range(2):
            b.add(("wo", cb, t), 2 * (cb % 2) + t, WO0 + (5 if cb == 0 else 4 * cb + 3))
    norm(2, 4)
    for j in range(4):
        b.add(("xq", j), j, XQ0 + j)
        if j == 1:
            b.add(("rb", 2), 4)
    for name, bank0 in (("xs", 4), ("xp", 0), ("xo", 4)):
        for h in range(4):
            b.add((name, h), bank0 + h)
    for cb in range(4):
        for t in range(2):
            b.add(("xw", cb, t), 2 * (cb % 2) + t, XO0 + cb)
    norm(3, 4)
    b.add(("rb", 3), 4)
    norm(4, 4)
    for c in range(16):
        b.add(("pq", c), c % 4, PQ0 + c)
    for i in range(8):
        b.add(("ps", i), i % 4)
    count, b.fills = [0] * 8, {}
    for name, (bank, _) in b.at.items():
        if name not in b.unit:
            count[bank] += 1
            b.fills[name] = count[bank]
    return b


class Chain:

    def __init__(self, eng, sem):
        self.eng, self.sem, self.n = eng, sem, 0

    def __call__(self, ins):
        ins.then_inc(self.sem, 1)
        self.n += 1
        return self.n

    def settle(self):
        self.eng.wait_ge(self.sem, self.n)


def hymba_peer(nc, T):
    ctx = ExitStack()
    with ctx:
        base = 16512

        def at(name, kb, shape, dt=F32):
            return nc.alloc_sbuf_tensor_at(name, shape, dt, offset=base + int(kb * 1024))

        def sem(name):
            return ctx.enter_context(nc.semaphore(name))

        def sems(name, n):
            return [sem(f"{name}{i}") for i in range(n)]

        raw = [at(f"raw{i}", 8 * i, [P, 2048]) for i in range(SLOTS)]
        lo = [at(f"lo{i}", 8 * i, [P, 2048], F32R) for i in range(SLOTS)]
        hi = [at(f"hi{i}", 32 + 8 * i, [P, 2048], F32R) for i in range(SLOTS)]
        H = at("H", 64, [P, NT, D])
        k = 80.0
        small = {}

        def sm(name, shape, dt=F32):
            nonlocal k
            n = 4
            for x in shape[1:]:
                n *= x
            small[name] = at(name, k, shape, dt)
            k += max(n, 32) / 1024
            k = math.ceil(k * 32) / 32
            return small[name]

        ident = sm("ident", [P, P])
        maskd = sm("maskd", [P, 2, P])
        vecs = sm("vecs", [P, VECS])
        vec = {n: vecs[:, o:o + c] for n, (o, c) in VEC_AT.items()}
        gains = vec["gains"].rearrange("p (n c) -> p n c", n=4)
        g_att, g_ssm, glu_b, d_skip = (vec[n] for n in ("g_att", "g_ssm", "glu_b", "d_skip"))
        lamv = vec["lam"].rearrange("p (n d) -> p n d", n=4)
        g_att8 = sm("g_att8", [P, 1])
        lams = sm("lams", [P, 8])
        posi = sm("posi", [P, NT], I32)
        posf = sm("posf", [P, NT])
        freq = sm("freq", [P, 8])
        rcos = sm("rcos", [P, NT, 8])
        rsin = sm("rsin", [P, NT, 8])
        stat = sm("stat", [P, 16])
        rstd = sm("rstd", [P, 8])
        assert k <= 84.1, k
        k = 84.25
        prm = at("prm", k, [P, 20, NBLK])
        k += 2.5
        st_max = at("st_max", k, [P, 32])
        st_sum = at("st_sum", k + 0.125, [P, 32])
        st_rec = at("st_rec", k + 0.25, [P, 32])
        head_ms = at("head_ms", k + 0.375, [P, 16])
        ones = at("ones", 207, [P, P])
        eps = at("eps", k + 0.5, [P, 1])
        magic = at("magic", k + 0.53125, [P, 1])
        one = at("one", k + 0.5625, [P, 1])
        half_mask = at("half_mask", k + 0.59375, [P, 2])
        quarter = at("quarter", k + 0.625, [P, 1])

        XTh = at("XTh", 88, [P, DC, S], F32R)
        XTl = at("XTl", 104, [P, DC, S], F32R)
        p0 = at("p0", 64, [P, HEADS, P])
        p1 = at("p1", 68, [P, HEADS, S])
        aT0 = at("aT0", 76, [P, HEADS, P])
        aT1 = at("aT1", 168, [P, HEADS, 2, P])
        zqk = at("zqk", 128, [P, NT, ATT])
        qkT = at("qkT", 136, [P, 2, HEADS // 2, S])
        mixh = at("mixh", 88, [P, DC, S], F32R)
        mixl = at("mixl", 104, [P, DC, S], F32R)
        uT = at("uT", 120, [P, SSM_C, S])
        sig = at("sig", 160, [P, SSM_C, S])
        nat = at("nat", 176, [P, NT, D])
        mem = at("mem", 152, [P, NT, D])
        memh = at("memh", 120, [P, DC, S], F32R)
        meml = at("meml", 136, [P, DC, S], F32R)
        XT2h = at("XT2h", 128, [P, DC, S], F32R)
        XT2l = at("XT2l", 144, [P, DC, S], F32R)
        att_n = at("att_n", 152, [P, NT, ATT])
        vnat = at("vnat", 144, [P, NT, ATT])
        junk = at("junk", 176, [P, D], BF16)
        hjunk = at("hjunk", 87.5, [P, P], BF16)
        BW = at("BW", 152, [P, 2, SSM_C, P])
        CW = at("CW", 160, [P, NBLK, 2, 32])
        yT = uT
        tab = [at(f"tab{i}", o, [P, 2, S]) for i, o in enumerate((176, 178, 190, 192))]
        tgrp = at("tgrp", 128, [P, 2, 2, 4, S])
        phF = at("phF", 168, [P, 2, 4, S])
        m1 = at("m1", 180, [P, 2, S])
        m2 = at("m2", 182, [P, 2, S])
        dem = at("dem", 184, [P, 2, S])
        xst = at("xst", 186, [P, 2, 2, S])
        phA = at("phA", 180, [P, 4, S])
        phR = at("phR", 184, [P, 4, S])
        kxT = at("kxT", 194, [P, XH, S])
        vx = at("vx", 198, [P, NT, XW])
        iota_t = at("iota_t", 202, [P, S])
        zero = at("zero", 203, [P, 512])
        diag = at("diag", 205, [P, NT, P])
        Rb = at("Rb", 206, [P, S])
        braw = at("braw", 180, [P, 2, SSM_C, 64])
        craw = at("craw", 184, [P, 2, NBLK, 16])
        ctmp = at("ctmp", 188, [P, 2, NBLK, 16])
        gTh = at("gTh", 128, [P, SSM_C, S], F32R)
        gTl = at("gTl", 136, [P, SSM_C, S], F32R)
        sqb = at("sqb", 176, [P, SSM_C, S])
        qxT = at("qxT", 88, [P, XH, S])
        px = at("px", 92, [P, NT, XH, S])
        pxT = at("pxT", 100, [P, XH, 2, S])
        oxh = at("oxh", 108, [P, XH, S], F32R)
        oxl = at("oxl", 112, [P, XH, S], F32R)
        keys = at("keys", 120, [P, 2 * PH, KEYS])
        qP = at("qP", 160, [P, 2 * PH, S])
        sc = at("sc", 144, [P, NT, 2 * PH, KEYS])
        cand = at("cand", 176, [P, PH, TOPK, TOPK])
        repl = at("repl", 184, [P, 256])
        k = 185.0
        tv = at("tv", k, [P, 2 * PH, TOPK])
        ti = at("ti", k + 1, [P, 2 * PH, TOPK], U32)
        tif = at("tif", k + 2, [P, 2 * PH, TOPK])
        ts = at("ts", k + 3, [P, PH, TOPK])
        ic = at("ic", k + 3.5, [P, PH, TOPK], U32)
        icx = at("icx", k + 4, [P, 2, PH, TOPK], U32)
        icf = at("icf", k + 5, [P, 2, PH, TOPK])
        ef = at("ef", k + 6, [P, 2, PH, TOPK])
        ei = at("ei", k + 7, [P, PH, TOPK])
        gate = at("gate", k + 7.5, [P, NT, PH, TOPK])
        eidx = at("eidx", k + 8.5, [P, NT, PH, TOPK], I32)
        io16 = at("io16", k + 9.5, [P, TOPK])
        tokf = at("tokf", k + 9.5625, [P, NT])
        g1 = at("g1", k + 9.625, [P, PH])
        g2 = at("g2", k + 9.6875, [P, PH])
        eq = at("eq", 160, [P, PH, TOPK, TOPK])
        eqv = at("eqv", 168, [P, PH, TOPK, TOPK])
        gbuf = at("gbuf", 128, [P, 2, 4, S])
        As = at("As", 144, [P, 2, 4, S])
        Gs = at("Gs", 152, [P, 2, 4, S])
        Wf = at("Wf", 160, [P, 4, S])
        Wh = at("Wh", 164, [P, 2, 4, S], F32R)
        Wl = at("Wl", 172, [P, 2, 4, S], F32R)
        zr = at("zr", 195, [P, 512], F32R)
        sqs = at("sqs", 160, [P, NT, D], BF16)
        sums = at("sums", 180, [P, NT, 4])
        g_fin = at("g_fin", 197, [P, D])

        ps = [ctx.enter_context(nc.psum_tensor(f"ps{i}", [P, 512], F32)) for i in range(8)]
        ACTS = nc.dram_tensor("acts_dram", (KEYS, P, S), F32, kind="Internal").ap()
        TABD = nc.dram_tensor("tables_dram", (GROUPS, P, 2, 4, S), F32, kind="Internal").ap()
        GD = nc.dram_tensor("gates_dram", (KEYS * P * S, 1), F32, kind="Internal").ap()
        gd_zero = GD.rearrange("(z p n) o -> z p (n o)", p=P, n=512)
        gd_slab = GD.rearrange("(n p t) o -> n p (t o)", p=P, t=S)

        plan = plan_banks()
        full = sems("full", 8)
        taken = sems("taken", 8)

        ssm_vectors_loaded = sem("ssm_vectors_loaded")
        vectors_loaded = sem("vectors_loaded")
        b_c_loaded = sem("b_c_loaded")
        mem_loaded = sems("mem_loaded", 4)
        x_loaded = sem("x_loaded")
        keys_loaded = sem("keys_loaded")
        final_gain_loaded = sem("final_gain_loaded")
        unit_loaded = sems("unit_loaded", SLOTS)
        hi_ready = sem("hi_ready")
        rest_ready_pool = sem("rest_ready_pool")
        rest_ready_vector = sem("rest_ready_vector")
        rest_ready_first = sem("rest_ready_first")
        units_used = sem("units_used")
        constants_ready = sem("constants_ready")
        zero_ready = sem("zero_ready")
        gates_cleared = sem("gates_cleared")
        squares_summed = sem("squares_summed")
        mean_ready = sem("mean_ready")
        root_ready = sem("root_ready")
        rows_normalised = sem("rows_normalised")
        hi_chunks = sem("hi_chunks")
        vector_own = sem("vector_own")
        scalar_own = sem("scalar_own")
        params_vector = sem("params_vector")
        params_scalar = sem("params_scalar")
        ssm_glu_inputs = sem("ssm_glu_inputs")
        phases_ready = sem("phases_ready")
        sines_read = sem("sines_read")
        tables_stored = sems("tables_stored", 2)
        table_loaded = sems("table_loaded", 4)
        diagonal_ready = sem("diagonal_ready")
        block_turned = sem("block_turned")
        states_ready = sem("states_ready")
        outputs_ready = sem("outputs_ready")
        y_ready = sem("y_ready")
        gelu_ready = sem("gelu_ready")
        glu_hi_ready = sem("glu_hi_ready")
        gated_ready = sem("gated_ready")
        mix_ready = sem("mix_ready")
        half_rotated = sem("half_rotated")
        maxima_ready = sem("maxima_ready")
        exps_ready = sem("exps_ready")
        differences_ready = sem("differences_ready")
        factors_ready = sem("factors_ready")
        second_scaled = sem("second_scaled")
        head_mean_ready = sem("head_mean_ready")
        head_squares = sem("head_squares")
        head_root_ready = sem("head_root_ready")
        cross_maxima_ready = sem("cross_maxima_ready")
        cross_probs_ready = sem("cross_probs_ready")
        picks_ready = sem("picks_ready")
        pick_exps_ready = sem("pick_exps_ready")
        places_ready = sem("places_ready")
        gates_added = sem("gates_added")
        acts_stored = sems("acts_stored", 2)
        slabs_loaded = sems("slabs_loaded", 2)
        weights_multiplied = sem("weights_multiplied")
        weight_parts_ready = sem("weight_parts_ready")
        output_added = sem("output_added")
        out_ready = sem("out_ready")
        out_stored = sem("out_stored")
        zeros_ready = sem("zeros_ready")
        u_bank_free = sem("u_bank_free")

        def fill_done(eng, name):
            b, _ = plan.at[name]
            if name in plan.unit:
                eng.wait_ge(units_used, plan.unit[name] + 1)
            else:
                eng.wait_ge(full[b], plan.fills[name])
            return ps[b]

        def stored(eng, name):
            b, n = plan.at[name]
            eng.wait_ge(taken[b], n + 1)

        def took(ins, name):
            return ins.then_inc(taken[plan.at[name][0]], 1)

        block = ctx.enter_context(nc.Block())

        @block.sync
        def _(sp):
            sp.dma_start(vecs[:, :], T["vecs"]).then_inc(vectors_loaded, 16)
            def load(src, k):
                sp.dma_start(raw[k][:, :], src).then_inc(unit_loaded[k], 16)

            def tables(j):
                return 0 if j < 0 else NBLK if j == 23 else min(NBLK, BLOCKS_BEFORE[max(0, j - 3)] + 2)

            def segment(name, first, n):
                for j in range(n):
                    u = first + j
                    if u >= SLOTS:
                        sp.wait_ge(units_used, u - SLOTS + 1)
                    load(T[name][j], u % SLOTS)
                    if u == WO0 + 1:
                        for x in range(2):
                            for i in range(3):
                                stored(sp, ("aT", x, i))
                        for i in range(4):
                            fill_done(sp, ("av", i))
                        sp.dma_start(H[:, :, :], T["x"]).then_inc(x_loaded, 16)
                    if u == 0:
                        for x in range(4):
                            part = slice(512 * x, 512 * x + 512)
                            sp.dma_start(mem[:, :, part], T["mem"][:, :, part]).then_inc(mem_loaded[x], 16)
                    if u == 1:
                        sp.dma_start(H[:, :, :], T["x"]).then_inc(x_loaded, 16)
                    if ZERO_AT <= u < ZERO_AT + 32:
                        if u == ZERO_AT:
                            sp.wait_ge(zero_ready, 1)
                        for z in range(2):
                            sp.dma_start(gd_zero[2 * (u - ZERO_AT) + z], zero[:, :]).then_inc(gates_cleared, 16)
                    if name == "w_qkv":
                        for b in range(tables(j - 1), tables(j)):
                            sp.wait_ge(tables_stored[b // 4 % 2], 16 * (b // 8 + 1))
                            if b >= 4:
                                sp.wait_ge(block_turned, b - 3)
                            sp.dma_start(tab[b % 4][:, :, :], TABD[b // 4, :, :, b % 4]).then_inc(table_loaded[b % 4], 16)

            segment("w_mk", 0, 4)
            segment("w_mv", 4, 4)
            segment("w_u", UW0, 8)
            segment("w_qkv", QKV0, 24)
            segment("w_glu", GLU0, 4)
            segment("w_wo", WO0, 16)
            segment("w_xq", XQ0, 4)
            segment("w_xo", XO0, 4)
            sp.dma_start(keys[:, :, :], T["keys"]).then_inc(keys_loaded, 16)
            segment("w_pq", PQ0, 16)
            with sp.Fori(0, KEYS // 4) as i:
                for j in range(4):
                    sp.wait_ge(units_used, i * 4 + (U0 + j - SLOTS + 1))
                    load(T["u"][bass.ds(i * 4 + j, 1)].rearrange("a p n -> p (a n)"), j)
            sp.wait_ge(gates_added, 16 * NT * PH * TOPK)
            for g in range(2):
                sp.wait_ge(acts_stored[g], 16)
                sp.dma_start(As[:, g], ACTS[4 * g:4 * g + 4].rearrange("n p t -> p n t")).then_inc(slabs_loaded[g], 16)
                sp.dma_start(Gs[:, g], gd_slab[4 * g:4 * g + 4].rearrange("n p t -> p n t")).then_inc(slabs_loaded[g], 16)
            for j in range(8):
                sp.wait_ge(units_used, V0 + j - SLOTS + 1)
                load(T["v"][j], j % 4)
            for g in range(2):
                sp.wait_ge(acts_stored[g], 16 * (KEYS // 8))
            sp.dma_start(g_fin[:, :], T["g_fin"].to_broadcast([P, D])).then_inc(final_gain_loaded, 16)
            with sp.Fori(0, KEYS // 8 - 1) as i:
                for g in range(2):
                    sp.wait_ge(weights_multiplied, i * 2 + (g + 1))
                    n0 = i * 8 + (8 + 4 * g)
                    sp.dma_start(As[:, g], ACTS[bass.ds(n0, 4)].rearrange("n p t -> p n t")).then_inc(slabs_loaded[g], 16)
                    sp.dma_start(Gs[:, g], gd_slab[bass.ds(n0, 4)].rearrange("n p t -> p n t")).then_inc(slabs_loaded[g], 16)
                    for j in range(4):
                        sp.wait_ge(units_used, i * 8 + (V0 + 8 + 4 * g + j - SLOTS + 1))
                        load(T["v"][bass.ds(n0 + j, 1)].rearrange("a p n -> p (a n)"), j)
            for t in range(NT):
                for x in range(2):
                    sp.wait_ge(out_ready, 2 * t + x + 1)
                    half = slice(D // 2 * x, D // 2 * x + D // 2)
                    sp.dma_start(T["out"][t * P:(t + 1) * P, half], H[:, t, half]).then_inc(out_stored, 16)
            sp.wait_ge(out_stored, 16 * 2 * NT)

        @block.gpsimd
        def _(pool):
            G = nc.gpsimd
            G.memset(ident[:, :], 0.0).then_inc(constants_ready, 1)
            G.memset(maskd[:, :, :], 0.0).then_inc(constants_ready, 1)
            G.memset(zero[:, :], 0.0).then_inc(zero_ready, 1)
            pool.wait_ge(constants_ready, 2)
            G.affine_select(out=ident[:, :], in_=ident[:, :], compare_op=ALU.not_equal, fill=1.0,
                            base=0, pattern=[[-1, P]], channel_multiplier=1).then_inc(constants_ready, 1)
            G.affine_select(out=maskd[:, 1, :], in_=maskd[:, 1, :], compare_op=ALU.is_ge, fill=NEG,
                            base=0, pattern=[[-1, P]], channel_multiplier=1).then_inc(constants_ready, 1)
            G.iota(iota_t[:, :], [[1, S]], base=0, channel_multiplier=0,
                   allow_small_or_imprecise_dtypes=True).then_inc(constants_ready, 1)
            for j in range(8):
                G.memset(freq[:, j:j + 1], ROPE[j]).then_inc(constants_ready, 1)
            G.memset(eps[:, :], EPS).then_inc(constants_ready, 1)
            G.memset(magic[:, :], ROUND).then_inc(constants_ready, 1)
            G.memset(ones[:, :], 1.0).then_inc(constants_ready, 1)
            G.memset(one[:, :], 1.0).then_inc(constants_ready, 1)
            G.memset(quarter[:, :], PI_IN / 2).then_inc(constants_ready, 1)

            def rest(j, hi_count):
                pool.wait_ge(hi_ready, hi_count)
                G.tensor_tensor(lo[j][:, :], raw[j][:, :], hi[j][:, :].bitcast(F32), ALU.subtract).then_inc(rest_ready_pool, 1)

            for j in range(1, SLOTS):
                rest(j, j + 1)
            with pool.Fori(1, POOL_UNITS // SLOTS) as i:
                for j in range(SLOTS):
                    rest(j, i * SLOTS + (j + 1))
            pool.wait_ge(places_ready, NT)
            pool.wait_ge(gates_cleared, 16 * 64)
            for h in range(PH):
                if h:
                    pool.wait_ge(gates_added, 16 * NT * TOPK * h)
                for t in range(NT):
                    for r in range(TOPK):
                        G.indirect_dma_start(GD, bass.IndirectOffsetOnAxis(ap=eidx[:, t, h, r:r + 1], axis=0),
                                             gate[:, t, h, r:r + 1], None,
                                             compute_op=ALU.add).then_inc(gates_added, 16)

        @block.scalar
        def _(act):
            A = nc.scalar
            own = Chain(act, scalar_own)
            act.dma_start(prm[:, 0:3, :], T["ssm"]).then_inc(ssm_vectors_loaded, 16)
            act.dma_start(posi[:, :], T["pos"]).then_inc(ssm_vectors_loaded, 16)

            def gelu(j):
                act.wait_ge(y_ready, j + 1)
                A.activation(yT[:, j], yT[:, j], ACT.Gelu).then_inc(gelu_ready, 1)

            def glu_hi(j):
                act.wait_ge(gelu_ready, j + 1)
                A.activation(gTh[:, j], yT[:, j], ACT.Copy).then_inc(glu_hi_ready, 1)

            def split(u):
                act.wait_ge(unit_loaded[u % SLOTS], 16 * (u // SLOTS + 1))
                A.activation(hi[u % SLOTS][:, :], raw[u % SLOTS][:, :], ACT.Copy).then_inc(hi_ready, 1)

            def norm_stats(kk, X):
                for t in range(NT):
                    if t or kk:
                        act.wait_ge(squares_summed, NT * kk + t)
                    A.activation(junk[:, :], X[:, t], ACT.Square,
                                 accum_out=stat[:, 4 * (kk % 2) + t:4 * (kk % 2) + t + 1]).then_inc(squares_summed, 1)

            def norm_root(kk):
                act.wait_ge(mean_ready, kk + 1)
                A.activation(stat[:, 8:8 + NT], stat[:, 4 * (kk % 2) + 2:4 * (kk % 2) + 4],
                             ACT.Sqrt).then_inc(root_ready, 1)

            def norm_hi(kk, g, cps=range(8)):
                dst = (memh, XTh, XT2h, XT2h, XTh)[kk]
                for cp in cps:
                    b = fill_done(act, ("norm", kk, cp))
                    for c in range(2):
                        A.activation(dst[:, 2 * cp + c], b[:, 256 * c:256 * c + 256], ACT.Copy,
                                     scale=gains[:, g, 2 * cp + c:2 * cp + c + 1]).then_inc(hi_chunks, 1)

            def evac(name, dst, cols=slice(0, 256), scale=1.0, by=1):
                src = fill_done(act, name)[:, cols]
                if by > 1:
                    src = src.rearrange("p (x t) -> p x t", x=by)
                took(A.activation(dst, src, ACT.Copy, scale=scale), name)

            def table_group(g):
                act.wait_ge(phases_ready, g + 1)
                if g == 0:
                    act.wait_ge(units_used, 8)
                if g > 1:
                    act.wait_ge(tables_stored[g % 2], 16 * (g // 2))
                cos, sin, ph = tgrp[:, g % 2, 0], tgrp[:, g % 2, 1], phF[:, g % 2]
                A.activation(sin, ph, ACT.Sin, scale=2 * PI_IN).then_inc(sines_read, 1)
                A.activation(cos, ph, ACT.Abs).then_inc(sines_read, 1)
                act.wait_ge(sines_read, 2 * g + 2)
                own(A.activation(cos, cos, ACT.Sin, scale=-2 * PI_IN, bias=quarter[:, 0:1]))
                own.settle()
                act.dma_start(TABD[g], tgrp[:, g % 2]).then_inc(tables_stored[g % 2], 16)

            act.wait_ge(constants_ready, CST)
            act.wait_ge(vectors_loaded, 16)
            split(0)
            norm_hi(0, 0)
            split(1)
            for x in range(4):
                act.wait_ge(mem_loaded[x], 16)
            norm_stats(0, mem)
            norm_root(0)
            act.wait_ge(x_loaded, 16)
            split(2)
            act.dma_start(braw[:, :, :, :], T["bT"]).then_inc(b_c_loaded, 16)
            act.dma_start(craw[:, :, :, :], T["cT"]).then_inc(b_c_loaded, 16)
            split(3)
            split(4)
            norm_hi(1, 1)
            norm_stats(1, H)
            norm_root(1)
            act.wait_ge(ssm_vectors_loaded, 32)
            own(A.activation(prm[:, 3, :], prm[:, 2, :], ACT.Exp))
            act.wait_ge(params_vector, 1)
            own(A.activation(prm[:, 6, :], prm[:, 4, :], ACT.Exp))
            A.activation(lams[:, 2:4], lams[:, 0:2], ACT.Exp).then_inc(params_scalar, 1)
            split(5)
            act.wait_ge(params_vector, 2)
            own(A.activation(prm[:, 8, :], prm[:, 7, :], ACT.Sin))
            own(A.activation(prm[:, 9, :], prm[:, 7, :], ACT.Sin, scale=0.5))
            own(A.activation(rsin[:, :, :], rcos[:, :, :], ACT.Sin))
            own(A.activation(rcos[:, :, :], rcos[:, :, :], ACT.Sin, scale=0.5))
            own.settle()
            own(A.activation(prm[:, 9, :], prm[:, 9, :], ACT.Square, scale=math.sqrt(2.0)))
            own(A.activation(rcos[:, :, :], rcos[:, :, :], ACT.Square, scale=math.sqrt(2.0)))
            own.settle()
            A.activation(prm[:, 9, :], prm[:, 9, :], ACT.Identity, scale=-1.0, bias=one[:, 0:1]).then_inc(params_scalar, 1)
            A.activation(rcos[:, :, :], rcos[:, :, :], ACT.Identity, scale=-1.0, bias=one[:, 0:1]).then_inc(params_scalar, 1)

            def weights(u):
                split(u)
                if TABLES_AT <= u < TABLES_AT + GROUPS:
                    table_group(u - TABLES_AT)

            for u in range(6, 10):
                split(u)
            for t in range(2):
                evac(("mv", t), vx[:, t], slice(0, 512), scale=rstd[:, t:t + 1])
            for u in range(10, 19):
                weights(u)
            def attention_step(g, hf):
                x = g - HALF_AT[hf]
                if 0 <= x - QKT_AT - 1 < 4:
                    i = x - QKT_AT - 1
                    evac(("qkT", hf, i), qkT[:, i // 2, :, P * (i % 2):P * (i % 2) + P], slice(0, 512), by=4)
                if x in (EXP_AT, EXP_AT + 1):
                    k = x - EXP_AT
                    p, o = (p0, p1)[k], 16 * hf + 8 * k
                    act.wait_ge(maxima_ready, 2 * hf + k + 1)
                    for i in range(HEADS):
                        A.activation(p[:, i], p[:, i], ACT.Exp, bias=st_max[:, o + i:o + i + 1],
                                     accum_out=st_sum[:, o + i:o + i + 1]).then_inc(exps_ready, 1)
                if x in (COMB_AT, COMB_AT + 1):
                    k = x - COMB_AT
                    p, o = (p0, p1)[k], 16 * hf + 8 * k
                    act.wait_ge(factors_ready, 2 * hf + k + 1)
                    for h in range(4):
                        A.activation(p[:, 2 * h + 1], p[:, 2 * h + 1], ACT.Copy,
                                     scale=st_rec[:, o + 2 * h + 1:o + 2 * h + 2]).then_inc(second_scaled, 1)
                if 0 <= x - AT_AT - 1 < 3:
                    i = x - AT_AT - 1
                    if i == 0:
                        evac(("aT", hf, i), aT0[:, 4 * hf:4 * hf + 4], slice(0, 512), by=4)
                    else:
                        h = 4 * hf + 2 * (i - 1)
                        evac(("aT", hf, i), aT1[:, h:h + 2].rearrange("p h k t -> p (h k) t"), slice(0, 512), by=4)

            for n in range(24):
                for c in range(4):
                    if c == 2:
                        weights(QKV0 + n + 3)
                    for hf in range(2):
                        attention_step(4 * n + c, hf)
                    if c == 3:
                        for j in range(SSM_C - 1):
                            if n == GELU_AT[j]:
                                gelu(j)
                    if 4 * n + c in GLU_HI_AT:
                        glu_hi(GLU_HI_AT.index(4 * n + c))
                if n % 4 == 3:
                    cb = n // 4
                    for x in range(2):
                        act.wait_ge(tables_stored[x], 16 * GROUPS // 2)
                    for t in range(2):
                        dst = zqk[:, t, 512 * (cb % 2):512 * (cb % 2) + 512] if cb < 4 else \
                            vnat[:, t, 512 * (cb - 4):512 * (cb - 4) + 512]
                        evac(("qkv", cb, t), dst, slice(0, 512), scale=rstd[:, 2 + t:3 + t])

            gelu(SSM_C - 1)
            glu_hi(SSM_C - 1)
            for j in range(4):
                split(GLU0 + j + 3)
                for c in range(2):
                    b = fill_done(act, ("glu", 2 * j + c))
                    took(A.activation(sig[:, 2 * j + c], b[:, 0:256], ACT.Sigmoid,
                                      bias=glu_b[:, 2 * j + c:2 * j + c + 1]), ("glu", 2 * j + c))
                if j == 0:
                    for i in range(4):
                        b = fill_done(act, ("av", i))
                        for x in range(4):
                            if 4 * i + x:
                                act.wait_ge(head_squares, 4 * i + x)
                            A.activation(hjunk[:, :], b[:, P * x:P * x + P], ACT.Square,
                                         accum_out=head_ms[:, 4 * i + x:4 * i + x + 1]).then_inc(head_squares, 1)
                    act.wait_ge(head_mean_ready, 1)
                    A.activation(head_ms[:, :], head_ms[:, :], ACT.Sqrt).then_inc(head_root_ready, 1)
                if j == 2:
                    for i in range(4):
                        b = fill_done(act, ("oT", i))
                        A.activation(mixh[:, 2 * i:2 * i + 2], b[:, :].rearrange("p (h t) -> p h t", h=2), ACT.Copy,
                                     scale=g_att8[:, 0:1]).then_inc(hi_chunks, 1)
            for j in range(SSM_C):
                act.wait_ge(gated_ready, j + 1)
                A.activation(sqb[:, j], yT[:, j], ACT.Square).then_inc(mix_ready, 1)
            split(WO0 + 3)
            b = fill_done(act, ("ssq", 0))
            took(A.activation(sig[:, 0], b[:, 0:256], ACT.Sqrt, scale=1.0 / SSM_W, bias=eps[:, 0:1]), ("ssq", 0))
            for j in range(SSM_C):
                act.wait_ge(gated_ready, SSM_C + 1 + j)
                A.activation(mixh[:, SSM_C + j], yT[:, j], ACT.Copy).then_inc(hi_chunks, 1)
            for n in range(1, 16):
                split(WO0 + n + 3)
                if n == 10:
                    norm_hi(2, 2, range(4))
                if n == 14:
                    norm_hi(2, 2, (4, 5))

            norm_hi(2, 2, (6, 7))
            for cb in range(4):
                for t in range(NT):
                    stored(act, ("wo", cb, t))
            norm_stats(2, H)
            norm_root(2)
            def exps(h):
                act.wait_ge(cross_maxima_ready, h + 1)
                b = fill_done(act, ("xs", h))
                for t in range(NT):
                    i = 2 * h + t
                    ins = A.activation(px[:, t, h], b[:, S * t:S * t + S], ACT.Exp, bias=st_max[:, i:i + 1],
                                       scale=P ** -0.5, accum_out=st_sum[:, i:i + 1])
                    if t == 0:
                        own(ins)
                    else:
                        took(ins, ("xs", h))

            def probs_out(h):
                evac(("xp", h), pxT[:, h].rearrange("p k t -> p (k t)"), slice(0, 512))

            def output_hi(h):
                b = fill_done(act, ("xo", h))
                A.activation(oxh[:, h], b[:, 0:256], ACT.Copy).then_inc(hi_chunks, 1)

            split(XQ0 + 3)
            split(XO0)
            for heads in ((0, 1), (2, 3)):
                for h in heads:
                    exps(h)
                if heads[0] == 0:
                    split(XO0 + 1)
                    for h in heads:
                        probs_out(h)
            for heads in ((0, 1), (2, 3)):
                for h in heads:
                    output_hi(h)
                if heads[0] == 0:
                    for h in (2, 3):
                        probs_out(h)
            for u in range(XO0 + 2, XO0 + 5):
                split(u)
            norm_hi(3, 3, (0, 1))
            split(XO0 + 5)
            norm_hi(3, 3, (2, 3))
            split(XO0 + 6)
            norm_hi(3, 3, range(4, 8))

            for cb in range(4):
                for t in range(NT):
                    stored(act, ("xw", cb, t))
            norm_stats(3, H)
            norm_root(3)
            for c in range(16):
                split(PQ0 + c + 3)
                if c in NAT_AT:
                    norm_hi(4, 3, NAT_AT[c])
            for i in range(8):
                t, c = i // 4, 4 * (i % 4)
                b = fill_done(act, ("ps", i))
                took(A.activation(sc[:, t, c:c + 4], b[:, :].rearrange("p (c n) -> p c n", c=4), ACT.Copy), ("ps", i))

            def unit_gelu(i, jj, u_base):
                g, j = jj // 4, jj % 4
                act.wait_ge(unit_loaded[(jj + 3) % SLOTS], i * 32 + 16 * ((u_base + jj + 3) // SLOTS + 1))
                A.activation(hi[(jj + 3) % SLOTS][:, :], raw[(jj + 3) % SLOTS][:, :], ACT.Copy).then_inc(hi_ready, 1)
                if j == 0:
                    act.wait_ge(acts_stored[g], i * 16 + 16 * ((u_base - U0) // 8))
                act.wait_ge(units_used, i * 8 + (u_base + jj + 1))
                A.activation(gbuf[:, g, j], ps[j][:, 0:256], ACT.Gelu).then_inc(u_bank_free, 1)
                if j == 3:
                    act.wait_ge(u_bank_free, i * 8 + (u_base - U0 + jj + 1 + 4))
                    n0 = i * 8 + (u_base - U0 + 4 * g)
                    act.dma_start(ACTS[bass.ds(n0, 4)].rearrange("n p t -> p n t"), gbuf[:, g]).then_inc(acts_stored[g], 16)

            for n in range(UA):
                if n in PICKS_AT:
                    t = PICKS_AT.index(n)
                    act.wait_ge(picks_ready, t + 1)
                    A.activation(gate[:, t], gate[:, t], ACT.Exp).then_inc(pick_exps_ready, 1)
                unit_gelu(n // 8, n % 8, U0)
            with act.Fori(0, KEYS // 8 - 4) as i:
                for jj in range(8):
                    unit_gelu(i, jj, U0 + 32)
            for u in range(V0 + 3, V0 + 8):
                split(u)
            with act.Fori(0, KEYS // 8 - 1) as i:
                for j in range(8):
                    act.wait_ge(unit_loaded[j % SLOTS], i * 32 + 16 * ((V0 + 8 + j) // SLOTS + 1))
                    A.activation(hi[j % SLOTS][:, :], raw[j % SLOTS][:, :], ACT.Copy).then_inc(hi_ready, 1)
            for t in range(NT):
                for c in range(4):
                    act.wait_ge(output_added, 4 * t + c + 1)
                    A.activation(sqs[:, t, 512 * c:512 * c + 512], H[:, t, 512 * c:512 * c + 512], ACT.Square,
                                 accum_out=sums[:, t, c:c + 1]).then_inc(squares_summed, 1)
                act.wait_ge(mean_ready, 5 + t)
                A.activation(stat[:, 8 + t:9 + t], stat[:, 2 + t:3 + t], ACT.Sqrt).then_inc(root_ready, 1)

        @block.vector
        def _(dve):
            V = nc.vector
            own = Chain(dve, vector_own)

            def pr(n):
                return prm[:, n, :]

            def reduce_angle(x, kk, tmp):
                own(V.tensor_scalar(kk, x, 1.0 / TWO_PI, ROUND, ALU.mult, ALU.add))
                own.settle()
                own(V.tensor_scalar(kk, kk, -ROUND, None, ALU.add))
                own.settle()
                for c in (C1, C2, C3):
                    own(V.tensor_scalar(tmp, kk, -c, None, ALU.mult))
                    own.settle()
                    own(V.tensor_tensor(x, x, tmp, ALU.add))
                    own.settle()
                own(V.tensor_scalar(x, x, PI_IN, -PI_IN, ALU.min, ALU.max))
                own.settle()

            def ssm_weights():
                dve.wait_ge(b_c_loaded, 32)
                odd = ident[:, :].rearrange("p (q g h) -> p q g h", q=4, g=2)
                for g in range(2):
                    own(V.tensor_reduce(half_mask[:, g:g + 1], odd[:, :, g, :], AX.XY, ALU.add))
                own.settle()
                for c in range(2):
                    for g in range(2):
                        last = V.tensor_scalar(BW[:, c, :, 64 * g:64 * g + 64], braw[:, c], half_mask[:, g:g + 1],
                                               None, ALU.mult)
                        own(last)
                dve.wait_ge(params_scalar, 3)
                own(V.tensor_tensor(pr(13), pr(6), pr(9), ALU.mult))
                own(V.tensor_tensor(pr(14), pr(6), pr(8), ALU.mult))
                own(V.tensor_tensor(pr(15), pr(0), pr(0), ALU.mult))
                own(V.tensor_tensor(pr(16), pr(1), pr(1), ALU.mult))
                own.settle()
                own(V.tensor_tensor(pr(15), pr(15), pr(16), ALU.add))
                own(V.tensor_scalar(pr(13), pr(13), -1.0, None, ALU.add))
                own.settle()
                own(V.reciprocal(pr(15), pr(15)))
                own(V.tensor_tensor(pr(16), pr(13), pr(0), ALU.mult))
                own(V.tensor_tensor(pr(17), pr(14), pr(1), ALU.mult))
                own(V.tensor_tensor(pr(18), pr(14), pr(0), ALU.mult))
                own(V.tensor_tensor(pr(19), pr(13), pr(1), ALU.mult))
                own.settle()
                own(V.tensor_tensor(pr(16), pr(16), pr(17), ALU.add))
                own(V.tensor_tensor(pr(18), pr(18), pr(19), ALU.subtract))
                own.settle()
                own(V.tensor_tensor(pr(16), pr(16), pr(15), ALU.mult))
                own(V.tensor_tensor(pr(18), pr(18), pr(15), ALU.mult))
                own(V.memset(CW[:, :, :, :], 0.0))
                own.settle()
                fre = pr(16).unsqueeze(2).to_broadcast([P, NBLK, 16])
                fim = pr(18).unsqueeze(2).to_broadcast([P, NBLK, 16])
                own(V.tensor_tensor(ctmp[:, 0], craw[:, 0], fre, ALU.mult))
                own(V.tensor_tensor(ctmp[:, 1], craw[:, 1], fim, ALU.mult))
                own.settle()
                for g in range(2):
                    r = slice(64 * g, 64 * g + 64)
                    own(V.tensor_tensor(CW[r, :, 0, 16 * g:16 * g + 16], ctmp[r, 0], ctmp[r, 1], ALU.subtract))
                own.settle()
                own(V.scalar_tensor_tensor(ctmp[:, 0], craw[:, 0], -1.0, fim, ALU.mult, ALU.mult))
                own(V.tensor_tensor(ctmp[:, 1], craw[:, 1], fre, ALU.mult))
                own.settle()
                for g in range(2):
                    r = slice(64 * g, 64 * g + 64)
                    V.tensor_tensor(CW[r, :, 1, 16 * g:16 * g + 16], ctmp[r, 0], ctmp[r, 1],
                                    ALU.subtract).then_inc(ssm_glu_inputs, 1)

            def norm_rstd(kk):
                o = 4 * (kk % 2)
                dve.wait_ge(squares_summed, NT * (kk + 1))
                V.tensor_scalar(stat[:, o + 2:o + 4], stat[:, o:o + 2], 1.0 / D, EPS, ALU.mult,
                                ALU.add).then_inc(mean_ready, 1)
                dve.wait_ge(root_ready, kk + 1)
                own(V.reciprocal(rstd[:, 2 * kk:2 * kk + 2], stat[:, 8:10]))
                own.settle()

            def norm_diag(kk):
                norm_rstd(kk)
                for t in range(NT):
                    V.tensor_scalar(diag[:, t], ident[:, :], rstd[:, 2 * kk + t:2 * kk + t + 1], None,
                                    ALU.mult).then_inc(diagonal_ready, 1)

            def norm_spread(kk):
                took(V.tensor_copy(Rb[:, :], fill_done(dve, ("rb", kk))[:, 0:256]), ("rb", kk))
                stored(dve, ("rb", kk))

            def evac(name, dst):
                took(V.tensor_tensor(dst, fill_done(dve, name)[:, 0:256], Rb[:, :], ALU.mult), name)

            def norm_lo(kk, g, hc0, cps=range(8)):
                dh, dl = ((memh, meml), (XTh, XTl), (XT2h, XT2l), (XT2h, XT2l), (XTh, XTl))[kk]
                for cp in cps:
                    dve.wait_ge(hi_chunks, hc0 + 2 * cp + 2)
                    for c in range(2):
                        ins = V.scalar_tensor_tensor(dl[:, 2 * cp + c], fill_done(dve, ("norm", kk, cp))[:, 256 * c:256 * c + 256],
                                                     gains[:, g, 2 * cp + c:2 * cp + c + 1],
                                                     dh[:, 2 * cp + c].bitcast(F32), ALU.mult, ALU.subtract)
                        if c == 0:
                            own(ins)
                        else:
                            took(ins, ("norm", kk, cp))

            def phases(g):
                if g == 0:
                    dve.wait_ge(ssm_glu_inputs, 2)
                if g > 1:
                    dve.wait_ge(sines_read, 2 * g - 2)
                blocks = [(x, 4 * g + x) for x in range(4)]
                for x, b in blocks:
                    own(V.tensor_scalar(phR[:, x], iota_t[:, :], prm[:, 10, b:b + 1], ROUND, ALU.mult, ALU.add))
                for x, b in blocks:
                    own(V.tensor_scalar(phA[:, x], iota_t[:, :], prm[:, 11, b:b + 1], None, ALU.mult))
                own.settle()
                for x, b in blocks:
                    own(V.scalar_tensor_tensor(phR[:, x], phR[:, x], ROUND, phA[:, x], ALU.subtract, ALU.subtract))
                own.settle()
                for x, b in blocks:
                    own(V.scalar_tensor_tensor(phF[:, g % 2, x], iota_t[:, :], prm[:, 12, b:b + 1], phR[:, x],
                                               ALU.mult, ALU.subtract))
                own.settle()
                V.tensor_scalar(phF[:, g % 2], phF[:, g % 2], 0.5, -0.5, ALU.min, ALU.max).then_inc(phases_ready, 1)

            dve.wait_ge(hi_ready, 1)
            V.tensor_tensor(lo[0][:, :], raw[0][:, :], hi[0][:, :].bitcast(F32), ALU.subtract).then_inc(rest_ready_first, 1)
            norm_lo(0, 0, 0)
            norm_diag(0)
            norm_spread(0)
            for j in range(2):
                evac(("mk", j), kxT[:, j])
            norm_lo(1, 1, 16)
            norm_diag(1)
            dve.wait_ge(ssm_vectors_loaded, 32)
            dve.wait_ge(scalar_own, 1)
            own(V.tensor_tensor(pr(4), pr(0), pr(3), ALU.mult))
            own(V.tensor_tensor(pr(5), pr(1), pr(3), ALU.mult))
            own(V.tensor_tensor_reduce(lamv[:, 0], lamv[:, 0], lamv[:, 1], 1.0, 0.0, ALU.mult, ALU.add, lams[:, 0:1]))
            own(V.tensor_tensor_reduce(lamv[:, 2], lamv[:, 2], lamv[:, 3], 1.0, 0.0, ALU.mult, ALU.add, lams[:, 1:2]))
            own.settle()
            V.tensor_copy(posf[:, :], posi[:, :]).then_inc(params_vector, 1)
            dve.wait_ge(params_vector, 1)
            dve.wait_ge(constants_ready, CST)

            for j in range(2, 4):
                evac(("mk", j), kxT[:, j])
            own(V.tensor_copy(pr(7), pr(5)))
            for t in range(NT):
                own(V.tensor_scalar(rcos[:, t], freq[:, :], posf[:, t:t + 1], None, ALU.mult))
            own.settle()
            rc = rcos[:, :, :].rearrange("p t j -> p (t j)")
            rs = rsin[:, :, :].rearrange("p t j -> p (t j)")
            reduce_angle(rc, rs, pr(18)[:, 0:16])
            reduce_angle(pr(7), pr(18), pr(19))
            dve.wait_ge(params_scalar, 1)
            own(V.tensor_tensor(lams[:, 4:5], lams[:, 3:4], lams[:, 2:3], ALU.subtract))
            V.tensor_scalar(g_att8[:, :], g_att[:, :], 1.0 - LAM_INIT, None, ALU.mult).then_inc(params_vector, 1)
            own.settle()
            own(V.tensor_scalar(lams[:, 5:6], lams[:, 4:5], -LAM_INIT, None, ALU.add))
            own(V.tensor_scalar(pr(10), pr(7), 1.0 / TWO_PI, None, ALU.mult))
            own.settle()
            own(V.tensor_scalar(pr(11), pr(10), ROUND15, None, ALU.add))
            own.settle()
            own(V.tensor_scalar(pr(11), pr(11), -ROUND15, None, ALU.add))
            own.settle()
            V.tensor_tensor(pr(12), pr(10), pr(11), ALU.subtract).then_inc(params_vector, 1)
            norm_spread(1)
            ssm_weights()
            phases(0)
            for j in range(8):
                if j < 7:
                    phases(1 + j)
                evac(("uw", j), uT[:, j])

            def turn_back(b):
                bank = fill_done(dve, ("bu", b))[:, :].rearrange("p (c t) -> p c t", c=2)
                dve.wait_ge(table_loaded[b % 4], 16 * (b // 4 + 1))
                if b:
                    dve.wait_ge(block_turned, b)
                cos = tab[b % 4][:, 0:1].to_broadcast([P, 2, S])
                sin = tab[b % 4][:, 1:2].to_broadcast([P, 2, S])
                own(V.tensor_tensor(m1[:, :, :], bank, cos, ALU.mult))
                took(V.tensor_tensor(m2[:, :, :], bank, sin, ALU.mult), ("bu", b))

            def scan(b):
                own.settle()
                stored(dve, ("bu", b))
                re_in = own(V.tensor_tensor(m1[:, 0], m1[:, 0], m2[:, 1], ALU.add))
                im_in = own(V.tensor_tensor(m1[:, 1], m1[:, 1], m2[:, 0], ALU.subtract))
                r = prm[:, 6, b:b + 1].to_broadcast([P, S])
                for c, n in ((0, re_in), (1, im_in)):
                    dve.wait_ge(vector_own, n)
                    own(V.tensor_tensor_scan(m1[:, c], r, m1[:, c], 0.0, ALU.mult, ALU.add))
                own.settle()
                if b >= 2:
                    dve.wait_ge(outputs_ready, b - 1)
                if b:
                    dve.wait_ge(states_ready, 2 * b)
                cos = tab[b % 4][:, 0:1].to_broadcast([P, 2, S])
                sin = tab[b % 4][:, 1:2].to_broadcast([P, 2, S])
                own(V.tensor_tensor(xst[:, b % 2], m1[:, :, :], cos, ALU.mult))
                V.tensor_tensor(dem[:, :, :], m1[:, :, :], sin, ALU.mult).then_inc(block_turned, 1)

            def states(b):
                x = xst[:, b % 2]
                own.settle()
                dve.wait_ge(block_turned, b + 1)
                V.tensor_tensor(x[:, 0], x[:, 0], dem[:, 1], ALU.subtract).then_inc(states_ready, 1)
                V.tensor_tensor(x[:, 1], x[:, 1], dem[:, 0], ALU.add).then_inc(states_ready, 1)

            def y_out(j):
                dve.wait_ge(outputs_ready, 4 * j + 4)
                V.scalar_tensor_tensor(yT[:, j], uT[:, j], d_skip[:, j:j + 1], ps[6 + j % 2][:, 0:256],
                                       ALU.mult, ALU.add).then_inc(y_ready, 1)

            def slot(s):
                turn_back(s)
                if s:
                    states(s - 1)
                scan(s)
                if s % 4 == 2 and s >= 6:
                    y_out(s // 4 - 1)

            def rope(hf, t):
                z = zqk[:, t].rearrange("p (h d) -> p h d", d=QK)
                r1, r2 = z[:, :, 0:8], z[:, :, 8:16]
                c = rcos[:, t:t + 1].to_broadcast([P, 16, 8])
                s = rsin[:, t:t + 1].to_broadcast([P, 16, 8])
                a = m1[:, :, :].rearrange("p a (b h d) -> p (a b) h d", b=2, d=8)
                if t or hf:
                    dve.wait_ge(half_rotated, 2 * (2 * hf + t))
                own(V.tensor_tensor(a[:, 0], r1, c, ALU.mult))
                own(V.tensor_tensor(a[:, 1], r2, s, ALU.mult))
                own(V.tensor_tensor(a[:, 2], r1, s, ALU.mult))
                own(V.tensor_tensor(a[:, 3], r2, c, ALU.mult))
                own.settle()
                V.tensor_tensor(r1, a[:, 0], a[:, 1], ALU.subtract).then_inc(half_rotated, 1)
                V.tensor_tensor(r2, a[:, 2], a[:, 3], ALU.add).then_inc(half_rotated, 1)

            def glu_lo(j):
                dve.wait_ge(glu_hi_ready, j + 1)
                V.tensor_tensor(gTl[:, j], yT[:, j], gTh[:, j].bitcast(F32), ALU.subtract).then_inc(ssm_glu_inputs, 1)

            def combine(hf, k):
                p, o = (p0, p1)[k], 16 * hf + 8 * k
                dve.wait_ge(exps_ready, o + 8)
                own(V.reciprocal(st_rec[:, o:o + 8], st_sum[:, o:o + 8]))
                own.settle()
                V.tensor_scalar(st_rec[:, o + 1:o + 8:2], st_rec[:, o + 1:o + 8:2], lams[:, 5:6], None,
                                ALU.mult).then_inc(factors_ready, 1)

            def difference(hf, k):
                p, o = (p0, p1)[k], 16 * hf + 8 * k
                dve.wait_ge(second_scaled, o // 2 + 4)
                for h in range(4):
                    V.scalar_tensor_tensor(p[:, 2 * h], p[:, 2 * h], st_rec[:, o + 2 * h:o + 2 * h + 1],
                                           p[:, 2 * h + 1], ALU.mult, ALU.add).then_inc(differences_ready, 1)

            def attention_step(g, hf):
                x = g - HALF_AT[hf]
                if x == ROPE_AT:
                    dve.wait_ge(block_turned, -(-g // BLOCK_EVERY))
                    for t in range(NT):
                        for kq in range(2):
                            stored(dve, ("qkv", 2 * hf + kq, t))
                        rope(hf, t)
                    dve.wait_ge(half_rotated, 4 * hf + 4)
                if 0 <= x - S0_AT - 1 < 2:
                    i = x - S0_AT - 1
                    if hf and i == 0:
                        for j in range(3):
                            fill_done(dve, ("aT", 0, j))
                    b = fill_done(dve, ("s0", hf, i))
                    took(V.scalar_tensor_tensor(p0[:, i:i + 7:2], b[:, :].rearrange("p (c n) -> p c n", c=4), QK ** -0.5,
                                                maskd[:, 1:2].to_broadcast([P, 4, P]), ALU.mult, ALU.add), ("s0", hf, i))
                if 0 <= x - S1_AT - 1 < 4:
                    i = x - S1_AT - 1
                    b = fill_done(dve, ("s1", hf, i))
                    o = 4 * (i // 2) + i % 2
                    took(V.scalar_tensor_tensor(p1[:, o:o + 3:2], b[:, :].rearrange("p (c n) -> p c n", c=2), QK ** -0.5,
                                                maskd[:, :, :].rearrange("p a n -> p (a n)").unsqueeze(1).to_broadcast([P, 2, S]),
                                                ALU.mult, ALU.add), ("s1", hf, i))
                if x == MAX_AT:
                    for i in range(2, 4):
                        stored(dve, ("s1", hf, i))
                    o = 16 * hf
                    own(V.tensor_reduce(st_max[:, o:o + 8], p0[:, :, :], AX.X, ALU.max))
                    own(V.tensor_reduce(st_max[:, o + 8:o + 16], p1[:, :, :], AX.X, ALU.max))
                    own.settle()
                    for k in range(2):
                        V.tensor_scalar(st_max[:, o + 8 * k:o + 8 * k + 8], st_max[:, o + 8 * k:o + 8 * k + 8], -1.0,
                                        None, ALU.mult).then_inc(maxima_ready, 1)
                if x in (COMB_AT, COMB_AT + 1):
                    combine(hf, x - COMB_AT)
                if x in (COMB_AT + 1, COMB_AT + 2):
                    difference(hf, x - COMB_AT - 1)

            for g in range(STEPS):
                for hf in range(2):
                    attention_step(g, hf)
                if g % BLOCK_EVERY == 0:
                    slot(g // BLOCK_EVERY)
                if g in GLU_LO_AT:
                    glu_lo(GLU_LO_AT.index(g))
            states(NBLK - 1)
            y_out(7)

            for j in range(len(GLU_LO_AT), SSM_C):
                glu_lo(j)
            dve.wait_ge(head_squares, 16)
            V.tensor_scalar(head_ms[:, :], head_ms[:, :], 1.0 / P, EPS, ALU.mult, ALU.add).then_inc(head_mean_ready, 1)
            dve.wait_ge(head_root_ready, 1)
            own(V.reciprocal(head_ms[:, :], head_ms[:, :]))
            own.settle()
            for i in range(4):
                t, hf = i // 2, i % 2
                b = fill_done(dve, ("av", i))
                took(V.tensor_tensor(att_n[:, t, 512 * hf:512 * hf + 512].rearrange("p (h e) -> p h e", h=4),
                                     b[:, :].rearrange("p (h e) -> p h e", h=4),
                                     head_ms[:, 4 * i:4 * i + 4].unsqueeze(2).to_broadcast([P, 4, P]), ALU.mult), ("av", i))

            def gated(j):
                stored(dve, ("glu", j))
                V.tensor_tensor(yT[:, j], yT[:, j], sig[:, j], ALU.mult).then_inc(gated_ready, 1)

            for j in range(6):
                gated(j)
            for i in range(4):
                dve.wait_ge(hi_chunks, 32 + i + 1)
                b = fill_done(dve, ("oT", i))
                took(V.scalar_tensor_tensor(mixl[:, 2 * i:2 * i + 2], b[:, :].rearrange("p (h t) -> p h t", h=2),
                                            g_att8[:, 0:1], mixh[:, 2 * i:2 * i + 2].bitcast(F32),
                                            ALU.mult, ALU.subtract), ("oT", i))
            for j in range(6, SSM_C):
                gated(j)

            stored(dve, ("ssq", 0))
            own(V.reciprocal(sig[:, 0], sig[:, 0]))
            own.settle()
            for j in range(SSM_C):
                V.scalar_tensor_tensor(yT[:, j], yT[:, j], g_ssm[:, j:j + 1], sig[:, 0], ALU.mult,
                                       ALU.mult).then_inc(gated_ready, 1)
            for j in range(SSM_C):
                dve.wait_ge(hi_chunks, 36 + j + 1)
                V.tensor_tensor(mixl[:, SSM_C + j], yT[:, j], mixh[:, SSM_C + j].bitcast(F32),
                                ALU.subtract).then_inc(mix_ready, 1)

            def residual(name, cb, t):
                b = fill_done(dve, (name, cb, t))
                took(V.tensor_tensor(H[:, t, 512 * cb:512 * cb + 512], b[:, :], H[:, t, 512 * cb:512 * cb + 512],
                                     ALU.add), (name, cb, t))

            dve.wait_ge(x_loaded, 32)
            for cb in range(4):
                for t in range(NT):
                    residual("wo", cb, t)
                if cb in (1, 2):
                    norm_lo(2, 2, 44, range(4) if cb == 1 else (4, 5))
            norm_lo(2, 2, 44, (6, 7))
            norm_diag(2)
            norm_spread(2)

            def head_max(h):
                b = fill_done(dve, ("xs", h))
                own(V.tensor_reduce(st_max[:, 2 * h:2 * h + 2], b[:, :].rearrange("p (t m) -> p t m", t=NT), AX.X, ALU.max))
                own.settle()
                V.tensor_scalar(st_max[:, 2 * h:2 * h + 2], st_max[:, 2 * h:2 * h + 2], -P ** -0.5, None,
                                ALU.mult).then_inc(cross_maxima_ready, 1)

            def head_norm(h):
                stored(dve, ("xs", h))
                own(V.reciprocal(st_rec[:, 2 * h:2 * h + 2], st_sum[:, 2 * h:2 * h + 2]))
                own.settle()
                for t in range(NT):
                    V.tensor_scalar(px[:, t, h], px[:, t, h], st_rec[:, 2 * h + t:2 * h + t + 1], None,
                                    ALU.mult).then_inc(cross_probs_ready, 1)

            for j in range(3):
                evac(("xq", j), qxT[:, j])
            for h in (0, 1):
                head_max(h)
            evac(("xq", 3), qxT[:, 3])
            for h in (0, 1):
                head_norm(h)
            for h in (2, 3):
                head_max(h)
            for h in (2, 3):
                head_norm(h)
            for h in range(XH):
                dve.wait_ge(hi_chunks, 60 + h + 1)
                b = fill_done(dve, ("xo", h))
                took(V.tensor_tensor(oxl[:, h], b[:, 0:256], oxh[:, h].bitcast(F32), ALU.subtract), ("xo", h))
            for cb in range(4):
                for t in range(NT):
                    residual("xw", cb, t)
                if cb:
                    norm_lo(3, 3, 64, (2 * cb - 2, 2 * cb - 1))
            norm_lo(3, 3, 64, (6, 7))
            V.memset(zr[:, :].bitcast(F32), 0.0).then_inc(zeros_ready, 1)
            norm_diag(3)
            norm_spread(3)
            for c in range(16):
                evac(("pq", c), qP[:, c])
                if c == 1:
                    for t in range(NT):
                        V.tensor_scalar(nat[:, t], H[:, t], rstd[:, 6 + t:7 + t], None, ALU.mult).then_inc(rows_normalised, 1)
                if c in NAT_AT:
                    norm_lo(4, 3, 80, NAT_AT[c])

            own(V.tensor_copy(io16[:, :], iota_t[:, 0:TOPK]))
            own(V.tensor_tensor_reduce(repl[:, 0:P], ident[:, :], iota_t[:, 0:P], 1.0, 0.0, ALU.mult, ALU.add,
                                       tokf[:, 0:1]))
            own.settle()
            own(V.tensor_scalar(tokf[:, 1:2], tokf[:, 0:1], float(P), None, ALU.add))

            def top16(vals, idx, x):
                n = x.shape[1]
                own(V.max(vals[:, 0:8], x))
                own.settle()
                own(V.max_index(idx[:, 0:8], vals[:, 0:8], x))
                own(V.match_replace(repl[:, 0:n], vals[:, 0:8], x, -3e38))
                own.settle()
                own(V.max(vals[:, 8:16], repl[:, 0:n]))
                own.settle()
                own(V.max_index(idx[:, 8:16], vals[:, 8:16], repl[:, 0:n]))

            for t in range(NT):
                for i in range(8):
                    stored(dve, ("ps", i))
                for c in range(2 * PH):
                    top16(tv[:, c], ti[:, c], sc[:, t, c])
                own.settle()
                own(V.tensor_copy(tif[:, :, :], ti[:, :, :]))
                tv4 = tv[:, :, :].rearrange("p (h s) a -> p h s a", s=2)
                own(V.tensor_tensor(cand[:, :, :, :], tv4[:, :, 0].unsqueeze(3).to_broadcast([P, PH, TOPK, TOPK]),
                                    tv4[:, :, 1].unsqueeze(2).to_broadcast([P, PH, TOPK, TOPK]), ALU.add))
                own.settle()
                for h in range(PH):
                    top16(ts[:, h], ic[:, h], cand[:, h].rearrange("p a b -> p (a b)"))
                own.settle()
                own(V.tensor_tensor(gate[:, t], ts[:, :, :], ts[:, :, 0:1].to_broadcast([P, PH, TOPK]), ALU.subtract))
                own(V.tensor_single_scalar(icx[:, 0], ic[:, :, :], 4, ALU.logical_shift_right))
                own(V.tensor_single_scalar(icx[:, 1], ic[:, :, :], 15, ALU.bitwise_and))
                own.settle()
                V.tensor_copy(icf[:, :, :, :], icx[:, :, :, :]).then_inc(picks_ready, 1)
                dve.wait_ge(picks_ready, t + 1)
                tif4 = tif[:, :, :].rearrange("p (h s) a -> p h s a", s=2)
                for x in range(2):
                    own(V.tensor_tensor(eq[:, :, :, :], icf[:, x].unsqueeze(3).to_broadcast([P, PH, TOPK, TOPK]),
                                        io16[:, :].unsqueeze(1).unsqueeze(1).to_broadcast([P, PH, TOPK, TOPK]), ALU.is_equal))
                    own.settle()
                    own(V.tensor_tensor(eqv[:, :, :, :], eq[:, :, :, :],
                                        tif4[:, :, x].unsqueeze(2).to_broadcast([P, PH, TOPK, TOPK]), ALU.mult))
                    own.settle()
                    own(V.tensor_reduce(ef[:, x], eqv[:, :, :, :], AX.X, ALU.add))
                own.settle()
                own(V.scalar_tensor_tensor(ei[:, :, :], ef[:, 1], float(KEYS), ef[:, 0], ALU.mult, ALU.add))
                own.settle()
                own(V.tensor_scalar(ei[:, :, :], ei[:, :, :], float(S), tokf[:, t:t + 1], ALU.mult, ALU.add))
                dve.wait_ge(pick_exps_ready, t + 1)
                own(V.tensor_reduce(g1[:, :], gate[:, t], AX.X, ALU.add))
                own.settle()
                own(V.reciprocal(g2[:, :], g1[:, :]))
                own.settle()
                own(V.tensor_tensor(gate[:, t], gate[:, t], g2[:, :].unsqueeze(2).to_broadcast([P, PH, TOPK]), ALU.mult))
                own.settle()
                V.tensor_copy(eidx[:, t], ei[:, :, :]).then_inc(places_ready, 1)

            def rest(i, j, base_hi, per):
                dve.wait_ge(hi_ready, i * per + (base_hi + j + 1))
                V.tensor_tensor(lo[j % SLOTS][:, :], raw[j % SLOTS][:, :], hi[j % SLOTS][:, :].bitcast(F32),
                                ALU.subtract).then_inc(rest_ready_vector, 1)

            with dve.Fori(0, (KEYS - UA) // 4) as i:
                for j in range(4):
                    rest(i, j, POOL_UNITS, 4)
            with dve.Fori(0, KEYS // 8) as i:
                for g in range(2):
                    dve.wait_ge(slabs_loaded[g], i * 32 + 32)
                    dve.wait_ge(units_used, i * 8 + (V0 + 4 * g - 4))
                    dve.wait_ge(weight_parts_ready, i * 4 + 2 * g)
                    V.tensor_tensor(Wf[:, :, :], As[:, g], Gs[:, g], ALU.mult).then_inc(weights_multiplied, 1)
                    dve.wait_ge(weights_multiplied, i * 2 + (g + 1))
                    V.tensor_copy(Wh[:, g], Wf[:, :, :]).then_inc(weight_parts_ready, 1)
                    dve.wait_ge(weight_parts_ready, i * 4 + (2 * g + 1))
                    V.tensor_tensor(Wl[:, g], Wf[:, :, :], Wh[:, g].bitcast(F32), ALU.subtract).then_inc(weight_parts_ready, 1)
                    for j in range(4):
                        rest(i, 4 * g + j, V0, 8)
            dve.wait_ge(final_gain_loaded, 16)
            dve.wait_ge(units_used, END)

            def add(t):
                for c in range(4):
                    V.tensor_tensor(H[:, t, 512 * c:512 * c + 512], ps[4 * t + c][:, :],
                                    H[:, t, 512 * c:512 * c + 512], ALU.add).then_inc(output_added, 1)

            def mean(t):
                dve.wait_ge(squares_summed, 2 * 4 + 4 * (t + 1))
                own(V.tensor_reduce(stat[:, t:t + 1], sums[:, t], AX.X, ALU.add))
                own.settle()
                V.tensor_scalar(stat[:, 2 + t:3 + t], stat[:, t:t + 1], 1.0 / D, EPS, ALU.mult, ALU.add).then_inc(mean_ready, 1)

            def out(t):
                dve.wait_ge(root_ready, 5 + t)
                own(V.reciprocal(stat[:, 12 + t:13 + t], stat[:, 8 + t:9 + t]))
                own.settle()
                dve.wait_ge(output_added, 4 * (t + 1))
                for x in range(2):
                    half = slice(D // 2 * x, D // 2 * x + D // 2)
                    V.scalar_tensor_tensor(H[:, t, half], H[:, t, half], stat[:, 12 + t:13 + t], g_fin[:, half], ALU.mult,
                                           ALU.mult).then_inc(out_ready, 1)

            add(0)
            add(1)
            mean(0)
            out(0)
            mean(1)
            out(1)

        @block.tensor
        def _(pe):
            M = nc.tensor

            def bank(name):
                b, n = plan.at[name]
                if n:
                    pe.wait_ge(taken[b], n)
                return ps[b]

            def filled(ins, name):
                ins.then_inc(full[plan.at[name][0]], 1)

            def used(ins):
                ins.then_inc(units_used, 1)

            def unit(u):
                if u == 0:
                    pe.wait_ge(rest_ready_first, 1)
                else:
                    pe.wait_ge(rest_ready_pool, u)

            def three(out, wh, wl, xh, xl, start, stop):
                M.matmul(out, wh, xh, start=start, stop=False)
                M.matmul(out, wh, xl, start=False, stop=False)
                return M.matmul(out, wl, xh, start=False, stop=stop)

            def norm(kk, src, cps=range(8)):
                for cp in cps:
                    b = bank(("norm", kk, cp))
                    for c in range(2):
                        for t in range(NT):
                            ins = M.transpose(b[:, 256 * c + P * t:256 * c + P * t + P],
                                              src[:, t, P * (2 * cp + c):P * (2 * cp + c) + P], ident[:, :])
                    filled(ins, ("norm", kk, cp))

            def spread(kk):
                b = bank(("rb", kk))
                pe.wait_ge(diagonal_ready, NT * (kk + 1))
                filled(M.matmul(b[:, 0:256], ones[:, :], diag[:, :, :].rearrange("p t n -> p (t n)"),
                                start=True, stop=True), ("rb", kk))

            def cols_unit(name, u, xh=XTh, xl=XTl, ready=None):
                b = bank(name)
                unit(u)
                s = u % SLOTS
                for c in range(DC):
                    if ready is not None and c % 2 == 0:
                        stored(pe, ("norm", ready, c // 2))
                    ins = three(b[:, 0:256], hi[s][:, P * c:P * c + P], lo[s][:, P * c:P * c + P],
                                xh[:, c], xl[:, c], c == 0, c == DC - 1)
                ins.then_inc(units_used, 1)

            def rows_unit(name, u, q, n, xh, xl, step=None, ready=False):
                if q == 0:
                    b = [bank((*name, t)) for t in range(NT)]
                else:
                    b = [ps[plan.at[(*name, t)][0]] for t in range(NT)]
                unit(u)
                s = u % SLOTS
                for c in range(4):
                    if ready:
                        stored(pe, ("xo", c))
                    for t in range(NT):
                        k = 4 * q + c
                        x_h, x_l = xh[:, k, P * t:P * t + P], xl[:, k, P * t:P * t + P]
                        w_h, w_l = hi[s][:, 512 * c:512 * c + 512], lo[s][:, 512 * c:512 * c + 512]
                        M.matmul(b[t][:, :], x_h, w_h, start=k == 0, stop=False)
                        M.matmul(b[t][:, :], x_h, w_l, start=False, stop=False)
                        ins = M.matmul(b[t][:, :], x_l, w_h, start=False, stop=k == 4 * n - 1)
                    if c == 3:
                        used(ins)
                    if step:
                        step(4 * q + c)

            def rows_block(name, u0, n, xh, xl, step=None):
                for q in range(n):
                    rows_unit(name, u0 + q, q, n, xh, xl, step)

            pe.wait_ge(constants_ready, CST)
            for x in range(4):
                pe.wait_ge(mem_loaded[x], 16)
                norm(0, mem, (2 * x, 2 * x + 1))
            for j in range(4):
                cols_unit(("mk", j), j, memh, meml, 0 if j == 0 else None)
                if j == 1:
                    spread(0)
                    pe.wait_ge(x_loaded, 16)
                    norm(1, H)
            spread(1)
            rows_block(("mv",), 4, 4, memh, meml)
            for cp in range(8):
                stored(pe, ("norm", 1, cp))
            for j in range(8):
                cols_unit(("uw", j), UW0 + j)
            pe.wait_ge(ssm_glu_inputs, 2)

            def bu(b):
                if b >= NBLK:
                    return
                j, q = b // 4, b % 4
                r = slice(32 * q, 32 * q + 32)
                out = bank(("bu", b))
                if q == 0:
                    stored(pe, ("uw", j))
                for c in range(2):
                    ins = M.matmul(out[:, 256 * c:256 * c + 256], BW[r, c, j], uT[r, j], start=True, stop=True,
                                   skip_group_check=True)
                filled(ins, ("bu", b))

            def y(b):
                if b < 0:
                    return
                j, q = b // 4, b % 4
                if q == 0 and j >= 2:
                    pe.wait_ge(y_ready, j - 1)
                pe.wait_ge(states_ready, 2 * b + 2)
                out = ps[6 + j % 2][32 * q:32 * q + 32, 0:256]
                M.matmul(out, CW[:, b, 0], xst[:, b % 2, 0], start=True, stop=False, skip_group_check=True)
                M.matmul(out, CW[:, b, 1], xst[:, b % 2, 1], start=False, stop=True,
                         skip_group_check=True).then_inc(outputs_ready, 1)

            def slot(s):
                bu(s)
                y(s - 2)

            def glu(j):
                unit(GLU0 + j)
                s = (GLU0 + j) % SLOTS
                for c in range(2):
                    b = bank(("glu", 2 * j + c))
                    for kk in range(SSM_C):
                        if j == 0 and c == 0:
                            pe.wait_ge(ssm_glu_inputs, 2 + kk + 1)
                        o = 1024 * c + P * kk
                        ins = three(b[:, 0:256], hi[s][:, o:o + P], lo[s][:, o:o + P], gTh[:, kk], gTl[:, kk],
                                    kk == 0, kk == SSM_C - 1)
                used(ins)

            def attention_step(g, hf):
                x = g - HALF_AT[hf]
                if 0 <= x - QKT_AT < 4:
                    i = x - QKT_AT
                    kq, t = i // 2, i % 2
                    b = bank(("qkT", hf, i))
                    pe.wait_ge(half_rotated, 4 * hf + 4)
                    for h in range(4):
                        col = 512 * kq + P * h
                        ins = M.transpose(b[:, P * h:P * h + P], zqk[:, t, col:col + P], ident[:, :])
                    filled(ins, ("qkT", hf, i))
                if 0 <= x - S0_AT < 2:
                    i = x - S0_AT
                    b = bank(("s0", hf, i))
                    if i == 0:
                        for k in range(4):
                            stored(pe, ("qkT", hf, k))
                    r = slice(64 * i, 64 * i + 64)
                    for h in range(4):
                        ins = M.matmul(b[:, P * h:P * h + P], qkT[r, 0, h, 0:P], qkT[r, 1, h, 0:P], start=True, stop=True,
                                       skip_group_check=True)
                    filled(ins, ("s0", hf, i))
                if 0 <= x - S1_AT < 4:
                    i = x - S1_AT
                    b = bank(("s1", hf, i))
                    c = i % 2
                    r = slice(64 * c, 64 * c + 64)
                    for k in range(2):
                        h = 2 * (i // 2) + k
                        ins = M.matmul(b[:, S * k:S * k + S], qkT[r, 0, h, P:S], qkT[r, 1, h, 0:S], start=True, stop=True,
                                       skip_group_check=True)
                    filled(ins, ("s1", hf, i))
                if x == AT_AT:
                    b = bank(("aT", hf, 0))
                    pe.wait_ge(differences_ready, 8 * hf + 4)
                    for h in range(4):
                        ins = M.transpose(b[:, P * h:P * h + P], p0[:, 2 * h], ident[:, :])
                    filled(ins, ("aT", hf, 0))
                if 1 <= x - AT_AT < 3:
                    i = x - AT_AT
                    b = bank(("aT", hf, i))
                    pe.wait_ge(differences_ready, 8 * hf + 4 + 2 * i)
                    for k in range(2):
                        for kk in range(2):
                            ins = M.transpose(b[:, P * (2 * k + kk):P * (2 * k + kk) + P],
                                              p1[:, 2 * (2 * (i - 1) + k), P * kk:P * kk + P], ident[:, :])
                    filled(ins, ("aT", hf, i))

            for cb in range(6):
                def step(x, cb=cb):
                    g = 16 * cb + x
                    if g % BLOCK_EVERY == 0:
                        slot(g // BLOCK_EVERY)
                    for hf in range(2):
                        attention_step(g, hf)
                rows_block(("qkv", cb), QKV0 + 4 * cb, 4, XTh, XTl, step)

            y(NBLK - 2)
            y(NBLK - 1)

            for hf in range(2):
                for i in range(3):
                    stored(pe, ("aT", hf, i))
                for t in range(NT):
                    stored(pe, ("qkv", 4 + hf, t))
            for i in range(4):
                t, hf = i // 2, i % 2
                b = bank(("av", i))
                if i >= 2:
                    pe.wait_ge(y_ready, SSM_C - 3 + i)
                for x in range(4):
                    h = 4 * hf + x
                    out = b[:, P * x:P * x + P]
                    if t == 0:
                        ins = M.matmul(out, aT0[:, h], vnat[:, 0, P * h:P * h + P], start=True, stop=True,
                                       skip_group_check=True)
                    else:
                        for kk in range(2):
                            ins = M.matmul(out, aT1[:, h, kk], vnat[:, kk, P * h:P * h + P],
                                           start=kk == 0, stop=kk == 1, skip_group_check=True)
                filled(ins, ("av", i))
            for j in range(3):
                glu(j)
            for i in range(4):
                b = bank(("oT", i))
                for t in range(NT):
                    stored(pe, ("av", 2 * t + i // 2))
                    for x in range(2):
                        h = 2 * i + x
                        ins = M.transpose(b[:, S * x + P * t:S * x + P * t + P], att_n[:, t, P * h:P * h + P], ident[:, :])
                filled(ins, ("oT", i))
            glu(3)
            for i in range(4):
                stored(pe, ("oT", i))
            for n in range(16):
                cb, q = WO_ORDER[n] // 4, WO_ORDER[n] % 4
                if n == 4:
                    pe.wait_ge(mix_ready, 2 * SSM_C)
                rows_unit(("wo", cb), WO0 + n, q, 4, mixh, mixl)
                if n == 0:
                    b = bank(("ssq", 0))
                    for j in range(SSM_C):
                        pe.wait_ge(mix_ready, j + 1)
                        ins = M.matmul(b[:, 0:256], ones[:, :], sqb[:, j], start=j == 0, stop=j == SSM_C - 1)
                    filled(ins, ("ssq", 0))
                if n == 9:
                    for c in range(2):
                        for t in range(NT):
                            stored(pe, ("wo", c, t))
                    norm(2, H, range(4))
                if n == 13:
                    for t in range(NT):
                        stored(pe, ("wo", 2, t))
                    norm(2, H, (4, 5))

            for t in range(NT):
                stored(pe, ("wo", 3, t))
            norm(2, H, (6, 7))
            def scores(h):
                b = bank(("xs", h))
                stored(pe, ("xq", h))
                for t in range(NT):
                    ins = M.matmul(b[:, S * t:S * t + S], qxT[:, h, P * t:P * t + P], kxT[:, h], start=True,
                                   stop=True, skip_group_check=True)
                filled(ins, ("xs", h))

            def probs(h):
                b = bank(("xp", h))
                pe.wait_ge(cross_probs_ready, 2 * h + 2)
                for kk in range(2):
                    for t in range(NT):
                        ins = M.transpose(b[:, S * kk + P * t:S * kk + P * t + P], px[:, t, h, P * kk:P * kk + P], ident[:, :])
                filled(ins, ("xp", h))

            def output(h):
                b = bank(("xo", h))
                stored(pe, ("xp", h))
                for kk in range(2):
                    ins = M.matmul(b[:, 0:256], vx[:, kk, P * h:P * h + P], pxT[:, h, kk], start=kk == 0, stop=kk == 1)
                filled(ins, ("xo", h))

            for j in range(4):
                cols_unit(("xq", j), XQ0 + j, XT2h, XT2l, 2 if j == 0 else None)
                if j == 1:
                    spread(2)
                if j == 2:
                    scores(0)
                    scores(1)
            for job, heads in ((probs, (0, 1)), (scores, (2, 3)), (output, (0, 1)), (probs, (2, 3)), (output, (2, 3))):
                for h in heads:
                    job(h)
            for cb in range(4):
                rows_unit(("xw", cb), XO0 + cb, 0, 1, oxh, oxl, ready=cb == 0)
                if cb:
                    for t in range(NT):
                        stored(pe, ("xw", cb - 1, t))
                    norm(3, H, (2 * cb - 2, 2 * cb - 1))
            for t in range(NT):
                stored(pe, ("xw", 3, t))
            norm(3, H, (6, 7))

            for c in range(16):
                cols_unit(("pq", c), PQ0 + c, XT2h, XT2l, 3 if c == 0 else None)
                if c == 1:
                    spread(3)
                if c in NAT_AT:
                    pe.wait_ge(rows_normalised, NT)
                    norm(4, nat, NAT_AT[c])
            for cp in range(8):
                stored(pe, ("norm", 4, cp))
            pe.wait_ge(keys_loaded, 16)
            for i in range(8):
                t = i // 4
                b = bank(("ps", i))
                for x in range(4):
                    c = 4 * (i % 4) + x
                    stored(pe, ("pq", c))
                    ins = M.matmul(b[:, P * x:P * x + P], qP[:, c, P * t:P * t + P], keys[:, c], start=True,
                                   stop=True, skip_group_check=True)
                filled(ins, ("ps", i))
            for i in range(4, 8):
                stored(pe, ("ps", i))
            pe.sem_inc(u_bank_free, 4)

            def expert_unit(i, j, gu0, lo_sem, lo0, per):
                pe.wait_ge(lo_sem, i * per + (lo0 + j + 1))
                pe.wait_ge(u_bank_free, i * per + (gu0 + j + 1))
                s = j % SLOTS
                for c in range(DC):
                    ins = three(ps[s][:, 0:256], hi[s][:, P * c:P * c + P], lo[s][:, P * c:P * c + P],
                                XTh[:, c], XTl[:, c], c == 0, c == DC - 1)
                used(ins)

            def clear(b):
                M.matmul(ps[b][:, :], zr[:, 0:P], zr[:, :], start=True, stop=False, skip_group_check=True)

            pe.wait_ge(zeros_ready, 1)
            for b in range(4, 8):
                clear(b)
            with pe.Fori(0, UA // 4) as i:
                for j in range(4):
                    expert_unit(i, j, 0, rest_ready_pool, U0 - 1, 4)
            with pe.Fori(0, (KEYS - UA) // 4) as i:
                for j in range(4):
                    expert_unit(i, j, UA, rest_ready_vector, 0, 4)
            for b in range(4):
                pe.wait_ge(u_bank_free, KEYS + 1 + b)
                clear(b)
            with pe.Fori(0, KEYS // 8) as i:
                for g in range(2):
                    pe.wait_ge(weight_parts_ready, i * 4 + (2 * g + 2))
                    for j in range(4):
                        pe.wait_ge(rest_ready_vector, i * 8 + (KEYS - UA + 4 * g + j + 1))
                        for t in range(NT):
                            wh, wl = Wh[:, g, j, P * t:P * t + P], Wl[:, g, j, P * t:P * t + P]
                            for x, v in ((wh, hi), (wh, lo), (wl, hi)):
                                for c in range(4):
                                    ins = M.matmul(ps[4 * t + c][:, :], x, v[j][:, 512 * c:512 * c + 512],
                                                   start=False, stop=True, skip_group_check=True)
                        ins.then_inc(units_used, 1)


def kernel(**inputs):
    import numpy as np
    import concourse.bacc as bacc
    from concourse.bass_utils import run_bass_kernel_spmd

    a = {k: np.asarray(v) for k, v in inputs.items()}

    def cont(x):
        return np.ascontiguousarray(x)

    def cols(v):
        return cont(v.reshape(-1, P).T)

    def by_cols(w):
        kc, n = w.shape[0] // P, w.shape[1] // P
        return cont(w.reshape(kc, P, n, P).transpose(2, 1, 0, 3)).reshape(-1, P, kc * P)

    def by_rows(w, order=None):
        q, n = w.shape[0] // (4 * P), w.shape[1] // 512
        return cont(w.reshape(q, 4, P, n, 512).transpose(3, 0, 2, 1, 4)[order or list(range(n))]).reshape(-1, P, D)

    w_in, w_kv = a["w_in"][0], a["xattn_wkv"][0]
    glu = by_cols(a["glu_w"][0]).reshape(4, 2, P, SSM_W).transpose(0, 2, 1, 3)
    b_all = np.stack([a["ssm_b_re"][0], a["ssm_b_im"][0]])
    c_all = np.stack([a["ssm_c_re"][0], a["ssm_c_im"][0]])
    keys = np.stack([a["peer_k1"][0], a["peer_k2"][0]], axis=1)
    vecs = np.zeros((P, VECS), np.float32)
    for n, v in (("gains", np.concatenate([cols(a[m][0]) for m in ("mem_norm_g", "mix_norm_g", "xattn_norm_g",
                                                                  "ffn_norm_g")], 1)),
                 ("g_att", cols(a["attn_head_g"][0])), ("g_ssm", cols(a["ssm_out_g"][0])), ("glu_b", cols(a["glu_b"][0])),
                 ("d_skip", cols(a["ssm_d"][0].reshape(-1))),
                 ("lam", np.concatenate([a[m].reshape(1, QK) for m in ("lam_q1", "lam_k1", "lam_q2", "lam_k2")], 1))):
        o, c = VEC_AT[n]
        vecs[:, o:o + c] = v
    arrays = {
        "x": a["x"][0], "mem": a["mem"][0],
        "w_mk": by_cols(w_kv[:, :XW]), "w_mv": by_rows(w_kv[:, XW:]),
        "w_u": by_cols(w_in[:, 3 * ATT:]), "w_qkv": by_rows(w_in[:, :3 * ATT], QKV_ORDER),
        "w_glu": cont(glu).reshape(4, P, D), "w_wo": by_rows(a["w_out"][0])[WO_ORDER],
        "w_xq": by_cols(a["xattn_wq"][0]), "w_xo": by_rows(a["xattn_wo"][0]),
        "w_pq": by_cols(a["peer_wq"][0]),
        "u": cont(a["peer_u"][0].reshape(KEYS, KEYS, DC, P).transpose(1, 3, 2, 0)).reshape(KEYS, P, D),
        "v": cont(a["peer_v"][0].reshape(KEYS, KEYS, D).transpose(1, 0, 2)),
        "vecs": vecs, "pos": cols(a["positions"][0]),
        "ssm": np.stack([cols(a["ssm_a_re"][0].reshape(-1)), cols(a["ssm_a_im"][0].reshape(-1)),
                         np.repeat(a["ssm_log_dt"].reshape(NBLK, 2).T, P // 2, axis=0)], 1),
        "bT": cont(b_all.reshape(2, SSM_C, 8, QK, 16).transpose(2, 4, 0, 1, 3)).reshape(P, 2, SSM_C, QK),
        "cT": cont(c_all.reshape(2, NBLK, 2, 16, QK).transpose(2, 4, 0, 1, 3)).reshape(P, 2, NBLK, 16),
        "keys": cont(keys.reshape(2 * PH, KEYS, P).transpose(2, 0, 1)),
        "g_fin": a["final_norm_g"].reshape(1, D),
    }
    arrays = {f"in_{n}": cont(v) for n, v in arrays.items()}
    nc = bacc.Bacc("TRN2", target_bir_lowering=False, num_devices=1)
    T = {n[3:]: nc.dram_tensor(n, v.shape, mybir.dt.from_np(v.dtype), kind="ExternalInput").ap()
         for n, v in arrays.items()}
    for n in ("x", "mem"):
        T[n] = T[n].rearrange("(t p) d -> p t d", p=P)
    T["out"] = nc.dram_tensor("out", (S, D), F32, kind="ExternalOutput").ap()
    hymba_peer(nc, T)
    r = run_bass_kernel_spmd(nc, [arrays], core_ids=[0])
    return r.results[0]["out"].reshape(1, S, D)
```
